# Optimizing a Trainium2 kernel written in Bass

```python
import jax
import jax.numpy as jnp
from jax import lax
import numpy as np

D_MODEL = 1024
BATCH = 1
SEQ = 1024
DEPTH = 1

CHUNK = 64
Q_BLOCK = 128
FOX_HEAD_DIM = 64
FOX_WIDTH = D_MODEL // 2
FOX_HEADS = FOX_WIDTH // FOX_HEAD_DIM
MLSTM_HEAD_DIM = 128
MLSTM_WIDTH = D_MODEL - FOX_WIDTH
MLSTM_HEADS = MLSTM_WIDTH // MLSTM_HEAD_DIM
MIX_WIDTH = FOX_WIDTH + MLSTM_WIDTH
CONV_WIDTH = 4
D_FF = 2816
N_MOD = 9
EPS = 1e-6
IN_SIZES = (FOX_WIDTH, FOX_WIDTH, FOX_WIDTH, FOX_HEADS,
            MLSTM_WIDTH, MLSTM_WIDTH, MLSTM_WIDTH, MLSTM_WIDTH, MLSTM_HEADS, MLSTM_HEADS)
IN_COLS = sum(IN_SIZES)

kernel_name = 'hymba_fox_mlstm_macaron_adaln'

def _split_points(sizes):
    pts, acc = [], 0
    for s in sizes[:-1]:
        acc += s
        pts.append(acc)
    return pts

def rms_normalize(x):
    xf = x.astype(jnp.float32)
    y = xf * lax.rsqrt(jnp.mean(xf * xf, axis=-1, keepdims=True) + EPS)
    return y.astype(x.dtype)

def modulate(h, shift, scale):
    return h * (1 + scale[:, None, :]) + shift[:, None, :]

def swiglu(h, w_in, w_out):
    g, u = jnp.split(h @ w_in, 2, axis=-1)
    return (jax.nn.silu(g) * u) @ w_out

def to_heads(t, n_heads):
    b, s, _ = t.shape
    return t.reshape(b, s, n_heads, -1).transpose(0, 2, 1, 3)

def from_heads(t):
    b, h, s, d = t.shape
    return t.transpose(0, 2, 1, 3).reshape(b, s, h * d)

def causal_depthwise_conv(x, w, b):
    ch = x.shape[-1]
    y = lax.conv_general_dilated(
        x, w[:, None, :], window_strides=(1,), padding=[(CONV_WIDTH - 1, 0)],
        dimension_numbers=('NWC', 'WIO', 'NWC'), feature_group_count=ch)
    return y + b

def forgetting_attention(q, k, v, log_f):
    b, h, s, dh = q.shape
    nb = s // Q_BLOCK
    cum = jnp.cumsum(log_f, axis=-1)
    kpos = jnp.arange(s)
    qb = q.reshape(b, h, nb, Q_BLOCK, dh).transpose(2, 0, 1, 3, 4)
    cb = cum.reshape(b, h, nb, Q_BLOCK).transpose(2, 0, 1, 3)
    qpos = kpos.reshape(nb, Q_BLOCK)
    scale = dh ** -0.5

    def block(args):
        q_i, c_i, pos_i = args
        logits = jnp.einsum('bhqd,bhkd->bhqk', q_i, k).astype(jnp.float32) * scale
        logits = logits + c_i[..., :, None] - cum[..., None, :]
        logits = jnp.where(pos_i[:, None] >= kpos[None, :], logits, -jnp.inf)
        p = jax.nn.softmax(logits, axis=-1)
        return jnp.einsum('bhqk,bhkd->bhqd', p.astype(v.dtype), v)

    out = lax.map(block, (qb, cb, qpos))
    return out.transpose(1, 2, 0, 3, 4).reshape(b, h, s, dh)

def mlstm_chunkwise(q, k, v, i_pre, log_f):
    b, h, s, dh = q.shape
    nc = s // CHUNK
    f32 = jnp.float32
    qc = q.astype(f32).reshape(b, h, nc, CHUNK, dh)
    kc = (k.astype(f32) * dh ** -0.5).reshape(b, h, nc, CHUNK, dh)
    vc = v.astype(f32).reshape(b, h, nc, CHUNK, dh)
    ic = i_pre.reshape(b, h, nc, CHUNK)
    a = jnp.cumsum(log_f.reshape(b, h, nc, CHUNK), axis=-1)
    g = a[..., -1]
    w_end = g[..., None] - a + ic

    def step(carry, xs):
        c_mat, n_vec, m = carry
        k_j, v_j, w_j, g_j = xs
        m_new = jnp.maximum(g_j + m, jnp.max(w_j, axis=-1))
        decay = jnp.exp(g_j + m - m_new)
        wt = jnp.exp(w_j - m_new[..., None])
        c_new = decay[..., None, None] * c_mat + jnp.einsum('bhl,bhld,bhle->bhde', wt, v_j, k_j)
        n_new = decay[..., None] * n_vec + jnp.einsum('bhl,bhle->bhe', wt, k_j)
        return (c_new, n_new, m_new), (c_mat, n_vec, m)

    init = (jnp.zeros((b, h, dh, dh), f32), jnp.zeros((b, h, dh), f32), jnp.zeros((b, h), f32))
    xs = (kc.transpose(2, 0, 1, 3, 4), vc.transpose(2, 0, 1, 3, 4),
          w_end.transpose(2, 0, 1, 3), g.transpose(2, 0, 1))
    _, (c_st, n_st, m_st) = lax.scan(step, init, xs)
    c_st = c_st.transpose(1, 2, 0, 3, 4)
    n_st = n_st.transpose(1, 2, 0, 3)
    m_st = m_st.transpose(1, 2, 0)

    causal = jnp.tril(jnp.ones((CHUNK, CHUNK), dtype=bool))
    d_log = a[..., :, None] - a[..., None, :] + ic[..., None, :]
    d_log = jnp.where(causal, d_log, -jnp.inf)
    inter = a + m_st[..., None]
    m_t = jnp.maximum(inter, jnp.max(d_log, axis=-1))
    p = jnp.exp(d_log - m_t[..., None])
    inter_w = jnp.exp(inter - m_t)
    scores = jnp.einsum('bhntd,bhnsd->bhnts', qc, kc) * p
    num = (jnp.einsum('bhnts,bhnsd->bhntd', scores, vc)
           + inter_w[..., None] * jnp.einsum('bhnde,bhnte->bhntd', c_st, qc))
    den = scores.sum(-1) + inter_w * jnp.einsum('bhne,bhnte->bhnt', n_st, qc)
    out = num / jnp.maximum(jnp.abs(den), jnp.exp(-m_t))[..., None]
    return out.reshape(b, h, s, dh)

def hybrid_mixer(h, w_in, b_fox_f, b_m_i, b_m_f, w_conv, b_conv, g_mhn, w_out):
    b, s, _ = h.shape
    f32 = jnp.float32
    proj = h @ w_in
    fq, fk, fv, ff, mq, mk, mv, mo, mi, mf = jnp.split(proj, _split_points(IN_SIZES), axis=-1)
    log_f_a = jax.nn.log_sigmoid((ff + b_fox_f).astype(f32)).transpose(0, 2, 1)
    y_a = from_heads(forgetting_attention(to_heads(fq, FOX_HEADS), to_heads(fk, FOX_HEADS),
                                          to_heads(fv, FOX_HEADS), log_f_a))
    qk = jax.nn.silu(causal_depthwise_conv(jnp.concatenate([mq, mk], axis=-1), w_conv, b_conv))
    mq_c, mk_c = jnp.split(qk, 2, axis=-1)
    i_pre = (mi + b_m_i).astype(f32).transpose(0, 2, 1)
    log_f_b = jax.nn.log_sigmoid((mf + b_m_f).astype(f32)).transpose(0, 2, 1)
    h_b = mlstm_chunkwise(to_heads(mq_c, MLSTM_HEADS), to_heads(mk_c, MLSTM_HEADS),
                          to_heads(mv, MLSTM_HEADS), i_pre, log_f_b)
    h_b = rms_normalize(h_b.transpose(0, 2, 1, 3)) * g_mhn.reshape(MLSTM_HEADS, MLSTM_HEAD_DIM).astype(f32)
    y_b = jax.nn.sigmoid(mo) * h_b.reshape(b, s, MLSTM_WIDTH).astype(h.dtype)
    return jnp.concatenate([y_a, y_b], axis=-1) @ w_out

def setup_inputs(seed: int = 0) -> dict:
    key = jax.random.key(seed)
    ks = jax.random.split(key, 20)
    f32 = jnp.float32

    def dense(k, shape, fan_in):
        return jax.random.normal(k, shape, f32) * fan_in ** -0.5

    def small(k, shape, s=0.02):
        return jax.random.normal(k, shape, f32) * s

    L = DEPTH
    return {
        'x': jax.random.normal(ks[0], (BATCH, SEQ, D_MODEL), f32),
        'c': jax.random.normal(ks[1], (BATCH, D_MODEL), f32),
        'w_ada': dense(ks[2], (L, D_MODEL, N_MOD * D_MODEL), D_MODEL),
        'b_ada': small(ks[3], (L, N_MOD * D_MODEL)),
        'w_ffn1_in': dense(ks[4], (L, D_MODEL, 2 * D_FF), D_MODEL),
        'w_ffn1_out': dense(ks[5], (L, D_FF, D_MODEL), D_FF),
        'w_mix_in': dense(ks[6], (L, D_MODEL, IN_COLS), D_MODEL),
        'b_fox_f': jnp.linspace(1.0, 5.0, FOX_HEADS, dtype=f32)[None] + small(ks[7], (L, FOX_HEADS), 0.1),
        'b_m_i': small(ks[8], (L, MLSTM_HEADS), 0.1),
        'b_m_f': jnp.linspace(3.0, 6.0, MLSTM_HEADS, dtype=f32)[None] + small(ks[9], (L, MLSTM_HEADS), 0.1),
        'w_conv': dense(ks[10], (L, CONV_WIDTH, 2 * MLSTM_WIDTH), CONV_WIDTH),
        'b_conv': small(ks[11], (L, 2 * MLSTM_WIDTH)),
        'g_mhn': 1.0 + small(ks[12], (L, MLSTM_WIDTH)),
        'w_mix_out': dense(ks[13], (L, MIX_WIDTH, D_MODEL), MIX_WIDTH),
        'w_ffn2_in': dense(ks[14], (L, D_MODEL, 2 * D_FF), D_MODEL),
        'w_ffn2_out': dense(ks[15], (L, D_FF, D_MODEL), D_FF),
        'g_final': 1.0 + small(ks[16], (D_MODEL,)),
    }

def reference(x, c, w_ada, b_ada, w_ffn1_in, w_ffn1_out, w_mix_in, b_fox_f, b_m_i, b_m_f,
              w_conv, b_conv, g_mhn, w_mix_out, w_ffn2_in, w_ffn2_out, g_final):
    c_act = jax.nn.silu(c)
    for layer in range(DEPTH):
        mod = c_act @ w_ada[layer] + b_ada[layer]
        (sh1, sc1, gt1, sh2, sc2, gt2, sh3, sc3, gt3) = jnp.split(mod, N_MOD, axis=-1)
        h = modulate(rms_normalize(x), sh1, sc1)
        x = x + 0.5 * gt1[:, None, :] * swiglu(h, w_ffn1_in[layer], w_ffn1_out[layer])
        h = modulate(rms_normalize(x), sh2, sc2)
        y = hybrid_mixer(h, w_mix_in[layer], b_fox_f[layer], b_m_i[layer], b_m_f[layer],
                         w_conv[layer], b_conv[layer], g_mhn[layer], w_mix_out[layer])
        x = x + gt2[:, None, :] * y
        h = modulate(rms_normalize(x), sh3, sc3)
        x = x + 0.5 * gt3[:, None, :] * swiglu(h, w_ffn2_in[layer], w_ffn2_out[layer])
    return rms_normalize(x) * g_final


_drawn_inputs = setup_inputs


def setup_inputs(seed=0):
    import zlib

    import numpy as np

    out = dict(_drawn_inputs(seed))
    spreads = {}
    factors = {'b_m_i': 64.0, 'b_conv': 8.0, 'g_mhn': 24.86, 'g_final': 2.836}
    for name, (base, spread) in spreads.items():
        noise = np.random.default_rng([zlib.crc32(name.encode()), seed]).standard_normal(out[name].shape)
        drawn = base * np.exp(spread * noise) if base else spread * noise
        out[name] = jnp.asarray(drawn.astype(out[name].dtype))
    for name, factor in factors.items():
        out[name] = (out[name] * factor).astype(out[name].dtype)
    return out
```

```python
from contextlib import ExitStack

import concourse.bass as bass
from concourse import mybir

F32 = mybir.dt.float32
F32R = mybir.dt.float32r
BF16 = mybir.dt.bfloat16
ALU = mybir.AluOpType
ACT = mybir.ActivationFunctionType
AX = mybir.AxisListType

P = 128
BANK = 512
EPS = 1e-6
NEG = -1e30


class Core:

    def __init__(self, nc, ctx, x, w_ffn_in, w_mix_in, w_conv, b_fox, b_m):
        self.nc, self.ctx, self.sems = nc, ctx, []
        self.S, self.D = x.shape[1], x.shape[2]
        self.F = w_ffn_in.shape[2] // 2
        self.KD = self.D // P
        self.NS = self.S // P
        self.NH = self.S // BANK
        self.xres = self.sb("xres", [P, self.NS, self.D])
        self.h_hi = self.sb("h_hi", [P, self.KD, self.S], F32R)
        self.h_lo = self.sb("h_lo", [P, self.KD, self.S], F32R)
        self.ident = self.sb("ident", [P, P])
        self.rms = self.sb("rms", [P, 3, self.NS])
        self.neg_half = self.sb("neg_half", [P, self.NS])
        self.bank = ctx.enter_context(nc.psum_tensor("bank", [P, 8, BANK], F32))
        self.mod_rows = nc.dram_tensor("mod_rows", (9 * self.D,), F32, kind="Internal").ap()

    def sb(self, name, shape, dt=F32, ctx=None):
        return (ctx or self.ctx).enter_context(self.nc.sbuf_tensor(name, shape, dt))

    def sem(self, name):
        self.sems.append(self.nc.alloc_semaphore(name=name))
        return self.sems[-1]

    def end_part(self):
        self.nc.clear_and_free_semaphores(self.sems)
        self.nc.all_engine_barrier()
        self.sems = []

    def mod(self, m):
        return self.mod_rows[m * self.D:(m + 1) * self.D].partition_broadcast(P)


class Norm:

    def __init__(self, core, tag, shift, scale1, junk, xn, first_bank):
        self.c, self.shift, self.scale1, self.junk, self.xn = core, shift, scale1, junk, xn
        self.first_bank = first_bank
        s = core.sem
        self.loaded = s(f"{tag}_mod_loaded")
        self.squared = s(f"{tag}_squared")
        self.mean_done = s(f"{tag}_mean_done")
        self.rms_done = s(f"{tag}_rms_done")
        self.scaled = s(f"{tag}_scaled")
        self.shifted = s(f"{tag}_shifted")
        self.turned = s(f"{tag}_turned")
        self.hi_done = s(f"{tag}_hi_done")
        self.lo_done = s(f"{tag}_lo_done")

    def load(self, sp, m):
        sp.dma_start(self.shift, self.c.mod(m)).then_inc(self.loaded, 16)
        sp.dma_start(self.scale1, self.c.mod(m + 1)).then_inc(self.loaded, 16)

    def bank_of(self, t):
        return self.first_bank + 2 * (t % 2)

    def square(self, act, t):
        if t:
            act.wait_ge(self.squared, t)
        act.activation(self.junk, self.c.xres[:, t, :], ACT.Square,
                       accum_out=self.c.rms[:, 0, t:t + 1]).then_inc(self.squared, 1)

    def inverse(self, pool, t):
        c = self.c
        pool.wait_ge(self.squared, t + 1)
        pool.tensor_scalar(c.rms[:, 1, t:t + 1], c.rms[:, 0, t:t + 1], 1.0 / c.D, EPS,
                           ALU.mult, ALU.add).then_inc(self.mean_done, 1)
        pool.wait_ge(self.mean_done, t + 1)
        pool.tensor_tensor(c.rms[:, 2, t:t + 1], c.rms[:, 1, t:t + 1], c.neg_half[:, t:t + 1],
                           ALU.pow).then_inc(self.rms_done, 1)

    def scale(self, dve, t):
        c, n = self.c, len(self.xn)
        if t == 0:
            dve.wait_ge(self.loaded, 32)
        dve.wait_ge(self.rms_done, t + 1)
        if t >= n:
            dve.wait_ge(self.turned, 2 * (t - n) + 2)
        dve.scalar_tensor_tensor(self.xn[t % n], c.xres[:, t, :], c.rms[:, 2, t:t + 1], self.scale1,
                                 ALU.mult, ALU.mult).then_inc(self.scaled, 1)

    def add_shift(self, pool, t):
        n = len(self.xn)
        if t == 0:
            pool.wait_ge(self.loaded, 32)
        pool.wait_ge(self.scaled, t + 1)
        pool.tensor_tensor(self.xn[t % n], self.xn[t % n], self.shift, ALU.add).then_inc(self.shifted, 1)

    def turn(self, pe, t):
        c, n = self.c, len(self.xn)
        pe.wait_ge(self.shifted, t + 1)
        if t >= 2:
            pe.wait_ge(self.lo_done, 2 * (t - 2) + 2)
        for half in range(2):
            for k in range(4):
                mm = pe.transpose(c.bank[:, self.bank_of(t) + half, k * P:(k + 1) * P],
                                  self.xn[t % n][:, (4 * half + k) * P:(4 * half + k + 1) * P], c.ident[:, :])
            mm.then_inc(self.turned, 1)

    def _h(self, which, t, half):
        return which[:, 4 * half:4 * half + 4, t * P:(t + 1) * P]

    def _turned(self, t, half):
        return self.c.bank[:, self.bank_of(t) + half, :].rearrange("p (k s) -> p k s", k=4)

    def keep_hi(self, act, t):
        for half in range(2):
            act.wait_ge(self.turned, 2 * t + half + 1)
            act.copy(self._h(self.c.h_hi, t, half), self._turned(t, half)).then_inc(self.hi_done, 1)

    def keep_lo(self, dve, t):
        for half in range(2):
            dve.wait_ge(self.hi_done, 2 * t + half + 1)
            dve.tensor_tensor(self._h(self.c.h_lo, t, half), self._turned(t, half),
                              self._h(self.c.h_hi, t, half).bitcast(F32),
                              ALU.subtract).then_inc(self.lo_done, 1)


def modulation(core, x, c_vec, w_ada, b_ada):
    nc, KD, D = core.nc, core.KD, core.D
    M = 9
    CH = 2 * D
    NCH = M * D // CH + (M * D % CH > 0)
    widths = [min(CH, M * D - i * CH) for i in range(NCH)]
    RING = 4
    with ExitStack() as ctx:
        sb = lambda *a: core.sb(*a, ctx=ctx)
        raw = sb("ada_raw", [P, RING, CH])
        acc = sb("ada_acc", [P, M * D])
        c_act = sb("c_act", [P, KD])
        brow = sb("b_ada_rows", [(M + 1) * KD, P])
        bcol = sb("b_ada_cols", [P, M * KD])
        ones = sb("ada_ones", [P, 1])
        mcol = sb("mod_cols", [P, M * KD])
        mrow = sb("mod_row_tiles", [M * KD, P])
        junk = sb("n1_junk", [P, D])
        shift, scale1 = sb("n1_shift", [P, D]), sb("n1_scale1", [P, D])
        xn = sb("n1_xn", [P, 2, D])
        s = core.sem
        x_loaded = s("x_loaded")
        small_loaded = s("small_loaded")
        consts = s("consts")
        ident_zero = s("ident_zero")
        raw_loaded = [s(f"ada_raw_loaded{i}") for i in range(RING)]
        c_act_done = s("c_act_done")
        acc_done = s("ada_acc_done")
        b_turned = s("b_turned")
        b_kept = s("b_kept")
        cols_done = s("mod_cols_done")
        bias_added = s("bias_added")
        one_added = s("one_added")
        gates_halved = s("gates_halved")
        rows_turned = s("rows_turned")
        rows_kept = s("rows_kept")
        rows_stored = s("rows_stored")
        norm = Norm(core, "n1", shift[:, :], scale1[:, :], junk[:, :], [xn[:, 0, :], xn[:, 1, :]], 4)

        pieces = [(i, k) for i in range(NCH) for k in range(KD)]
        with nc.Block() as block:

            @block.sync
            def _(sp):
                sp.dma_start(brow[M * KD:, :], c_vec.rearrange("a (k p) -> (a k) p", p=P)).then_inc(small_loaded, 16)
                sp.dma_start(brow[0:M * KD, :], b_ada.rearrange("a (r n) -> (a r) n", n=P)).then_inc(small_loaded, 16)
                sp.dma_start(core.xres[:, :, :], x.rearrange("a (t p) d -> p (a t) d", p=P)).then_inc(x_loaded, 16)
                for n, (i, k) in enumerate(pieces):
                    if n >= RING:
                        sp.wait_ge(acc_done, n - RING + 1)
                    sp.dma_start(raw[:, n % RING, 0:widths[i]],
                                 w_ada[0, k * P:(k + 1) * P, i * CH:i * CH + widths[i]])\
                        .then_inc(raw_loaded[n % RING], 16)
                sp.wait_ge(rows_kept, 1)
                sp.dma_start(core.mod_rows.rearrange("(r n) -> r n", n=P), mrow[:, :]).then_inc(rows_stored, 16)
                sp.wait_ge(rows_stored, 16)
                norm.load(sp, 0)

            @block.gpsimd
            def _(pool):
                pool.memset(core.ident[:, :], 0.0).then_inc(ident_zero, 1)
                pool.wait_ge(ident_zero, 1)
                pool.affine_select(out=core.ident[:, :], in_=core.ident[:, :], compare_op=ALU.not_equal,
                                   fill=1.0, base=0, pattern=[[-1, P]], channel_multiplier=1).then_inc(consts, 1)
                pool.memset(ones[:, :], 1.0).then_inc(consts, 1)
                pool.memset(core.neg_half[:, :], -0.5).then_inc(consts, 1)
                pool.wait_ge(consts, 3)
                for t in range(core.NS):
                    norm.inverse(pool, t)
                for t in range(core.NS):
                    norm.add_shift(pool, t)

            @block.scalar
            def _(act):
                act.wait_ge(b_turned, 1)
                act.activation(c_act[:, :], core.bank[:, 0, M * KD:(M + 1) * KD], ACT.Silu).then_inc(c_act_done, 1)
                act.wait_ge(x_loaded, 16)
                for t in range(core.NS):
                    norm.square(act, t)
                for t in range(core.NS):
                    norm.keep_hi(act, t)

            @block.vector
            def _(dve):
                dve.wait_ge(c_act_done, 1)
                for n, (i, k) in enumerate(pieces):
                    dve.wait_ge(raw_loaded[n % RING], 16 * (n // RING + 1))
                    part, piece = acc[:, i * CH:i * CH + widths[i]], raw[:, n % RING, 0:widths[i]]
                    c_k = c_act[:, k:k + 1]
                    if k == 0:
                        dve.tensor_scalar(part, piece, c_k, None, ALU.mult).then_inc(acc_done, 1)
                    else:
                        dve.wait_ge(acc_done, n)
                        dve.scalar_tensor_tensor(part, piece, c_k, part, ALU.mult, ALU.add).then_inc(acc_done, 1)
                dve.wait_ge(b_turned, 1)
                dve.tensor_copy(bcol[:, :], core.bank[:, 0, 0:M * KD]).then_inc(b_kept, 1)
                dve.wait_ge(b_kept, 1)
                dve.wait_ge(cols_done, 1)
                dve.tensor_tensor(mcol[:, :], core.bank[:, 1, 0:M * KD], bcol[:, :], ALU.add).then_inc(bias_added, 1)
                dve.wait_ge(bias_added, 1)
                for sub in range(3):
                    sc = mcol[:, (3 * sub + 1) * KD:(3 * sub + 2) * KD]
                    dve.tensor_scalar(sc, sc, 1.0, None, ALU.add).then_inc(one_added, 1)
                for sub in (0, 2):
                    gt = mcol[:, (3 * sub + 2) * KD:(3 * sub + 3) * KD]
                    dve.tensor_scalar(gt, gt, 0.5, None, ALU.mult).then_inc(gates_halved, 1)
                dve.wait_ge(rows_turned, 1)
                dve.tensor_copy(mrow[:, :], core.bank[0:M * KD, 2, 0:P]).then_inc(rows_kept, 1)
                for t in range(core.NS + 1):
                    if t < core.NS:
                        norm.scale(dve, t)
                    if t >= 1:
                        norm.keep_lo(dve, t - 1)

            @block.tensor
            def _(pe):
                pe.wait_ge(consts, 3)
                pe.wait_ge(small_loaded, 32)
                pe.transpose(core.bank[:, 0, 0:(M + 1) * KD], brow[:, :],
                             core.ident[0:(M + 1) * KD, 0:(M + 1) * KD])\
                    .then_inc(b_turned, 1)
                pe.wait_ge(acc_done, len(pieces))
                for r in range(M * KD):
                    mm = pe.matmul(core.bank[:, 1, r:r + 1], acc[:, r * P:(r + 1) * P], ones[:, :],
                                   start=True, stop=True)
                mm.then_inc(cols_done, 1)
                pe.wait_ge(one_added, 3)
                pe.wait_ge(gates_halved, 2)
                pe.transpose(core.bank[0:M * KD, 2, 0:P], mcol[:, :], core.ident[:, :]).then_inc(rows_turned, 1)
                for t in range(core.NS):
                    norm.turn(pe, t)


def ffn(core, tag, w_in, w_out, gate_row, next_mod=None, g_final=None, out=None):
    nc, KD, D, F, NS = core.nc, core.KD, core.D, core.F, core.NS
    TPS = 2
    STEPS = F // (TPS * P)
    NG = 2 * NS
    src_in = w_in.rearrange("a (k p) (g n) -> (a p) k g n", p=P, g=2)
    src_out = w_out.rearrange("a f d -> (a f) d")
    with ExitStack() as ctx:
        sb = lambda n, *a: core.sb(f"{tag}_{n}", *a, ctx=ctx)
        raw_in = sb("raw_in", [P, TPS, KD, 2, P])
        in_hi = sb("in_hi", [P, TPS, KD, 2, P], F32R)
        in_lo = sb("in_lo", [P, TPS, KD, 2, P], F32R)
        raw_out = sb("raw_out", [P, TPS, D])
        out_hi = sb("out_hi", [P, TPS, D], F32R)
        out_lo = sb("out_lo", [P, TPS, D], F32R)
        act_hi = sb("act_hi", [P, TPS, core.S], F32R)
        act_lo = sb("act_lo", [P, TPS, core.S], F32R)
        silu_g = sb("silu_g", [P, 2, BANK])
        act_f = sb("act_f", [P, 2, BANK])
        gate = sb("gate", [P, D])
        shift, scale1 = sb("shift", [P, D]), sb("scale1", [P, D])
        s = lambda n: core.sem(f"{tag}_{n}")
        in_loaded = [s(f"in_loaded{j}") for j in range(TPS)]
        out_loaded = [s(f"out_loaded{j}") for j in range(TPS)]
        gate_loaded = s("gate_loaded")
        in_hi_done, in_lo_done = s("in_hi_done"), s("in_lo_done")
        out_gated, out_hi_done, out_lo_done = s("out_gated"), s("out_hi_done"), s("out_lo_done")
        g_ready, u_ready = s("g_ready"), s("u_ready")
        silu_done, mult_done = s("silu_done"), s("mult_done")
        act_hi_done, act_lo_done = s("act_hi_done"), s("act_lo_done")
        y_ready, y_added = s("y_ready"), s("y_added")
        xn = [raw_in[:, j].rearrange("p k g n -> p (k g n)")[:, i * D:(i + 1) * D]
              for i in range(2) for j in range(TPS)]
        norm = Norm(core, tag + "n", shift[:, :], scale1[:, :], raw_out[:, 0, :], xn, 0)
        stored = s("stored")
        flat = lambda t, j: t[:, j].rearrange("p k g n -> p (k g n)")

        def steps(eng, body):
            body(0, True, False)
            with eng.Fori(1, STEPS - 1) as b:
                body(b, False, False)
            body(STEPS - 1, False, True)

        with nc.Block() as block:

            @block.sync
            def _(sp):
                sp.dma_start(gate[:, :], core.mod(gate_row)).then_inc(gate_loaded, 16)

                def load(b, first, last):
                    for j in range(TPS):
                        if not first:
                            sp.wait_ge(in_lo_done, b * TPS + (j - TPS + 1))
                        for g in range(2):
                            sp.dma_start(raw_in[:, j, :, g, :], src_in[:, :, g, bass.ts(b * TPS + j, P)])\
                                .then_inc(in_loaded[j], 16)
                    for j in range(TPS):
                        if not first:
                            sp.wait_ge(out_lo_done, b * TPS + (j - TPS + 1))
                        sp.dma_start(raw_out[:, j, :], src_out[bass.ts(b * TPS + j, P), :])\
                            .then_inc(out_loaded[j], 16)

                steps(sp, load)
                if next_mod is not None:
                    norm.load(sp, next_mod)
                else:
                    sp.dma_start(scale1[:, :], g_final.partition_broadcast(P)).then_inc(norm.loaded, 16)
                    for t in range(NS):
                        sp.wait_ge(norm.scaled, t + 1)
                        sp.dma_start(out[0, t * P:(t + 1) * P, :], core.xres[:, t, :]).then_inc(stored, 16)
                    sp.wait_ge(stored, 16 * NS)

            @block.gpsimd
            def _(pool):
                def cut_in(b, first):
                    for j in range(TPS):
                        pool.wait_ge(in_hi_done, b * TPS + (j + 1))
                        if not first:
                            pool.wait_ge(u_ready, b * 4 + (j - 1))
                        pool.tensor_tensor(flat(in_lo, j), flat(raw_in, j), flat(in_hi, j).bitcast(F32),
                                           ALU.subtract).then_inc(in_lo_done, 1)

                def cut_out(b, first, last):
                    for j in range(TPS):
                        pool.wait_ge(out_loaded[j], b * 16 + 16)
                        pool.tensor_tensor(raw_out[:, j, :], raw_out[:, j, :], gate[:, :], ALU.mult)\
                            .then_inc(out_gated, 1)
                    for j in range(TPS):
                        pool.wait_ge(out_hi_done, b * TPS + (j + 1))
                        if not first:
                            pool.wait_ge(y_ready, b * NG)
                        pool.tensor_tensor(out_lo[:, j, :], raw_out[:, j, :], out_hi[:, j, :].bitcast(F32),
                                           ALU.subtract).then_inc(out_lo_done, 1)

                def body(b, first, last):
                    cut_out(b, first, last)
                    if not last:
                        cut_in(b + 1, False)

                pool.wait_ge(gate_loaded, 16)
                cut_in(0, True)
                steps(pool, body)
                for t in range(NS + 1):
                    if t < NS:
                        norm.inverse(pool, t)
                    if t >= 1 and next_mod is not None:
                        norm.add_shift(pool, t - 1)

            @block.scalar
            def _(act):
                def cut_in(b, first):
                    for j in range(TPS):
                        act.wait_ge(in_loaded[j], b * 32 + 32)
                        if not first:
                            act.wait_ge(u_ready, b * 4 + (j - 1))
                        act.copy(flat(in_hi, j), flat(raw_in, j)).then_inc(in_hi_done, 1)

                def silu(b, q):
                    act.wait_ge(g_ready, b * 4 + (q + 1))
                    if not (isinstance(b, int) and b * 4 + q < 2):
                        act.wait_ge(mult_done, b * 4 + (q - 1))
                    act.activation(silu_g[:, q % 2, :], core.bank[:, 2 * (q % 2), :], ACT.Silu)\
                        .then_inc(silu_done, 1)

                def hidden_hi(b, q, first):
                    h, j = q // 2, q % 2
                    act.wait_ge(mult_done, b * 4 + (q + 1))
                    if not first:
                        act.wait_ge(y_ready, b * NG + (h - 1) * (NG // 2))
                    act.copy(act_hi[:, j, h * BANK:(h + 1) * BANK], act_f[:, q % 2, :]).then_inc(act_hi_done, 1)

                def body(b, first, last):
                    for j in range(TPS):
                        act.wait_ge(out_gated, b * TPS + (j + 1))
                        if not first:
                            act.wait_ge(y_ready, b * NG)
                        act.copy(out_hi[:, j, :], raw_out[:, j, :]).then_inc(out_hi_done, 1)
                    for q in range(5):
                        if q < 4:
                            silu(b, q)
                        if q >= 1:
                            hidden_hi(b, q - 1, first)
                    if not last:
                        cut_in(b + 1, False)

                cut_in(0, True)
                steps(act, body)
                for t in range(NS + 2):
                    if t < NS:
                        act.wait_ge(y_added, (STEPS - 1) * NG + 2 * t + 2)
                        if t == 0:
                            act.wait_ge(out_lo_done, STEPS * TPS)
                        norm.square(act, t)
                    if t >= 2 and next_mod is not None:
                        norm.keep_hi(act, t - 2)

            @block.vector
            def _(dve):
                def hidden(b, q):
                    h, j = q // 2, q % 2
                    dve.wait_ge(silu_done, b * 4 + (q + 1))
                    dve.wait_ge(u_ready, b * 4 + (q + 1))
                    if not (isinstance(b, int) and b * 4 + q < 2):
                        dve.wait_ge(act_lo_done, b * 4 + (q - 1))
                    dve.tensor_tensor(act_f[:, q % 2, :], core.bank[:, 2 * (q % 2) + 1, :], silu_g[:, q % 2, :],
                                      ALU.mult).then_inc(mult_done, 1)
                    dve.wait_ge(act_hi_done, b * 4 + (q + 1))
                    half = slice(h * BANK, (h + 1) * BANK)
                    dve.tensor_tensor(act_lo[:, j, half], act_f[:, q % 2, :], act_hi[:, j, half].bitcast(F32),
                                      ALU.subtract).then_inc(act_lo_done, 1)

                def add(b, g):
                    part = core.xres[:, g // 2, (g % 2) * BANK:(g % 2 + 1) * BANK]
                    dve.wait_ge(y_ready, b * NG + (g + 1))
                    dve.tensor_tensor(part, core.bank[:, 4 + g % 4, :], part, ALU.add).then_inc(y_added, 1)

                def body(b, first, last):
                    for q in range(4):
                        hidden(b, q)
                    if not last:
                        for g in range(NG):
                            add(b, g)

                steps(dve, body)
                for t in range(NS + 4):
                    if t < NS:
                        add(STEPS - 1, 2 * t)
                        add(STEPS - 1, 2 * t + 1)
                    if 2 <= t < NS + 2:
                        if next_mod is not None:
                            if t == 2:
                                dve.wait_ge(in_lo_done, STEPS * TPS)
                            norm.scale(dve, t - 2)
                        else:
                            if t == 2:
                                dve.wait_ge(norm.loaded, 16)
                            dve.wait_ge(norm.rms_done, t - 1)
                            dve.scalar_tensor_tensor(core.xres[:, t - 2, :], core.xres[:, t - 2, :],
                                                     core.rms[:, 2, t - 2:t - 1], scale1[:, :],
                                                     ALU.mult, ALU.mult).then_inc(norm.scaled, 1)
                    if 4 <= t and next_mod is not None:
                        norm.keep_lo(dve, t - 4)

            @block.tensor
            def _(pe):
                def quarter(b, q):
                    h, j = q // 2, q % 2
                    half = slice(h * BANK, (h + 1) * BANK)
                    if h == 0:
                        pe.wait_ge(in_lo_done, b * TPS + (j + 1))
                    for g in range(2):
                        if not (isinstance(b, int) and b * 4 + q < 2):
                            pe.wait_ge(silu_done if g == 0 else mult_done, b * 4 + (q - 1))
                        dst = core.bank[:, 2 * (q % 2) + g, :]
                        for k in range(KD):
                            w_hi, w_lo = in_hi[:, j, k, g, :], in_lo[:, j, k, g, :]
                            pe.matmul(dst, w_hi, core.h_hi[:, k, half], start=(k == 0), stop=False)
                            pe.matmul(dst, w_hi, core.h_lo[:, k, half], start=False, stop=False)
                            mm = pe.matmul(dst, w_lo, core.h_hi[:, k, half], start=False, stop=(k == KD - 1))
                        mm.then_inc(u_ready if g else g_ready, 1)

                def group(b, g):
                    t, dh = g // 2, g % 2
                    tok, cols = slice(t * P, (t + 1) * P), slice(dh * BANK, (dh + 1) * BANK)
                    if g == 0:
                        pe.wait_ge(out_lo_done, b * TPS + TPS)
                    if g in (0, NG // 2):
                        pe.wait_ge(act_lo_done, b * 4 + (2 if g == 0 else 4))
                    if not (isinstance(b, int) and b == 0 and g < 4):
                        pe.wait_ge(y_added, b * NG + (g - 3))
                    dst = core.bank[:, 4 + g % 4, :]
                    for j in range(TPS):
                        a_hi, a_lo = act_hi[:, j, tok], act_lo[:, j, tok]
                        pe.matmul(dst, a_hi, out_hi[:, j, cols], start=(j == 0), stop=False)
                        pe.matmul(dst, a_hi, out_lo[:, j, cols], start=False, stop=False)
                        mm = pe.matmul(dst, a_lo, out_hi[:, j, cols], start=False, stop=(j == TPS - 1))
                    mm.then_inc(y_ready, 1)

                def body(b, first, last):
                    for q in range(4):
                        quarter(b, q)
                    for g in range(NG):
                        group(b, g)
                        if last and next_mod is not None and g % 2 and g >= 9:
                            norm.turn(pe, (g - 9) // 2)

                steps(pe, body)
                if next_mod is not None:
                    for t in range(4, NS):
                        norm.turn(pe, t)


class Chain:

    def __init__(self, eng, sem):
        self.eng, self.sem, self.base, self.done, self.per = eng, sem, 0, 0, 0

    def at(self, i):
        if isinstance(i, int) and i == 0:
            self.start, self.per = self.done, 0
        elif self.per == 0:
            self.per = self.done - self.start
        if not (isinstance(i, int) and i == 0):
            self.base, self.done = i * self.per, self.start

    def leave(self, n):
        self.base, self.done = 0, self.start + n * self.per

    def __call__(self, ins):
        ins.then_inc(self.sem, 1)
        self.done += 1
        self.eng.wait_ge(self.sem, self.base + self.done)


def mixer(core, w_mix_in, b_fox_f, b_m_i, b_m_f, w_conv, b_conv, g_mhn, w_mix_out, gate_row, next_mod):
    nc, KD, D, S, NS = core.nc, core.KD, core.D, core.S, core.NS
    FH, MH = b_fox_f.shape[1], b_m_i.shape[1]
    FW = D // 2
    HD = FW // FH
    MW = D - FW
    PAIRS = FH // 2
    TAPS = w_conv.shape[1]
    COL_Q, COL_K, COL_V, COL_F = 0, FW, 2 * FW, 3 * FW
    COL_MQ = COL_F + FH
    COL_MK, COL_MV, COL_MO, COL_MG = COL_MQ + MW, COL_MQ + 2 * MW, COL_MQ + 3 * MW, COL_MQ + 4 * MW
    NG = FH + 2 * MH
    NR = FH + MH
    V1 = P + 1
    K_SCALE = float(P) ** -0.5
    w_in = w_mix_in.rearrange("a (k p) n -> (a p) k n", p=P)
    w_out = w_mix_out.rearrange("a (k p) n -> (a p) k n", p=P)
    gate_rows = nc.dram_tensor("gate_rows", (NR * S,), F32, kind="Internal").ap()

    with ExitStack() as ctx:
        sb = lambda n, *a: core.sb(f"mx_{n}", *a, ctx=ctx)
        raw_w = sb("raw_w", [P, 2, KD * P])
        w_hi = sb("w_hi", [P, 2, KD * P], F32R)
        w_lo = sb("w_lo", [P, 2, KD * P], F32R)
        yT_fox = sb("yT_fox", [P, PAIRS, S])
        NCONST = (TAPS + 1) * 2 * MH + MH
        consts = sb("consts", [P, NCONST])
        mask_m = sb("mask_m", [P, P])
        m_total = sb("m_total", [P, MH, NS])
        m_cum = sb("m_cum", [P, MH, NS])
        m_b = sb("m_b", [P, MH, NS])

        s = lambda n: core.sem(f"mx_{n}")
        w_loaded = [s("w_loaded0"), s("w_loaded1")]
        w_hi_done = [s("w_hi_done0"), s("w_hi_done1")]
        w_lo_done = [s("w_lo_done0"), s("w_lo_done1")]
        w_used = [s("w_used0"), s("w_used1")]
        small_loaded = s("small_loaded")
        pool_set = s("pool_set")
        gw_cut = s("gw_cut")
        gw_hi_done = s("gw_hi_done")
        z_ready, z_done = s("z_ready"), s("z_done")
        neg_done, exp_done, ln_done = s("neg_done"), s("exp_done"), s("ln_done")
        logf_done = s("logf_done")
        sums_ready, rows_ready = s("sums_ready"), s("rows_ready")
        rows_turned, rows_kept, rows_stored = s("rows_turned"), s("rows_kept"), s("rows_stored")
        const_turned, const_kept = s("const_turned"), s("const_kept")
        dve_step, act_step, pool_step = s("dve_step"), s("act_step"), s("pool_step")
        v_ready, v_kept_even, v_kept_odd = s("v_ready"), s("v_kept_even"), s("v_kept_odd")
        fq_ready, fq_kept = s("fq_ready"), s("fq_kept")
        cum_loaded = s("cum_loaded")
        score_ready, logit_done, prob_done = s("score_ready"), s("logit_done"), s("prob_done")
        pt_ready, pt_act, pt_dve = s("pt_ready"), s("pt_act"), s("pt_dve")
        pv_ready, y_done = s("pv_ready"), s("y_done")
        yt_ready, yt_kept = s("yt_ready"), s("yt_kept")
        x_ready, x_kept = s("x_ready"), s("x_kept")
        b_loaded = s("b_loaded")
        max_done, args_done, weights_done = s("max_done"), s("args_done"), s("weights_done")
        conv_done, silu_done = s("conv_done"), s("silu_done")
        sig_done, sg_done = s("sig_done"), s("sg_done")
        kt_ready, kw_done = s("kt_ready"), s("kw_done")
        qk_ready, sp_done = s("qk_ready"), s("sp_done")
        u_ready, state_done = s("u_ready"), s("state_done")
        spt_ready, spt_kept = s("spt_ready"), s("spt_kept")
        num_ready, inter_kept, o_done = s("num_ready"), s("inter_kept"), s("o_done")
        sq_done, var_done, rpow_done = s("sq_done"), s("var_done"), s("rpow_done")
        yb_done, ybt_ready, ybt_kept = s("yb_done"), s("ybt_ready"), s("ybt_kept")
        gate_loaded, gated = s("gate_loaded"), s("gated")
        y_hi, y_lo = s("y_hi"), s("y_lo")
        out_ready, out_added = s("out_ready"), s("out_added")

        fox = ExitStack()
        fsb = lambda n, *a: core.sb(f"mx_{n}", *a, ctx=fox)
        gw_raw = fsb("gw_raw", [P, KD, NG])
        gw_hi, gw_lo = fsb("gw_hi", [P, KD, NG], F32R), fsb("gw_lo", [P, KD, NG], F32R)
        gbias = fsb("gbias", [P, NG])
        z = fsb("z", [P, NS, NG])
        zneg = fsb("zneg", [P, NS, NG])
        logf = fsb("logf", [P, NS, NG])
        cum_in = fsb("cum_in", [P, NS, NG])
        total = fsb("total", [P, NS, NG])
        before = fsb("before", [P, NS, FH])
        rows_in = fsb("rows_in", [P, NR, NS])
        rows_out = fsb("rows_out", [NR * NS, P])
        upper = fsb("upper", [P, P])
        ones = fsb("ones", [P, P])
        const_rows = fsb("const_rows", [(TAPS + 1) * 2 * MH + MH, P])
        mask_f = fsb("mask_f", [P, P], BF16)
        ident_b = fsb("ident_b", [P, P], BF16)
        v_fox = fsb("v_fox", [P, NS, FW])
        fqT, fkT = fsb("fqT", [P, S]), fsb("fkT", [P, S])
        cum_bc = fsb("cum_bc", [P, 2, S])
        RP = 3
        prob = fsb("prob", [P, RP, S])
        probT = fsb("probT", [P, 2, S])
        y_tok = fsb("y_tok", [P, NS, 2 * HD])
        low = fsb("low", [P, 4 * NS])
        rowsum = fsb("rowsum", [P, 2 * NS])
        rinv = fsb("rinv", [P, 2 * NS])
        wait_tile = fsb("wait_tile", [P, 2 * NS])
        fox.close()
        late = ExitStack()
        yT_ml = core.sb("mx_yT_ml", [P, MH, S], ctx=late)
        ml = ExitStack()
        msb = lambda n, *a: core.sb(f"mx_{n}", *a, ctx=ml)
        v_ml = msb("v_ml", [P, NS, MH, V1])
        pre_q = msb("pre_q", [P, TAPS - 1 + S])
        pre_k = msb("pre_k", [P, TAPS - 1 + S])
        mo = msb("mo", [P, S])
        sg = msb("sg", [P, S])
        mqT = msb("mqT", [P, S])
        mkT = msb("mkT", [P, NS * V1])
        kw = msb("kw", [P, NS * V1])
        dec = msb("dec", [P, S])
        arg = msb("arg", [P, 4, NS])
        mst = msb("mst", [P, NS + 1])
        tiny = msb("tiny", [P, 8, NS])
        sq_junk = msb("sq_junk", [P, P])
        ml.close()
        fin = ExitStack()
        gate = core.sb("mx_gate", [P, D], ctx=fin)
        shift, scale1 = core.sb("mx_shift", [P, D], ctx=fin), core.sb("mx_scale1", [P, D], ctx=fin)
        junk = core.sb("mx_junk", [P, D], ctx=fin)
        xn3 = core.sb("mx_xn", [P, 4, D], ctx=fin)
        fin.close()
        late.close()
        states = mkT[:, :].rearrange("p (c v) -> p c v", v=V1)
        o_all = kw[:, :].rearrange("p (c v) -> p c v", v=V1)
        kw_c = kw[:, 0:S]
        norm = Norm(core, "mxn", shift[:, :], scale1[:, :], junk[:, :], [xn3[:, i, :] for i in range(4)], 0)

        C_V = (0, 0)
        C_F = (2, 2)
        C_MV = (2 + PAIRS, 2 + PAIRS)
        C_M = (4 + PAIRS, 4 + PAIRS)
        C_O = (C_M[0] + 2 * MH, C_M[1] + MH)
        X_PER = 6

        def w_load(sp, slot, c, src):
            if not (isinstance(c, int) and c == 0):
                sp.wait_ge(w_lo_done[slot], c)
            dst = raw_w[:, slot, :].rearrange("p (k n) -> p k n", n=src.shape[2])
            sp.dma_start(dst, src).then_inc(w_loaded[slot], 16)

        def w_cut_hi(act, slot, c, freed=None, is_gated=None):
            if is_gated is None:
                act.wait_ge(w_loaded[slot], c * 16 + 16)
            else:
                act.wait_ge(gated, is_gated)
            if freed is not None:
                act.wait_ge(*freed)
            act.copy(w_hi[:, slot, :], raw_w[:, slot, :]).then_inc(w_hi_done[slot], 1)

        def w_cut_lo(pool, slot, c):
            pool.wait_ge(w_hi_done[slot], c + 1)
            pool.tensor_tensor(w_lo[:, slot, :], raw_w[:, slot, :], w_hi[:, slot, :].bitcast(F32),
                               ALU.subtract).then_inc(w_lo_done[slot], 1)

        def three(pe, dst, a_hi, a_lo, b_hi, b_lo, start, stop):
            pe.matmul(dst, a_hi, b_hi, start=start, stop=False)
            pe.matmul(dst, a_hi, b_lo, start=False, stop=False)
            return pe.matmul(dst, a_lo, b_hi, start=False, stop=stop)

        def by_token(pe, c, ready, before):
            for k in range(KD):
                slot = k // 2 % 2
                if k % 2 == 0:
                    pe.wait_ge(w_lo_done[slot], c[slot] + k // 4 + 1)
                cols = slice(k % 2 * BANK, (k % 2 + 1) * BANK)
                for t in range(NS):
                    before(k, t)
                    tok = slice(t * P, (t + 1) * P)
                    mm = three(pe, core.bank[:, t, :], core.h_hi[:, k, tok], core.h_lo[:, k, tok],
                               w_hi[:, slot, cols], w_lo[:, slot, cols], k == 0, k == KD - 1)
                    if k == KD - 1:
                        mm.then_inc(ready, 1)
                if k % 2 and k < KD - 1:
                    mm.then_inc(w_used[slot], 1)

        def by_feature(pe, dst, slot, half):
            tok = slice(half * BANK, (half + 1) * BANK)
            for k in range(KD):
                cols = slice(k * P, (k + 1) * P)
                mm = three(pe, dst, w_hi[:, slot, cols], w_lo[:, slot, cols],
                           core.h_hi[:, k, tok], core.h_lo[:, k, tok], k == 0, k == KD - 1)
            return mm

        def repeat(eng, n, body):
            body(0, True, False)
            with eng.Fori(1, n - 1) as i:
                body(i, False, False)
            body(n - 1, False, True)

        PER = 2 * NS
        STEP = lambda p, n: p * PER + n

        with nc.Block() as block:

            @block.sync
            def _(sp):
                with nc.allow_non_contiguous_dma(reason="16 gate columns"):
                    sp.dma_start(gw_raw[:, :, 0:FH], w_in[:, :, COL_F:COL_F + FH]).then_inc(small_loaded, 16)
                    sp.dma_start(gw_raw[:, :, FH:NG], w_in[:, :, COL_MG:COL_MG + 2 * MH]).then_inc(small_loaded, 16)
                for lo, hi, src in ((0, FH, b_fox_f), (FH, FH + MH, b_m_i), (FH + MH, NG, b_m_f)):
                    sp.dma_start(gbias[:, lo:hi], src.rearrange("a n -> (a n)").partition_broadcast(P))\
                        .then_inc(small_loaded, 16)
                R0, R1 = TAPS * 2 * MH, (TAPS + 1) * 2 * MH
                sp.dma_start(const_rows[0:R0, :], w_conv.rearrange("a w (c p) -> (a w c) p", p=P)).then_inc(small_loaded, 16)
                sp.dma_start(const_rows[R0:R1, :], b_conv.rearrange("a (c p) -> (a c) p", p=P)).then_inc(small_loaded, 16)
                sp.dma_start(const_rows[R1:, :], g_mhn.rearrange("a (c p) -> (a c) p", p=P)).then_inc(small_loaded, 16)
                for piece in range(4):
                    w_load(sp, piece % 2, C_V[0] + piece // 2, w_in[:, 2 * piece:2 * piece + 2, COL_V:COL_V + FW])
                for slot, col in ((0, COL_Q), (1, COL_K)):
                    w_load(sp, slot, C_F[slot], w_in[:, :, col:col + P])
                sp.wait_ge(rows_kept, 1)
                sp.dma_start(gate_rows.rearrange("(r n) -> r n", n=P), rows_out[:, :]).then_inc(rows_stored, 16)
                sp.wait_ge(rows_stored, 16)

                def fox_loads(p, first, last):
                    if not first:
                        sp.wait_ge(logit_done, p * PER)
                    sp.dma_start(cum_bc[:, :, :], gate_rows[bass.ds(p * (2 * S), 2 * S)]
                                 .rearrange("(e s) -> e s", e=2).partition_broadcast(P)).then_inc(cum_loaded, 16)
                    if not last:
                        for slot, col in ((0, COL_Q), (1, COL_K)):
                            w_load(sp, slot, p + (C_F[slot] + 1), w_in[:, :, bass.ds(p * P + (col + P), P)])

                repeat(sp, PAIRS, fox_loads)
                for piece in range(4):
                    w_load(sp, piece % 2, C_MV[0] + piece // 2, w_in[:, 2 * piece:2 * piece + 2, COL_MV:COL_MV + MW])

                def ml_w(h, c, col):
                    w_load(sp, c % 2, c // 2 + (h * 2 + C_M[0] if c % 2 == 0 else h + C_M[1]),
                           w_in[:, :, bass.ds(h * P + col, P)])

                def ml_loads(h, first, last):
                    if not last:
                        ml_w(h + 1, 0, COL_MQ)
                        ml_w(h + 1, 1, COL_MK)
                    if first:
                        sp.wait_ge(yt_kept, 2 * PAIRS)
                        sp.wait_ge(y_done, PAIRS * PER)
                    else:
                        sp.wait_ge(num_ready, h * 3)
                    sp.dma_start(dec[:, :], gate_rows[bass.ds(h * S + FH * S, S)].partition_broadcast(P))\
                        .then_inc(b_loaded, 16)
                    if not last:
                        ml_w(h + 1, 2, COL_MO)

                for c, col in ((0, COL_MQ), (1, COL_MK), (2, COL_MO)):
                    ml_w(0, c, col)
                repeat(sp, MH, ml_loads)
                sp.wait_ge(ybt_kept, 2 * MH)
                sp.dma_start(gate[:, :], core.mod(gate_row)).then_inc(gate_loaded, 16)
                norm.load(sp, next_mod)
                for n in range(8):
                    dh, piece = n // 4, n % 4
                    w_load(sp, n % 2, C_O[n % 2] + n // 2,
                           w_out[:, 2 * piece:2 * piece + 2, dh * BANK:(dh + 1) * BANK])

            @block.gpsimd
            def _(pool):
                link = Chain(pool, pool_step)
                link(pool.memset(ones[:, :], 1.0))
                link(pool.affine_select(out=upper[:, :], in_=ones[:, :], compare_op=ALU.is_ge, fill=0.0,
                                        base=0, pattern=[[1, P]], channel_multiplier=-1))
                link(pool.memset(mask_m[:, :], 0.0))
                link(pool.affine_select(out=mask_m[:, :], in_=mask_m[:, :], compare_op=ALU.is_ge, fill=NEG,
                                        base=0, pattern=[[-1, P]], channel_multiplier=1))
                link(pool.tensor_scalar(mask_f[:, :], mask_m[:, :], -1.0, None, ALU.mult))
                pool.tensor_copy(ident_b[:, :], core.ident[:, :]).then_inc(pool_set, 1)
                pool.wait_ge(pool_set, 1)
                pool.wait_ge(gw_hi_done, 1)
                flat = lambda t: t[:, :, :].rearrange("p k n -> p (k n)")
                pool.tensor_tensor(flat(gw_lo), flat(gw_raw), flat(gw_hi).bitcast(F32), ALU.subtract)\
                    .then_inc(gw_cut, 1)
                for piece in range(4):
                    w_cut_lo(pool, piece % 2, C_V[0] + piece // 2)
                w_cut_lo(pool, 0, C_F[0])
                w_cut_lo(pool, 1, C_F[1])

                def fox_cut(p, first, last):
                    if not last:
                        w_cut_lo(pool, 0, p + (C_F[0] + 1))
                        w_cut_lo(pool, 1, p + (C_F[1] + 1))

                repeat(pool, PAIRS, fox_cut)
                for piece in range(4):
                    w_cut_lo(pool, piece % 2, C_MV[0] + piece // 2)
                w_cut_lo(pool, 0, C_M[0])
                w_cut_lo(pool, 1, C_M[1])
                w_cut_lo(pool, 0, C_M[0] + 1)

                def ml_cut(h, first, last):
                    if not last:
                        w_cut_lo(pool, 0, h * 2 + (C_M[0] + 2))
                        w_cut_lo(pool, 1, h + (C_M[1] + 1))
                        w_cut_lo(pool, 0, h * 2 + (C_M[0] + 3))
                    pool.wait_ge(var_done, h + 1)
                    pool.tensor_tensor(tiny[:, 5, :], tiny[:, 4, :], core.neg_half[:, :], ALU.pow)\
                        .then_inc(rpow_done, 1)

                repeat(pool, MH, ml_cut)
                pool.wait_ge(gate_loaded, 16)
                for n in range(8):
                    slot, c, dh = n % 2, C_O[n % 2] + n // 2, n // 4
                    pool.wait_ge(w_loaded[slot], 16 * (c + 1))
                    for kk in range(2):
                        piece = raw_w[:, slot, kk * BANK:(kk + 1) * BANK]
                        pool.tensor_tensor(piece, piece, gate[:, dh * BANK:(dh + 1) * BANK], ALU.mult)\
                            .then_inc(gated, 1)
                    w_cut_lo(pool, slot, c)
                for t in range(NS + 1):
                    if t < NS:
                        norm.inverse(pool, t)
                    if t >= 1:
                        norm.add_shift(pool, t - 1)

            @block.scalar
            def _(act):
                link = Chain(act, act_step)
                flat = lambda t: t[:, :, :].rearrange("p k n -> p (k n)")
                act.wait_ge(small_loaded, 16 * 8)
                act.copy(flat(gw_hi), flat(gw_raw)).then_inc(gw_hi_done, 1)
                w_cut_hi(act, 0, 0)
                w_cut_hi(act, 1, 0)
                act.wait_ge(neg_done, 1)
                act.activation(flat(zneg), flat(zneg), ACT.Exp).then_inc(exp_done, 1)
                act.wait_ge(exp_done, 1)
                act.activation(flat(zneg), flat(zneg), ACT.Ln, bias=1.0).then_inc(ln_done, 1)
                w_cut_hi(act, 0, 1, freed=(w_used[0], 1))
                w_cut_hi(act, 1, 1, freed=(w_used[1], 1))
                w_cut_hi(act, 0, C_F[0], freed=(w_used[0], 2))
                for t in range(0, NS, 2):
                    act.wait_ge(v_ready, t + 1)
                    act.copy(v_fox[:, t, :], core.bank[:, t, :]).then_inc(v_kept_even, 1)
                w_cut_hi(act, 1, C_F[1], freed=(v_ready, NS))

                def keep_qk(p, g):
                    half = slice((g % 2) * BANK, (g % 2 + 1) * BANK)
                    act.wait_ge(fq_ready, p * 4 + (g + 1))
                    if g < 2:
                        act.mul(fqT[:, half], core.bank[:, g, :], -float(HD) ** -0.5).then_inc(fq_kept, 1)
                    else:
                        act.copy(fkT[:, half], core.bank[:, g, :]).then_inc(fq_kept, 1)

                for g in range(4):
                    keep_qk(0, g)

                def exp_rows(p, n):
                    w = (n % NS + 1) * P
                    act.wait_ge(logit_done, p * PER + (n + 1))
                    rows = prob[:, n % RP, 0:w]
                    act.activation(rows, rows, ACT.Exp, bias=low[:, n:n + 1], scale=-1.0,
                                   accum_out=rowsum[:, n:n + 1]).then_inc(prob_done, 1)

                def keep_pt(p, n, first):
                    w = min((n % NS + 1) * P, BANK)
                    act.wait_ge(pt_ready, p * PER + (n + 1))
                    if not (first and n < 2):
                        act.wait_ge(pv_ready, p * PER + (n - 1))
                    act.copy(probT[:, n % 2, 0:w], core.bank[:, 4, 0:w]).then_inc(pt_act, 1)

                def fox_body(p, first, last):
                    for m in range(PER + 2):
                        if 1 <= m <= PER:
                            exp_rows(p, m - 1)
                        if m == 3 and not last:
                            w_cut_hi(act, 0, p + (C_F[0] + 1), freed=(fq_ready, p * 4 + 2))
                            w_cut_hi(act, 1, p + (C_F[1] + 1), freed=(fq_ready, p * 4 + 4))
                        if m >= 2:
                            keep_pt(p, m - 2, first)
                    if not last:
                        for g in range(4):
                            keep_qk(p + 1, g)
                    for half in range(2):
                        act.wait_ge(yt_ready, p * 2 + (half + 1))
                        act.copy(yT_fox[:, bass.ds(p, 1), half * BANK:(half + 1) * BANK].rearrange("p a s -> p (a s)"),
                                 core.bank[:, 4 + half, :]).then_inc(yt_kept, 1)

                repeat(act, PAIRS, fox_body)
                w_cut_hi(act, 0, C_MV[0], freed=(fq_ready, 4 * PAIRS - 2))
                w_cut_hi(act, 1, C_MV[1], freed=(fq_ready, 4 * PAIRS))
                w_cut_hi(act, 0, C_MV[0] + 1, freed=(w_used[0], 3))
                w_cut_hi(act, 1, C_MV[1] + 1, freed=(w_used[1], 2))
                w_cut_hi(act, 0, C_M[0], freed=(w_used[0], 4))
                act.wait_ge(y_done, PAIRS * PER)
                for t in range(0, NS, 2):
                    act.wait_ge(v_ready, NS + t + 1)
                    act.copy(v_ml[:, t, :, 0:P], core.bank[:, t, :].rearrange("p (h v) -> p h v", v=P))\
                        .then_inc(v_kept_even, 1)
                w_cut_hi(act, 1, C_M[1], freed=(v_ready, 2 * NS))

                def keep_x(h, g, first):
                    off = (TAPS - 1 if g < 4 else 0) + (g % 2) * BANK
                    act.wait_ge(x_ready, h * X_PER + (g + 1))
                    if not first and g in (0, 2):
                        act.wait_ge(conv_done, h * 2 + (-1 if g == 0 else 0))
                    act.copy((pre_q, pre_k, mo)[g // 2][:, off:off + BANK], core.bank[:, g % 4, :])\
                        .then_inc(x_kept, 1)
                    if g == 1:
                        w_cut_hi(act, 0, h * 2 + (C_M[0] + 1), freed=(x_ready, h * X_PER + 2))

                for g in range(X_PER):
                    keep_x(0, g, True)

                def ml_body(h, first, last):
                    link.at(h)
                    bias = lambda c: consts[:, bass.ds(h + (TAPS * 2 * MH + c), 1)]
                    if not last:
                        w_cut_hi(act, 0, h * 2 + (C_M[0] + 2), freed=(x_ready, h * X_PER + 6))
                        w_cut_hi(act, 1, h + (C_M[1] + 1), freed=(x_ready, h * X_PER + 4))
                    if not first:
                        act.wait_ge(ybt_kept, h * 2)
                    act.wait_ge(x_kept, h * X_PER + X_PER)
                    act.activation(sg[:, :], mo[:, :], ACT.Sigmoid).then_inc(sig_done, 1)
                    for i, buf in enumerate((mqT[:, :], mkT[:, 0:S])):
                        act.wait_ge(conv_done, h * 2 + (i + 1))
                        act.activation(buf, buf, ACT.Silu, bias=bias(i * MH)).then_inc(silu_done, 1)
                        if not last:
                            keep_x(h + 1, 2 * i, False)
                            keep_x(h + 1, 2 * i + 1, False)
                    act.wait_ge(args_done, h + 1)
                    act.activation(arg[:, :, :], arg[:, :, :], ACT.Exp).then_inc(weights_done, 1)
                    act.activation(dec[:, :], dec[:, :], ACT.Exp).then_inc(weights_done, 1)
                    if not last:
                        act.wait_ge(sig_done, h + 1)
                        keep_x(h + 1, 4, False)
                    for half in range(2):
                        act.wait_ge(spt_ready, h * 2 + 2)
                        act.copy(dec[:, half * BANK:(half + 1) * BANK], core.bank[:, (7, 4)[half], :])\
                            .then_inc(spt_kept, 1)
                    if not last:
                        keep_x(h + 1, 5, False)
                    for j in range(NS):
                        r, jj = j // 3, j % 3
                        act.wait_ge(num_ready, h * 3 + (r + 1))
                        act.mul(o_all[:, j, :], core.bank[:, (6, 4, 6)[r], jj * V1:(jj + 1) * V1],
                                arg[:, 2, j:j + 1]).then_inc(inter_kept, 1)
                    for j in range(NS):
                        act.wait_ge(o_done, h * 3 + (j // 3 + 1))
                        link(act.activation(sq_junk[:, :], o_all[:, j, 0:P], ACT.Square,
                                            accum_out=tiny[:, 0, j:j + 1]))
                    act.activation(sq_junk[:, 0:NS], tiny[:, 0, :], ACT.Copy).then_inc(sq_done, 1)

                repeat(act, MH, ml_body)
                for k in range(KD):
                    src = yT_fox[:, k, :] if k < PAIRS else yT_ml[:, k - PAIRS, :]
                    if k in (0, PAIRS):
                        act.wait_ge(*((yt_kept, 2 * PAIRS) if k == 0 else (ybt_kept, 2 * MH)))
                    act.copy(core.h_hi[:, k, :], src).then_inc(y_hi, 1)
                    if k < 2:
                        w_cut_hi(act, k, C_O[k], freed=(x_ready, MH * X_PER - 2 * k), is_gated=2 * k + 2)
                for n, freed in ((2, (w_used[0], 5)), (3, (w_used[1], 3)), (4, (w_used[0], 6)),
                                 (5, (out_ready, NS)), (6, (w_used[0], 7)), (7, (w_used[1], 4))):
                    w_cut_hi(act, n % 2, C_O[n % 2] + n // 2, freed=freed, is_gated=2 * n + 2)
                for t in range(NS + 2):
                    if t < NS:
                        act.wait_ge(out_added, NS + t + 1)
                        norm.square(act, t)
                    if t >= 2:
                        norm.keep_hi(act, t - 2)

            @block.vector
            def _(dve):
                link = Chain(dve, dve_step)
                gates = lambda t, a, b: t[:, :, a:b].rearrange("p t g -> p g t")
                dve.wait_ge(small_loaded, 16 * 8)
                dve.wait_ge(const_turned, 1)
                dve.tensor_copy(consts[:, :], core.bank[:, 1, 0:NCONST]).then_inc(const_kept, 1)
                dve.wait_ge(z_ready, 1)
                dve.tensor_tensor(z[:, :, :], core.bank[:, 0, 0:NS * NG].rearrange("p (t g) -> p t g", g=NG),
                                  gbias[:, :].unsqueeze(1).to_broadcast([P, NS, NG]), ALU.add).then_inc(z_done, 1)
                dve.wait_ge(z_done, 1)
                link(dve.tensor_scalar(logf[:, :, :], z[:, :, :], 0.0, None, ALU.min))
                dve.scalar_tensor_tensor(zneg[:, :, :], logf[:, :, :], 2.0, z[:, :, :], ALU.mult, ALU.subtract)\
                    .then_inc(neg_done, 1)
                dve.wait_ge(ln_done, 1)
                dve.tensor_tensor(logf[:, :, :], logf[:, :, :], zneg[:, :, :], ALU.subtract).then_inc(logf_done, 1)
                for t in range(1, NS, 2):
                    dve.wait_ge(v_ready, t + 1)
                    dve.tensor_copy(v_fox[:, t, :], core.bank[:, t, :]).then_inc(v_kept_odd, 1)
                dve.wait_ge(sums_ready, 1)
                tg = lambda b: core.bank[:, b, 0:NS * NG].rearrange("p (t g) -> p t g", g=NG)
                link(dve.tensor_copy(cum_in[:, :, :], tg(4)))
                link(dve.tensor_copy(total[:, :, :], tg(5)))
                link(dve.memset(before[:, 0, :], 0.0))
                for t in range(1, NS):
                    link(dve.tensor_tensor(before[:, t, :], before[:, t - 1, :], total[:, t - 1, 0:FH], ALU.add))
                link(dve.tensor_tensor(rows_in[:, 0:FH, :], gates(cum_in, 0, FH), gates(before, 0, FH), ALU.add))
                link(dve.tensor_tensor(rows_in[:, FH:NR, :], gates(z, FH, FH + MH), gates(cum_in, FH + MH, NG),
                                       ALU.subtract))
                link(dve.tensor_copy(m_b[:, :, :], rows_in[:, FH:NR, :]))
                link(dve.tensor_copy(m_total[:, :, :], gates(total, FH + MH, NG)))
                dve.tensor_copy(m_cum[:, :, :], gates(cum_in, FH + MH, NG)).then_inc(rows_ready, 1)
                dve.wait_ge(rows_turned, 1)
                dve.tensor_copy(rows_out[:, :], core.bank[0:NR * NS, 6, 0:P]).then_inc(rows_kept, 1)

                def logits(p, n, first):
                    w = (n % NS + 1) * P
                    if n == 0:
                        dve.wait_ge(cum_loaded, p * 16 + 16)
                    dve.wait_ge(score_ready, p * PER + (n + 1))
                    if not (first and n < RP):
                        dve.wait_ge(pt_ready, p * PER + (n - RP + 1))
                    b = 2 * (n % 2)
                    dve.memset(wait_tile[:, n:n + 1], 0.0)
                    dve.tensor_tensor_reduce(prob[:, n % RP, 0:w],
                                             core.bank[:, b:b + 2, :].rearrange("p b n -> p (b n)")[:, 0:w],
                                             cum_bc[:, n // NS, 0:w], 1.0, 3e38, ALU.add, ALU.min,
                                             low[:, n:n + 1]).then_inc(logit_done, 1)

                def keep_pt(p, n, first):
                    w = (n % NS + 1) * P
                    if w <= BANK:
                        return
                    dve.wait_ge(pt_ready, p * PER + (n + 1))
                    dve.wait_ge(pv_ready, p * PER + (n - 1))
                    dve.tensor_copy(probT[:, n % 2, BANK:w], core.bank[:, 5, 0:w - BANK]).then_inc(pt_dve, 1)

                def normalise(p, n, first):
                    dve.wait_ge(pv_ready, p * PER + (n + 1))
                    if not first and n == 0:
                        dve.wait_ge(yt_ready, p * 2)
                    link(dve.reciprocal(rinv[:, n:n + 1], rowsum[:, n:n + 1]))
                    dve.tensor_scalar(y_tok[:, n % NS, (n // NS) * HD:(n // NS + 1) * HD],
                                      core.bank[:, 6 + n % 2, 0:HD], rinv[:, n:n + 1], None, ALU.mult)\
                        .then_inc(y_done, 1)

                def fox_body(p, first, last):
                    link.at(p)
                    for m in range(PER + 3):
                        if m < PER:
                            logits(p, m, first)
                        if 2 <= m < PER + 2:
                            keep_pt(p, m - 2, first)
                        if m >= 3:
                            normalise(p, m - 3, first)

                repeat(dve, PAIRS, fox_body)
                link.leave(PAIRS)
                dve.wait_ge(yt_kept, 2 * PAIRS)
                link(dve.memset(v_ml[:, :, :, P:V1], 1.0))
                link(dve.memset(pre_q[:, 0:TAPS - 1], 0.0))
                link(dve.memset(pre_k[:, 0:TAPS - 1], 0.0))
                link(dve.memset(mst[:, 0:1], 0.0))
                for t in range(1, NS, 2):
                    dve.wait_ge(v_ready, NS + t + 1)
                    dve.tensor_copy(v_ml[:, t, :, 0:P], core.bank[:, t, :].rearrange("p (h v) -> p h v", v=P))\
                        .then_inc(v_kept_odd, 1)

                chunks = lambda t: t.rearrange("p (c s) -> p c s", s=P)

                def ml_body(h, first, last):
                    link.at(h)
                    if not first:
                        dve.wait_ge(num_ready, h * 3)
                    for i, (src, dst) in enumerate(((pre_q, mqT[:, :]), (pre_k, mkT[:, 0:S]))):
                        dve.wait_ge(x_kept, h * X_PER + (2 * i + 2))
                        for w in range(TAPS):
                            tap = consts[:, bass.ds(h + (w * 2 * MH + i * MH), 1)]
                            if w == 0:
                                link(dve.tensor_scalar(dst, src[:, 0:S], tap, None, ALU.mult))
                            elif w < TAPS - 1:
                                link(dve.scalar_tensor_tensor(dst, src[:, w:w + S], tap, dst, ALU.mult, ALU.add))
                            else:
                                dve.scalar_tensor_tensor(dst, src[:, w:w + S], tap, dst, ALU.mult, ALU.add)\
                                    .then_inc(conv_done, 1)
                    head = lambda t: t[:, bass.ds(h, 1), :].rearrange("p a c -> p (a c)")
                    prev = mst[:, 0:NS]
                    dve.wait_ge(b_loaded, h * 16 + 16)
                    link(dve.tensor_reduce(tiny[:, 1, :], chunks(dec[:, :]), AX.X, ALU.max))
                    link(dve.tensor_tensor_scan(mst[:, 1:NS + 1], tiny[:, 1, :], head(m_total), 0.0, ALU.max, ALU.add))
                    link(dve.tensor_tensor(tiny[:, 1, :], tiny[:, 1, :], prev, ALU.max))
                    link(dve.tensor_tensor(arg[:, 0, :], prev, tiny[:, 1, :], ALU.subtract))
                    link(dve.tensor_tensor(arg[:, 1, :], head(m_b), tiny[:, 1, :], ALU.subtract))
                    link(dve.tensor_tensor(chunks(dec[:, :]), chunks(dec[:, :]),
                                           mask_m[:, :].unsqueeze(1).to_broadcast([P, NS, P]), ALU.add))
                    link(dve.tensor_reduce(tiny[:, 2, :], chunks(dec[:, :]), AX.X, ALU.max))
                    link(dve.tensor_tensor(tiny[:, 2, :], tiny[:, 2, :], prev, ALU.max))
                    link(dve.tensor_tensor(arg[:, 2, :], prev, tiny[:, 2, :], ALU.subtract))
                    link(dve.scalar_tensor_tensor(arg[:, 3, :], head(m_cum), -1.0, tiny[:, 2, :],
                                                  ALU.mult, ALU.subtract))
                    dve.tensor_tensor(chunks(dec[:, :]), chunks(dec[:, :]),
                                      tiny[:, 2, :].unsqueeze(2).to_broadcast([P, NS, P]), ALU.subtract)\
                        .then_inc(args_done, 1)
                    dve.wait_ge(sig_done, h + 1)
                    dve.tensor_scalar(sg[:, :], sg[:, :], consts[:, bass.ds(h + (TAPS + 1) * 2 * MH, 1)], None,
                                      ALU.mult).then_inc(sg_done, 1)
                    dve.wait_ge(weights_done, h * 2 + 2)
                    link(dve.tensor_scalar(arg[:, 1, :], arg[:, 1, :], K_SCALE, None, ALU.mult))
                    for half in range(2):
                        c4 = slice(4 * half, 4 * half + 4)
                        dve.wait_ge(kt_ready, h * 2 + (half + 1))
                        dve.tensor_tensor(chunks(kw_c)[:, c4, :], chunks(core.bank[:, 4 + half, :]),
                                          arg[:, 1, c4].unsqueeze(2).to_broadcast([P, 4, P]), ALU.mult)\
                            .then_inc(kw_done, 1)
                    for half in range(2):
                        part = dec[:, half * BANK:(half + 1) * BANK]
                        dve.wait_ge(qk_ready, h * 2 + (half + 1))
                        dve.scalar_tensor_tensor(part, core.bank[:, 6 + half, :], K_SCALE, part, ALU.mult, ALU.mult)\
                            .then_inc(sp_done, 1)
                    dve.memset(states[:, 0, :], 0.0).then_inc(state_done, 1)
                    for j in range(NS - 1):
                        dve.wait_ge(u_ready, h * 3 + (j // 3 + 1))
                        dve.wait_ge(state_done, h * NS + (j + 1))
                        dve.scalar_tensor_tensor(states[:, j + 1, :], states[:, j, :], arg[:, 0, j:j + 1],
                                                 core.bank[:, 4 + j // 3, (j % 3) * V1:(j % 3 + 1) * V1],
                                                 ALU.mult, ALU.add).then_inc(state_done, 1)
                    for r in range(3):
                        j0, j1 = 3 * r, min(3 * r + 3, NS)
                        dve.wait_ge(inter_kept, h * NS + j1)
                        dve.tensor_tensor(o_all[:, j0:j1, :], o_all[:, j0:j1, :],
                                          core.bank[:, (5, 7, 5)[r], 0:(j1 - j0) * V1]
                                          .rearrange("p (c v) -> p c v", v=V1), ALU.add).then_inc(o_done, 1)
                    den = o_all[:, :, P:V1].rearrange("p c v -> p (c v)")
                    dve.wait_ge(o_done, h * 3 + 3)
                    link(dve.scalar_tensor_tensor(tiny[:, 1, :], den, -1.0, den, ALU.mult, ALU.max))
                    link(dve.tensor_tensor(tiny[:, 1, :], tiny[:, 1, :], arg[:, 3, :], ALU.max))
                    link(dve.reciprocal(tiny[:, 2, :], tiny[:, 1, :]))
                    dve.wait_ge(sq_done, h + 1)
                    link(dve.tensor_tensor(tiny[:, 3, :], tiny[:, 0, :], tiny[:, 2, :], ALU.mult))
                    link(dve.tensor_tensor(tiny[:, 3, :], tiny[:, 3, :], tiny[:, 2, :], ALU.mult))
                    dve.tensor_scalar(tiny[:, 4, :], tiny[:, 3, :], 1.0 / P, EPS, ALU.mult, ALU.add)\
                        .then_inc(var_done, 1)
                    dve.wait_ge(rpow_done, h + 1)
                    link(dve.tensor_tensor(tiny[:, 6, :], tiny[:, 5, :], tiny[:, 2, :], ALU.mult))
                    dve.tensor_tensor(o_all[:, :, 0:P], o_all[:, :, 0:P],
                                      tiny[:, 6, :].unsqueeze(2).to_broadcast([P, NS, P]), ALU.mult)\
                        .then_inc(yb_done, 1)
                    for half in range(2):
                        dve.wait_ge(ybt_ready, h * 2 + (half + 1))
                        cols = slice(half * BANK, (half + 1) * BANK)
                        dve.tensor_tensor(yT_ml[:, bass.ds(h, 1), cols].rearrange("p a s -> p (a s)"),
                                          core.bank[:, (7, 4)[half], :], sg[:, cols], ALU.mult)\
                            .then_inc(ybt_kept, 1)

                repeat(dve, MH, ml_body)
                link.leave(MH)
                for k in range(KD):
                    src = yT_fox[:, k, :] if k < PAIRS else yT_ml[:, k - PAIRS, :]
                    dve.wait_ge(y_hi, k + 1)
                    dve.tensor_tensor(core.h_lo[:, k, :], src, core.h_hi[:, k, :].bitcast(F32), ALU.subtract)\
                        .then_inc(y_lo, 1)
                for n in range(2 * NS):
                    t, dh = n % NS, n // NS
                    part = core.xres[:, t, dh * BANK:(dh + 1) * BANK]
                    dve.wait_ge(out_ready, n + 1)
                    dve.tensor_tensor(part, core.bank[:, t, :], part, ALU.add).then_inc(out_added, 1)
                for t in range(NS + 2):
                    if t < NS:
                        norm.scale(dve, t)
                    if t >= 2:
                        norm.keep_lo(dve, t - 2)

            @block.tensor
            def _(pe):
                pe.wait_ge(small_loaded, 16 * 8)
                pe.transpose(core.bank[:, 1, 0:NCONST], const_rows[:, :], core.ident[0:NCONST, 0:NCONST])\
                    .then_inc(const_turned, 1)
                pe.wait_ge(gw_cut, 1)
                for t in range(NS):
                    tok = slice(t * P, (t + 1) * P)
                    for k in range(KD):
                        mm = three(pe, core.bank[:, 0, t * NG:(t + 1) * NG], core.h_hi[:, k, tok],
                                   core.h_lo[:, k, tok], gw_hi[:, k, :], gw_lo[:, k, :], k == 0, k == KD - 1)
                mm.then_inc(z_ready, 1)

                def v_waits(k, t):
                    if k == 0 and t < 2:
                        pe.wait_ge((z_done, const_kept)[t], 1)

                by_token(pe, C_V, v_ready, v_waits)
                pe.wait_ge(logf_done, 1)
                pe.wait_ge(pool_set, 1)
                pe.wait_ge(v_kept_even, NS // 2)
                pe.wait_ge(v_kept_odd, NS // 2)
                flat = lambda t: t[:, :, :].rearrange("p k n -> p (k n)")
                pe.matmul(core.bank[:, 4, 0:NS * NG], upper[:, :], flat(logf), start=True, stop=True)
                pe.matmul(core.bank[:, 5, 0:NS * NG], ones[:, :], flat(logf), start=True, stop=True)\
                    .then_inc(sums_ready, 1)

                def project_qk(p, g):
                    if g % 2 == 0:
                        pe.wait_ge(w_lo_done[g // 2], p + (C_F[g // 2] + 1))
                    by_feature(pe, core.bank[:, g, :], g // 2, g % 2).then_inc(fq_ready, 1)

                project_qk(0, 0)
                project_qk(0, 1)
                pe.wait_ge(rows_ready, 1)
                pe.transpose(core.bank[0:NR * NS, 6, 0:P], rows_in[:, :, :].rearrange("p r t -> p (r t)"),
                             core.ident[:, :]).then_inc(rows_turned, 1)
                project_qk(0, 2)
                project_qk(0, 3)

                def scores(p, n, first):
                    e, i = n // NS, n % NS
                    heads = slice(e * HD, (e + 1) * HD)
                    w = (i + 1) * P
                    if n == 0:
                        pe.wait_ge(fq_kept, p * 4 + 4)
                        if first:
                            pe.wait_ge(rows_kept, 1)
                    if not (first and n < 2):
                        pe.wait_ge(logit_done, p * PER + (n - 1))
                    for b in range((w + BANK - 1) // BANK):
                        k0, k1 = b * BANK, min((b + 1) * BANK, w)
                        pe.matmul(core.bank[:, 2 * (n % 2) + b, 0:k1 - k0], fqT[heads, i * P:(i + 1) * P],
                                  fkT[heads, k0:k1], start=True, stop=(k1 < w))
                    mm = pe.matmul(core.bank[:, 2 * (n % 2) + b, k1 - k0 - P:k1 - k0], ident_b[:, :], mask_f[:, :],
                                   start=False, stop=True)
                    mm.then_inc(score_ready, 1)

                def turn_prob(p, n, first):
                    i = n % NS
                    pe.wait_ge(prob_done, p * PER + (n + 1))
                    if n >= 1:
                        pe.wait_ge(pt_act, p * PER + n)
                        hi = 4 * ((n - 1) // NS) + max(0, (n - 1) % NS - 3)
                        if hi:
                            pe.wait_ge(pt_dve, p * NS + hi)
                    elif not first:
                        pe.wait_ge(yt_kept, p * 2)
                    for j in range(i + 1):
                        mm = pe.transpose(core.bank[:, 4 + j // 4, (j % 4) * P:(j % 4 + 1) * P],
                                          prob[:, n % RP, j * P:(j + 1) * P], core.ident[:, :])
                    mm.then_inc(pt_ready, 1)

                def values(p, n, first):
                    e, i = n // NS, n % NS
                    pe.wait_ge(pt_act, p * PER + (n + 1))
                    hi = 4 * e + max(0, i - 3)
                    if hi:
                        pe.wait_ge(pt_dve, p * NS + hi)
                    if not (first and n < 2):
                        pe.wait_ge(y_done, p * PER + (n - 1))
                    for j in range(i + 1):
                        mm = pe.matmul(core.bank[:, 6 + n % 2, 0:HD], probT[:, n % 2, j * P:(j + 1) * P],
                                       v_fox[:, j, bass.ds(p * (2 * HD) + e * HD, HD)], start=(j == 0), stop=(j == i))
                    mm.then_inc(pv_ready, 1)

                def fox_body(p, first, last):
                    for m in range(PER + 3):
                        if m < PER:
                            scores(p, m, first)
                        if 2 <= m < PER + 2:
                            turn_prob(p, m - 2, first)
                        if m >= 3:
                            values(p, m - 3, first)
                        if m in (PER, PER + 1) and not last:
                            pe.wait_ge(logit_done, p * PER + (m - 1))
                            project_qk(p + 1, 2 * (m - PER))
                            project_qk(p + 1, 2 * (m - PER) + 1)
                    pe.wait_ge(y_done, p * PER + PER)
                    pe.wait_ge(pt_act, p * PER + PER)
                    for t in range(NS):
                        mm = pe.transpose(core.bank[:, 4 + t // 4, (t % 4) * P:(t % 4 + 1) * P], y_tok[:, t, :],
                                          core.ident[:, :])
                        if t % 4 == 3:
                            mm.then_inc(yt_ready, 1)

                repeat(pe, PAIRS, fox_body)

                def mv_waits(k, t):
                    if k == 0 and t in (0, 4):
                        if t == 0:
                            pe.wait_ge(logit_done, PAIRS * PER)
                        else:
                            pe.wait_ge(yt_kept, 2 * PAIRS)

                by_token(pe, C_MV, v_ready, mv_waits)

                def project(h, g):
                    slot = g // 2 % 2
                    if g % 2 == 0:
                        pe.wait_ge(w_lo_done[slot], h + (C_M[1] + 1) if slot else h * 2 + (C_M[0] + g // 4 + 1))
                    if g < 4:
                        if not (isinstance(h, int) and h == 0):
                            pe.wait_ge(x_kept, h * X_PER)
                    else:
                        pe.wait_ge(x_kept, h * X_PER + (g - 3))
                    by_feature(pe, core.bank[:, g % 4, :], slot, g % 2).then_inc(x_ready, 1)

                pe.wait_ge(v_kept_even, NS)
                pe.wait_ge(v_kept_odd, NS)
                for g in range(X_PER):
                    project(0, g)

                def ml_body(h, first, last):
                    c_of = lambda j: slice(j * P, (j + 1) * P)
                    if not last:
                        for g in range(4):
                            project(h + 1, g)
                    pe.wait_ge(silu_done, h * 2 + 2)
                    if not first:
                        pe.wait_ge(ybt_kept, h * 2)
                    for j in range(NS):
                        mm = pe.transpose(core.bank[:, 4 + j // 4, c_of(j % 4)], mkT[:, c_of(j)], core.ident[:, :])
                        if j % 4 == 3:
                            mm.then_inc(kt_ready, 1)
                    for j in range(NS):
                        mm = pe.matmul(core.bank[:, 6 + j // 4, c_of(j % 4)], mqT[:, c_of(j)], mkT[:, c_of(j)],
                                       start=True, stop=True)
                        if j % 4 == 3:
                            mm.then_inc(qk_ready, 1)
                    if not last:
                        project(h + 1, 4)
                    for j in range(NS - 1):
                        if j in (0, 3):
                            pe.wait_ge(kw_done, h * 2 + 2)
                        if j == 6:
                            pe.wait_ge(sp_done, h * 2 + 1)
                        mm = pe.matmul(core.bank[:, 4 + j // 3, (j % 3) * V1:(j % 3 + 1) * V1], kw_c[:, c_of(j)],
                                       v_ml[:, j, bass.ds(h, 1), :].rearrange("p a v -> p (a v)"),
                                       start=True, stop=True)
                        if j in (2, 5, 6):
                            mm.then_inc(u_ready, 1)
                    pe.wait_ge(sp_done, h * 2 + 2)
                    pe.wait_ge(state_done, h * NS + 4)
                    for j in range(NS):
                        mm = pe.transpose(core.bank[:, (7, 4)[j // 4], c_of(j % 4)], dec[:, c_of(j)],
                                          core.ident[:, :])
                        if j % 4 == 3:
                            mm.then_inc(spt_ready, 1)
                    if not last:
                        project(h + 1, 5)
                    pe.wait_ge(state_done, h * NS + NS)
                    for r in range(3):
                        num_b, int_b = ((5, 6), (7, 4), (5, 6))[r]
                        if r == 0:
                            pe.wait_ge(spt_kept, h * 2 + 2)
                        if r == 2:
                            pe.wait_ge(o_done, h * 3 + 1)
                        for j in range(3 * r, min(3 * r + 3, NS)):
                            cols = slice((j % 3) * V1, (j % 3 + 1) * V1)
                            pe.matmul(core.bank[:, num_b, cols], dec[:, c_of(j)],
                                      v_ml[:, j, bass.ds(h, 1), :].rearrange("p a v -> p (a v)"),
                                      start=True, stop=True)
                            mm = pe.matmul(core.bank[:, int_b, cols], mqT[:, c_of(j)], states[:, j, :],
                                           start=True, stop=True)
                        mm.then_inc(num_ready, 1)
                    pe.wait_ge(yb_done, h + 1)
                    for j in range(NS):
                        mm = pe.transpose(core.bank[:, (7, 4)[j // 4], c_of(j % 4)], o_all[:, j, 0:P],
                                          core.ident[:, :])
                        if j % 4 == 3:
                            mm.then_inc(ybt_ready, 1)

                repeat(pe, MH, ml_body)

                def out_waits(k, t, dh):
                    if t == 0 and dh == 0:
                        pe.wait_ge(y_lo, k + 1)
                        if k == 0:
                            pe.wait_ge(ybt_kept, 2 * MH)
                    if k == 0 and dh == 1:
                        pe.wait_ge(out_added, t + 1)

                for dh in range(2):
                    by_token(pe, (C_O[0] + 2 * dh, C_O[1] + 2 * dh), out_ready, lambda k, t: out_waits(k, t, dh))
                pe.wait_ge(out_added, 2 * NS)
                for t in range(NS):
                    norm.turn(pe, t)


def program(nc, x, c, w_ada, b_ada, w_ffn1_in, w_ffn1_out, w_mix_in, b_fox_f, b_m_i, b_m_f,
            w_conv, b_conv, g_mhn, w_mix_out, w_ffn2_in, w_ffn2_out, g_final, out):
    with ExitStack() as ctx:
        core = Core(nc, ctx, x, w_ffn1_in, w_mix_in, w_conv, b_fox_f, b_m_f)
        modulation(core, x, c, w_ada, b_ada)
        core.end_part()
        ffn(core, "f1", w_ffn1_in, w_ffn1_out, 2, next_mod=3)
        core.end_part()
        mixer(core, w_mix_in, b_fox_f, b_m_i, b_m_f, w_conv, b_conv, g_mhn, w_mix_out, 5, 6)
        core.end_part()
        ffn(core, "f2", w_ffn2_in, w_ffn2_out, 8, g_final=g_final, out=out)


_INS = ['x', 'c', 'w_ada', 'b_ada', 'w_ffn1_in', 'w_ffn1_out', 'w_mix_in', 'b_fox_f', 'b_m_i', 'b_m_f',
        'w_conv', 'b_conv', 'g_mhn', 'w_mix_out', 'w_ffn2_in', 'w_ffn2_out', 'g_final']


def kernel(**inputs):
    import numpy as np
    import concourse.bacc as bacc
    from concourse.bass_utils import run_bass_kernel_spmd

    nc = bacc.Bacc("TRN2", target_bir_lowering=False, num_devices=1)
    arrays, args = {}, []
    for name in _INS:
        a = np.ascontiguousarray(inputs[name])
        arrays[f"in_{name}"] = a
        args.append(nc.dram_tensor(f"in_{name}", a.shape, mybir.dt.from_np(a.dtype), kind="ExternalInput").ap())
    shape = inputs['x'].shape
    args.append(nc.dram_tensor("out_y", shape, F32, kind="ExternalOutput").ap())
    program(nc, *args)
    r = run_bass_kernel_spmd(nc, [arrays], core_ids=[0])
    return r.results[0]["out_y"]
```

```python
from contextlib import ExitStack

import concourse.bass as bass
from concourse import mybir

F32 = mybir.dt.float32
F32R = mybir.dt.float32r
BF16 = mybir.dt.bfloat16
ALU = mybir.AluOpType
ACT = mybir.ActivationFunctionType
AX = mybir.AxisListType

P = 128
BANK = 512
EPS = 1e-6
NEG = -1e30


class Core:

    def __init__(self, nc, ctx, x):
        self.nc, self.ctx, self.sems = nc, ctx, []
        self.S, self.D = x.shape[1], x.shape[2]
        self.KD = self.D // P
        self.NS = self.S // P
        self.NH = self.S // BANK
        self.xres = self.sb("xres", [P, self.NS, self.D])
        self.h_hi = self.sb("h_hi", [P, self.KD, self.S], F32R)
        with ExitStack() as early:
            self.x_turned = self.sb("x_turned", [P, self.KD, self.S], ctx=early)
        self.h_lo = self.sb("h_lo", [P, self.KD, self.S], F32R)
        self.ident = self.sb("ident", [P, P])
        self.rms = self.sb("rms", [P, 3, self.NS])
        self.neg_half = self.sb("neg_half", [P, self.NS])
        self.bank = ctx.enter_context(nc.psum_tensor("bank", [P, 8, BANK], F32))
        self.mod_rows = nc.dram_tensor("mod_rows", (9 * self.D,), F32, kind="Internal").ap()

    def sb(self, name, shape, dt=F32, ctx=None):
        return (ctx or self.ctx).enter_context(self.nc.sbuf_tensor(name, shape, dt))

    def sem(self, name):
        self.sems.append(self.nc.alloc_semaphore(name=name))
        return self.sems[-1]

    def end_part(self):
        self.nc.clear_and_free_semaphores(self.sems)
        self.nc.all_engine_barrier()
        self.sems = []

    def mod(self, m):
        return self.mod_rows[m * self.D:(m + 1) * self.D].partition_broadcast(P)


class Norm:

    def __init__(self, core, tag, shift, scale1, junk, xn, first_bank):
        self.c, self.shift, self.scale1, self.junk, self.xn = core, shift, scale1, junk, xn
        self.first_bank = first_bank
        s = core.sem
        self.loaded = s(f"{tag}_mod_loaded")
        self.squared = s(f"{tag}_squared")
        self.mean_done = s(f"{tag}_mean_done")
        self.rms_done = s(f"{tag}_rms_done")
        self.scaled = s(f"{tag}_scaled")
        self.shifted = s(f"{tag}_shifted")
        self.turned = s(f"{tag}_turned")
        self.hi_done = s(f"{tag}_hi_done")
        self.lo_done = s(f"{tag}_lo_done")

    def load(self, sp, m):
        sp.dma_start(self.shift, self.c.mod(m)).then_inc(self.loaded, 16)
        sp.dma_start(self.scale1, self.c.mod(m + 1)).then_inc(self.loaded, 16)

    def bank_of(self, t):
        return self.first_bank + 2 * (t % 2)

    def square(self, act, t):
        if t:
            act.wait_ge(self.squared, t)
        act.activation(self.junk, self.c.xres[:, t, :], ACT.Square,
                       accum_out=self.c.rms[:, 0, t:t + 1]).then_inc(self.squared, 1)

    def inverse(self, pool, t):
        c = self.c
        pool.wait_ge(self.squared, t + 1)
        pool.tensor_scalar(c.rms[:, 1, t:t + 1], c.rms[:, 0, t:t + 1], 1.0 / c.D, EPS,
                           ALU.mult, ALU.add).then_inc(self.mean_done, 1)
        pool.wait_ge(self.mean_done, t + 1)
        pool.tensor_tensor(c.rms[:, 2, t:t + 1], c.rms[:, 1, t:t + 1], c.neg_half[:, t:t + 1],
                           ALU.pow).then_inc(self.rms_done, 1)

    def scale(self, dve, t):
        c, n = self.c, len(self.xn)
        if t == 0:
            dve.wait_ge(self.loaded, 32)
        dve.wait_ge(self.rms_done, t + 1)
        if t >= n:
            dve.wait_ge(self.turned, 2 * (t - n) + 2)
        dve.scalar_tensor_tensor(self.xn[t % n], c.xres[:, t, :], c.rms[:, 2, t:t + 1], self.scale1,
                                 ALU.mult, ALU.mult).then_inc(self.scaled, 1)

    def add_shift(self, pool, t):
        n = len(self.xn)
        if t == 0:
            pool.wait_ge(self.loaded, 32)
        pool.wait_ge(self.scaled, t + 1)
        pool.tensor_tensor(self.xn[t % n], self.xn[t % n], self.shift, ALU.add).then_inc(self.shifted, 1)

    def turn(self, pe, t):
        c, n = self.c, len(self.xn)
        pe.wait_ge(self.shifted, t + 1)
        if t >= 2:
            pe.wait_ge(self.lo_done, 2 * (t - 2) + 2)
        for half in range(2):
            for k in range(4):
                mm = pe.transpose(c.bank[:, self.bank_of(t) + half, k * P:(k + 1) * P],
                                  self.xn[t % n][:, (4 * half + k) * P:(4 * half + k + 1) * P], c.ident[:, :])
            mm.then_inc(self.turned, 1)

    def _h(self, which, t, half):
        return which[:, 4 * half:4 * half + 4, t * P:(t + 1) * P]

    def _turned(self, t, half):
        return self.c.bank[:, self.bank_of(t) + half, :].rearrange("p (k s) -> p k s", k=4)

    def keep_hi(self, act, t):
        for half in range(2):
            act.wait_ge(self.turned, 2 * t + half + 1)
            act.copy(self._h(self.c.h_hi, t, half), self._turned(t, half)).then_inc(self.hi_done, 1)

    def keep_lo(self, dve, t):
        for half in range(2):
            dve.wait_ge(self.hi_done, 2 * t + half + 1)
            dve.tensor_tensor(self._h(self.c.h_lo, t, half), self._turned(t, half),
                              self._h(self.c.h_hi, t, half).bitcast(F32),
                              ALU.subtract).then_inc(self.lo_done, 1)


class Start:
    RING = 4

    def __init__(self, core, x, c_vec, w_ada, b_ada, steps, acc, ring, xn, junk, gate, sb):
        self.c, self.x, self.c_vec, self.w_ada, self.b_ada = core, x, c_vec, w_ada, b_ada
        self.acc, self.ring, self.xn, self.junk, self.gate = acc, ring, xn, junk, gate
        KD, D = core.KD, core.D
        self.M = w_ada.shape[2] // D
        self.COLS = (self.M - 3) * D // steps
        self.TILES = self.COLS // P
        self.c_act = sb("c_act", [P, KD])
        self.brow = sb("b_ada_rows", [(self.M + 1) * KD, P])
        self.bcol = sb("b_ada_cols", [P, self.M * KD])
        self.mcol = sb("mod_cols", [P, self.M * KD])
        self.mrow = sb("mod_row_tiles", [(self.M - 3) * KD, P])
        self.ones = sb("ada_ones", [P, 1])
        self.halves = sb("ada_halves", [P, P])
        s = core.sem
        self.small_loaded, self.bias_loaded = s("small_loaded"), s("gate_bias_loaded")
        self.x_loaded = [s(f"x_loaded{t}") for t in range(core.NS)]
        self.ring_loaded = [s(f"ada_loaded{i}") for i in range(self.RING)]
        self.ident_zero, self.consts = s("ident_zero"), s("consts")
        self.b_turned, self.b_kept, self.c_act_done = s("b_turned"), s("b_kept"), s("c_act_done")
        self.squared, self.mean_done, self.rms_done = s("squared"), s("mean_done"), s("rms_done")
        self.xn_done, self.turned = s("xn_done"), s("turned")
        self.kept_low, self.kept_high = s("turned_kept_low"), s("turned_kept_high")
        self.lead_summed, self.lead_cols, self.lead_done = s("lead_summed"), s("lead_cols"), s("lead_done")
        self.h_made, self.h_hi_done, self.h_lo_done = s("h_made"), s("h_hi_done"), s("h_lo_done")
        self.gate_summed, self.gate_spread, self.gate_made = s("gate_summed"), s("gate_spread"), s("gate_made")
        self.rest_loaded, self.rest_summed = s("rest_loaded"), s("rest_summed")
        self.rest_cols, self.rest_kept = s("rest_cols"), s("rest_kept")
        self.rest_final, self.rows_turned = s("rest_final"), s("rows_turned")
        self.rows_kept, self.rows_stored = s("rows_kept"), s("rows_stored")

    def load(self, sp, first_weights):
        KD, D = self.c.KD, self.c.D
        sp.dma_start(self.brow[self.M * KD:, :], self.c_vec.rearrange("a (k p) -> (a k) p", p=P))\
            .then_inc(self.small_loaded, 16)
        sp.dma_start(self.brow[0:self.M * KD, :], self.b_ada.rearrange("a (r n) -> (a r) n", n=P))\
            .then_inc(self.small_loaded, 16)
        for k in range(KD):
            if k >= self.RING:
                sp.wait_ge(self.lead_summed, k - self.RING + 1)
            sp.dma_start(self.ring[k % self.RING], self.w_ada[0, k * P:(k + 1) * P, 0:2 * D])\
                .then_inc(self.ring_loaded[k % self.RING], 16)
            if k < self.RING:
                for t in (2 * k, 2 * k + 1):
                    sp.dma_start(self.c.xres[:, t, :], self.x[0, t * P:(t + 1) * P, :])\
                        .then_inc(self.x_loaded[t], 16)
            if k == KD - 3:
                first_weights()
        sp.dma_start(self.gate, self.b_ada[0, 2 * D:3 * D].partition_broadcast(P)).then_inc(self.bias_loaded, 16)
        for r in range(self.RING):
            sp.wait_ge(self.lead_summed, KD - self.RING + r + 1)
            sp.dma_start(self.ring[r].rearrange("p (k d) -> p k d", k=2),
                         self.w_ada[0, 2 * r * P:(2 * r + 2) * P, 2 * D:3 * D].rearrange("(k p) d -> p k d", p=P))\
                .then_inc(self.ring_loaded[r], 16)

    def load_rest(self, sp, b):
        KD, D = self.c.KD, self.c.D
        for k in range(KD):
            sp.wait_ge(self.rest_summed, (b - 1) * KD + k)
            sp.dma_start(self.acc[:, self.COLS:2 * self.COLS],
                         self.w_ada[0, k * P:(k + 1) * P, bass.ds((b - 1) * self.COLS + 3 * D, self.COLS)])\
                .then_inc(self.rest_loaded, 16)

    def store_rows(self, sp):
        sp.wait_ge(self.rows_kept, 1)
        sp.dma_start(self.c.mod_rows[3 * self.c.D:].rearrange("(r n) -> r n", n=P), self.mrow[:, :])\
            .then_inc(self.rows_stored, 16)
        sp.wait_ge(self.rows_stored, 16)

    def pool_part(self, pool):
        c = self.c
        pool.memset(c.ident[:, :], 0.0).then_inc(self.ident_zero, 1)
        pool.wait_ge(self.ident_zero, 1)
        pool.affine_select(out=c.ident[:, :], in_=c.ident[:, :], compare_op=ALU.not_equal,
                           fill=1.0, base=0, pattern=[[-1, P]], channel_multiplier=1).then_inc(self.consts, 1)
        pool.memset(self.ones[:, :], 1.0).then_inc(self.consts, 1)
        pool.memset(self.halves[:, :], 0.5).then_inc(self.consts, 1)
        pool.memset(c.neg_half[:, :], -0.5).then_inc(self.consts, 1)
        pool.wait_ge(self.consts, 4)
        for t in range(c.NS):
            pool.wait_ge(self.squared, t + 1)
            pool.tensor_scalar(c.rms[:, 1, t:t + 1], c.rms[:, 0, t:t + 1], 1.0 / c.D, EPS,
                               ALU.mult, ALU.add).then_inc(self.mean_done, 1)
            pool.wait_ge(self.mean_done, t + 1)
            pool.tensor_tensor(c.rms[:, 2, t:t + 1], c.rms[:, 1, t:t + 1], c.neg_half[:, t:t + 1],
                               ALU.pow).then_inc(self.rms_done, 1)

    def _turned_dst(self, t, half):
        return self.c.x_turned[:, 4 * half:4 * half + 4, t * P:(t + 1) * P]

    def _turned_src(self, t, half):
        return self.c.bank[:, 4 + 2 * (t % 2) + half, :].rearrange("p (k s) -> p k s", k=4)

    def act_part(self, act):
        c, KD = self.c, self.c.KD
        act.wait_ge(self.b_turned, 1)
        act.activation(self.c_act[:, :], c.bank[:, 0, self.M * KD:(self.M + 1) * KD], ACT.Silu)\
            .then_inc(self.c_act_done, 1)
        for t in range(c.NS + 2):
            if t < c.NS:
                act.wait_ge(self.x_loaded[t], 16)
                if t:
                    act.wait_ge(self.squared, t)
                act.activation(self.junk, c.xres[:, t, :], ACT.Square,
                               accum_out=c.rms[:, 0, t:t + 1]).then_inc(self.squared, 1)
            if 1 <= t <= c.NS:
                act.wait_ge(self.rms_done, t)
                if t >= 3:
                    act.wait_ge(self.turned, 2 * (t - 3) + 2)
                act.activation(self.xn[(t - 1) % 2], c.xres[:, t - 1, :], ACT.Copy,
                               scale=c.rms[:, 2, t - 1:t]).then_inc(self.xn_done, 1)
            if t >= 2:
                act.wait_ge(self.turned, 2 * (t - 2) + 2)
                act.copy(self._turned_dst(t - 2, 1), self._turned_src(t - 2, 1)).then_inc(self.kept_high, 1)

    def pe_part(self, pe):
        c, KD = self.c, self.c.KD
        pe.wait_ge(self.consts, 4)
        pe.wait_ge(self.small_loaded, 32)
        pe.transpose(c.bank[:, 0, 0:(self.M + 1) * KD], self.brow[:, :],
                     c.ident[0:(self.M + 1) * KD, 0:(self.M + 1) * KD]).then_inc(self.b_turned, 1)
        for t in range(c.NS):
            pe.wait_ge(self.xn_done, t + 1)
            if t >= 2:
                pe.wait_ge(self.kept_low, t - 1)
                pe.wait_ge(self.kept_high, t - 1)
            for half in range(2):
                for k in range(4):
                    mm = pe.transpose(c.bank[:, 4 + 2 * (t % 2) + half, k * P:(k + 1) * P],
                                      self.xn[t % 2][:, (4 * half + k) * P:(4 * half + k + 1) * P], c.ident[:, :])
                mm.then_inc(self.turned, 1)
        pe.wait_ge(self.lead_summed, KD)
        for r in range(2 * KD):
            mm = pe.matmul(c.bank[:, 1, r:r + 1], self.acc[:, r * P:(r + 1) * P], self.ones[:, :],
                           start=True, stop=True)
        mm.then_inc(self.lead_cols, 1)

    def dve_lead(self, dve):
        c, KD, D = self.c, self.c.KD, self.c.D
        dve.wait_ge(self.c_act_done, 1)
        dve.wait_ge(self.b_turned, 1)
        dve.tensor_copy(self.bcol[:, :], c.bank[:, 0, 0:self.M * KD]).then_inc(self.b_kept, 1)
        tiles_after = {1: (0,), 2: (1,), 3: (2, 3), 4: (4, 5), 5: (6,), 6: (7,)}
        for k in range(KD):
            dve.wait_ge(self.ring_loaded[k % self.RING], 16 * (k // self.RING + 1))
            piece, c_k = self.ring[k % self.RING], self.c_act[:, k:k + 1]
            if k == 0:
                dve.tensor_scalar(self.acc, piece, c_k, None, ALU.mult).then_inc(self.lead_summed, 1)
            else:
                dve.wait_ge(self.lead_summed, k)
                dve.scalar_tensor_tensor(self.acc, piece, c_k, self.acc, ALU.mult, ALU.add)\
                    .then_inc(self.lead_summed, 1)
            for t in tiles_after.get(k, ()):
                dve.wait_ge(self.turned, 2 * t + 1)
                dve.tensor_copy(self._turned_dst(t, 0), self._turned_src(t, 0)).then_inc(self.kept_low, 1)
        dve.wait_ge(self.lead_cols, 1)
        dve.wait_ge(self.b_kept, 1)
        dve.tensor_tensor(self.mcol[:, 0:KD], c.bank[:, 1, 0:KD], self.bcol[:, 0:KD], ALU.add)\
            .then_inc(self.lead_done, 1)
        dve.scalar_tensor_tensor(self.mcol[:, KD:2 * KD], c.bank[:, 1, KD:2 * KD], 1.0, self.bcol[:, KD:2 * KD],
                                 ALU.add, ALU.add).then_inc(self.lead_done, 1)

    def _piece(self, which, n):
        half, k = n // self.c.KD, n % self.c.KD
        return which[:, k, half * BANK:(half + 1) * BANK]

    def dve_h(self, dve):
        c, KD = self.c, self.c.KD
        dve.wait_ge(self.lead_done, 2)
        dve.wait_ge(self.kept_high, c.NS)
        dve.wait_ge(self.kept_low, c.NS)
        for n in range(c.NH * KD + 1):
            if n < c.NH * KD:
                x_n, k = self._piece(c.x_turned, n), n % KD
                dve.tensor_scalar(x_n, x_n, self.mcol[:, KD + k:KD + k + 1], self.mcol[:, k:k + 1],
                                  ALU.mult, ALU.add).then_inc(self.h_made, 1)
            if n:
                dve.wait_ge(self.h_hi_done, n)
                dve.wait_ge(self.h_made, n)
                dve.tensor_tensor(self._piece(c.h_lo, n - 1), self._piece(c.x_turned, n - 1),
                                  self._piece(c.h_hi, n - 1).bitcast(F32), ALU.subtract).then_inc(self.h_lo_done, 1)

    def act_h(self, act):
        c = self.c
        for n in range(c.NH * c.KD):
            act.wait_ge(self.h_made, n + 1)
            act.copy(self._piece(c.h_hi, n), self._piece(c.x_turned, n)).then_inc(self.h_hi_done, 1)

    def dve_gate(self, dve):
        KD, D = self.c.KD, self.c.D
        acc = self.acc[:, 0:D]
        for k in range(KD):
            dve.wait_ge(self.ring_loaded[k // 2], 48)
            piece, c_k = self.ring[k // 2][:, (k % 2) * D:(k % 2 + 1) * D], self.c_act[:, k:k + 1]
            if k == 0:
                dve.wait_ge(self.lead_cols, 1)
                dve.tensor_scalar(acc, piece, c_k, None, ALU.mult).then_inc(self.gate_summed, 1)
            else:
                dve.wait_ge(self.gate_summed, k)
                dve.scalar_tensor_tensor(acc, piece, c_k, acc, ALU.mult, ALU.add).then_inc(self.gate_summed, 1)

    def pe_gate(self, pe):
        pe.wait_ge(self.gate_summed, self.c.KD)
        for i in range(2):
            pe.matmul(self.c.bank[:, 4 + i, :], self.halves[:, :], self.acc[:, i * BANK:(i + 1) * BANK],
                      start=True, stop=True).then_inc(self.gate_spread, 1)

    def dve_gate_done(self, dve):
        dve.wait_ge(self.bias_loaded, 16)
        for i in range(2):
            half = self.gate[:, i * BANK:(i + 1) * BANK]
            dve.wait_ge(self.gate_spread, i + 1)
            dve.scalar_tensor_tensor(half, half, 0.5, self.c.bank[:, 4 + i, :], ALU.mult, ALU.add)\
                .then_inc(self.gate_made, 1)

    def dve_rest(self, dve, b, k):
        dve.wait_ge(self.rest_loaded, (b - 1) * (16 * self.c.KD) + 16 * (k + 1))
        acc, piece = self.acc[:, 0:self.COLS], self.acc[:, self.COLS:2 * self.COLS]
        c_k = self.c_act[:, k:k + 1]
        if k == 0:
            dve.wait_ge(self.rest_cols, b - 1)
            dve.tensor_scalar(acc, piece, c_k, None, ALU.mult).then_inc(self.rest_summed, 1)
        else:
            dve.wait_ge(self.rest_summed, (b - 1) * self.c.KD + k)
            dve.scalar_tensor_tensor(acc, piece, c_k, acc, ALU.mult, ALU.add).then_inc(self.rest_summed, 1)

    def pe_rest(self, pe, b):
        pe.wait_ge(self.rest_summed, b * self.c.KD)
        for r in range(self.TILES):
            mm = pe.matmul(self.c.bank[:, 4, r:r + 1], self.acc[:, r * P:(r + 1) * P], self.ones[:, :],
                           start=True, stop=True)
        mm.then_inc(self.rest_cols, 1)

    def dve_rest_kept(self, dve, b):
        at = bass.ds((b - 1) * self.TILES + 3 * self.c.KD, self.TILES)
        dve.wait_ge(self.rest_cols, b)
        dve.tensor_tensor(self.mcol[:, at], self.c.bank[:, 4, 0:self.TILES], self.bcol[:, at], ALU.add)\
            .then_inc(self.rest_kept, 1)

    def dve_finish(self, dve, steps):
        KD = self.c.KD
        dve.wait_ge(self.rest_kept, steps)
        for m in (4, 7):
            v = self.mcol[:, m * KD:(m + 1) * KD]
            dve.tensor_scalar(v, v, 1.0, None, ALU.add).then_inc(self.rest_final, 1)
        v = self.mcol[:, 8 * KD:9 * KD]
        dve.tensor_scalar(v, v, 0.5, None, ALU.mult).then_inc(self.rest_final, 1)

    def pe_finish(self, pe):
        pe.wait_ge(self.rest_final, 3)
        pe.transpose(self.c.bank[0:(self.M - 3) * self.c.KD, 4, 0:P], self.mcol[:, 3 * self.c.KD:], self.c.ident[:, :])\
            .then_inc(self.rows_turned, 1)

    def dve_rows(self, dve):
        dve.wait_ge(self.rows_turned, 1)
        dve.tensor_copy(self.mrow[:, :], self.c.bank[0:(self.M - 3) * self.c.KD, 4, 0:P]).then_inc(self.rows_kept, 1)


def ffn(core, tag, w_in, w_out, gate_row=None, next_mod=None, g_final=None, out=None, start_in=None):
    nc, KD, D, F, NS = core.nc, core.KD, core.D, w_out.shape[1], core.NS
    TPS = 2
    STEPS = F // (TPS * P)
    NG = 2 * NS
    src_in = w_in.rearrange("a (k p) (g n) -> (a p) k g n", p=P, g=2)
    src_out = w_out.rearrange("a f d -> (a f) d")
    with ExitStack() as ctx:
        sb = lambda n, *a: core.sb(f"{tag}_{n}", *a, ctx=ctx)
        raw_in = sb("raw_in", [P, TPS, KD, 2, P])
        in_hi = sb("in_hi", [P, TPS, KD, 2, P], F32R)
        in_lo = sb("in_lo", [P, TPS, KD, 2, P], F32R)
        raw_out = sb("raw_out", [P, TPS, D])
        with ExitStack() as early:
            ring = core.sb(f"{tag}_ada_ring", [P, Start.RING, 2 * D], ctx=early) if start_in else None
        out_hi = sb("out_hi", [P, TPS, D], F32R)
        out_lo = sb("out_lo", [P, TPS, D], F32R)
        act_hi = sb("act_hi", [P, TPS, core.S], F32R)
        act_lo = sb("act_lo", [P, TPS, core.S], F32R)
        silu_g = sb("silu_g", [P, 2, BANK])
        act_f = sb("act_f", [P, 2, BANK])
        gate = sb("gate", [P, D])
        shift_scale = sb("shift_scale", [P, 2 * D])
        shift, scale1 = shift_scale[:, 0:D], shift_scale[:, D:2 * D]
        s = lambda n: core.sem(f"{tag}_{n}")
        in_loaded = [s(f"in_loaded{j}") for j in range(TPS)]
        out_loaded = [s(f"out_loaded{j}") for j in range(TPS)]
        gate_loaded = s("gate_loaded")
        in_hi_done, in_lo_done = s("in_hi_done"), s("in_lo_done")
        out_gated, out_hi_done, out_lo_done = s("out_gated"), s("out_hi_done"), s("out_lo_done")
        g_ready, u_ready = s("g_ready"), s("u_ready")
        silu_done, mult_done = s("silu_done"), s("mult_done")
        act_hi_done, act_lo_done = s("act_hi_done"), s("act_lo_done")
        y_ready, y_added = s("y_ready"), s("y_added")
        xn = [raw_in[:, j].rearrange("p k g n -> p (k g n)")[:, i * D:(i + 1) * D]
              for i in range(2) for j in range(TPS)]
        norm = Norm(core, tag + "n", shift, scale1, raw_out[:, 0, :], xn, 0)
        stored = s("stored")
        flat = lambda t, j: t[:, j].rearrange("p k g n -> p (k g n)")
        LOOP = STEPS - 3
        start = None
        if start_in:
            start = Start(core, *start_in, LOOP, shift_scale[:, :], [ring[:, r, :] for r in range(Start.RING)], [raw_out[:, 0, :], raw_out[:, 1, :]],
                          act_f[:, :, :].rearrange("p j n -> p (j n)"), gate[:, :], sb)

        def steps(eng, body):
            body(0, True, False)
            with eng.Fori(1, LOOP + 1) as b:
                body(b, False, False)
            body(STEPS - 2, False, False)
            body(STEPS - 1, False, True)

        with nc.Block() as block:

            @block.sync
            def _(sp):
                def load_in(b, first):
                    for j in range(TPS):
                        if not first:
                            sp.wait_ge(in_lo_done, b * TPS + (j - TPS + 1))
                        for g in range(2):
                            sp.dma_start(raw_in[:, j, :, g, :], src_in[:, :, g, bass.ts(b * TPS + j, P)])\
                                .then_inc(in_loaded[j], 16)

                def load_out(b, first):
                    for j in range(TPS):
                        if not first:
                            sp.wait_ge(out_lo_done, b * TPS + (j - TPS + 1))
                        sp.dma_start(raw_out[:, j, :], src_out[bass.ts(b * TPS + j, P), :])\
                            .then_inc(out_loaded[j], 16)

                def load(b):
                    load_in(b, False)
                    load_out(b, False)

                if start:
                    start.load(sp, lambda: load_in(0, True))
                    sp.wait_ge(start.turned, 2 * NS)
                else:
                    load_in(0, True)
                    sp.dma_start(gate[:, :], core.mod(gate_row)).then_inc(gate_loaded, 16)
                load_out(0, True)
                load(1)
                if start:
                    sp.wait_ge(start.gate_made, 2)
                with sp.Fori(1, LOOP + 1) as b:
                    load(b + 1)
                    if start:
                        start.load_rest(sp, b)
                load(STEPS - 1)
                if start:
                    start.store_rows(sp)
                if next_mod is not None:
                    norm.load(sp, next_mod)
                else:
                    sp.dma_start(scale1, g_final.partition_broadcast(P)).then_inc(norm.loaded, 16)
                    for t in range(NS):
                        sp.wait_ge(norm.scaled, t + 1)
                        sp.dma_start(out[0, t * P:(t + 1) * P, :], core.xres[:, t, :]).then_inc(stored, 16)
                    sp.wait_ge(stored, 16 * NS)

            @block.gpsimd
            def _(pool):
                def cut_in(b, first):
                    for j in range(TPS):
                        pool.wait_ge(in_hi_done, b * TPS + (j + 1))
                        if not first:
                            pool.wait_ge(u_ready, b * 4 + (j - 1))
                        pool.tensor_tensor(flat(in_lo, j), flat(raw_in, j), flat(in_hi, j).bitcast(F32),
                                           ALU.subtract).then_inc(in_lo_done, 1)

                def cut_out(b, first, last):
                    for j in range(TPS):
                        pool.wait_ge(out_loaded[j], b * 16 + 16)
                        pool.tensor_tensor(raw_out[:, j, :], raw_out[:, j, :], gate[:, :], ALU.mult)\
                            .then_inc(out_gated, 1)
                    for j in range(TPS):
                        pool.wait_ge(out_hi_done, b * TPS + (j + 1))
                        if not first:
                            pool.wait_ge(y_ready, b * NG)
                        pool.tensor_tensor(out_lo[:, j, :], raw_out[:, j, :], out_hi[:, j, :].bitcast(F32),
                                           ALU.subtract).then_inc(out_lo_done, 1)

                def body(b, first, last):
                    cut_out(b, first, last)
                    if not last:
                        cut_in(b + 1, False)

                if start:
                    start.pool_part(pool)
                    cut_in(0, True)
                    pool.wait_ge(start.gate_made, 2)
                else:
                    cut_in(0, True)
                    pool.wait_ge(gate_loaded, 16)
                steps(pool, body)
                for t in range(NS + 1):
                    if t < NS:
                        norm.inverse(pool, t)
                    if t >= 1 and next_mod is not None:
                        norm.add_shift(pool, t - 1)

            @block.scalar
            def _(act):
                def cut_in(b, first):
                    for j in range(TPS):
                        act.wait_ge(in_loaded[j], b * 32 + 32)
                        if not first:
                            act.wait_ge(u_ready, b * 4 + (j - 1))
                        act.copy(flat(in_hi, j), flat(raw_in, j)).then_inc(in_hi_done, 1)

                def silu(b, q):
                    act.wait_ge(g_ready, b * 4 + (q + 1))
                    if not (isinstance(b, int) and b * 4 + q < 2):
                        act.wait_ge(mult_done, b * 4 + (q - 1))
                    act.activation(silu_g[:, q % 2, :], core.bank[:, 2 * (q % 2), :], ACT.Silu)\
                        .then_inc(silu_done, 1)

                def hidden_hi(b, q, first):
                    h, j = q // 2, q % 2
                    act.wait_ge(mult_done, b * 4 + (q + 1))
                    if not first:
                        act.wait_ge(y_ready, b * NG + (h - 1) * (NG // 2))
                    act.copy(act_hi[:, j, h * BANK:(h + 1) * BANK], act_f[:, q % 2, :]).then_inc(act_hi_done, 1)

                def cut_out(b, first):
                    for j in range(TPS):
                        act.wait_ge(out_gated, b * TPS + (j + 1))
                        if not first:
                            act.wait_ge(y_ready, b * NG)
                        act.copy(out_hi[:, j, :], raw_out[:, j, :]).then_inc(out_hi_done, 1)

                def body(b, first, last):
                    if not first:
                        cut_out(b, first)
                    for q in range(5):
                        if q < 4:
                            silu(b, q)
                        if q >= 1:
                            hidden_hi(b, q - 1, first)
                        if first and q == 2:
                            cut_out(b, first)
                    if not last:
                        cut_in(b + 1, False)

                if start:
                    start.act_part(act)
                cut_in(0, True)
                if start:
                    start.act_h(act)
                steps(act, body)
                for t in range(NS + 2):
                    if t < NS:
                        act.wait_ge(y_added, (STEPS - 1) * NG + 2 * t + 2)
                        if t == 0:
                            act.wait_ge(out_lo_done, STEPS * TPS)
                        norm.square(act, t)
                    if t >= 2 and next_mod is not None:
                        norm.keep_hi(act, t - 2)

            @block.vector
            def _(dve):
                def hidden(b, q):
                    h, j = q // 2, q % 2
                    dve.wait_ge(silu_done, b * 4 + (q + 1))
                    dve.wait_ge(u_ready, b * 4 + (q + 1))
                    if not (isinstance(b, int) and b * 4 + q < 2):
                        dve.wait_ge(act_lo_done, b * 4 + (q - 1))
                    dve.tensor_tensor(act_f[:, q % 2, :], core.bank[:, 2 * (q % 2) + 1, :], silu_g[:, q % 2, :],
                                      ALU.mult).then_inc(mult_done, 1)
                    dve.wait_ge(act_hi_done, b * 4 + (q + 1))
                    half = slice(h * BANK, (h + 1) * BANK)
                    dve.tensor_tensor(act_lo[:, j, half], act_f[:, q % 2, :], act_hi[:, j, half].bitcast(F32),
                                      ALU.subtract).then_inc(act_lo_done, 1)

                def add(b, g):
                    part = core.xres[:, g // 2, (g % 2) * BANK:(g % 2 + 1) * BANK]
                    dve.wait_ge(y_ready, b * NG + (g + 1))
                    dve.tensor_tensor(part, core.bank[:, 4 + g % 4, :], part, ALU.add).then_inc(y_added, 1)

                def body(b, first, last):
                    in_loop = start and not isinstance(b, int)
                    if start and first:
                        start.dve_lead(dve)
                        start.dve_h(dve)
                        start.dve_gate(dve)
                    if start and isinstance(b, int) and b == STEPS - 2:
                        start.dve_finish(dve, LOOP)
                    for q in range(4):
                        hidden(b, q)
                        if in_loop:
                            start.dve_rest(dve, b, q)
                        if start and first and q == 0:
                            start.dve_gate_done(dve)
                        if start and isinstance(b, int) and b == STEPS - 2 and q == 2:
                            start.dve_rows(dve)
                    if not last:
                        for g in range(NG):
                            add(b, g)
                            if in_loop and g in (1, 4, 7, 10):
                                start.dve_rest(dve, b, 4 + g // 3)
                        if in_loop:
                            start.dve_rest_kept(dve, b)

                steps(dve, body)
                for t in range(NS + 4):
                    if t < NS:
                        add(STEPS - 1, 2 * t)
                        add(STEPS - 1, 2 * t + 1)
                    if 2 <= t < NS + 2:
                        if next_mod is not None:
                            if t == 2:
                                dve.wait_ge(in_lo_done, STEPS * TPS)
                            norm.scale(dve, t - 2)
                        else:
                            if t == 2:
                                dve.wait_ge(norm.loaded, 16)
                            dve.wait_ge(norm.rms_done, t - 1)
                            dve.scalar_tensor_tensor(core.xres[:, t - 2, :], core.xres[:, t - 2, :],
                                                     core.rms[:, 2, t - 2:t - 1], scale1[:, :],
                                                     ALU.mult, ALU.mult).then_inc(norm.scaled, 1)
                    if 4 <= t and next_mod is not None:
                        norm.keep_lo(dve, t - 4)

            @block.tensor
            def _(pe):
                def quarter(b, q):
                    h, j = q // 2, q % 2
                    half = slice(h * BANK, (h + 1) * BANK)
                    if h == 0:
                        pe.wait_ge(in_lo_done, b * TPS + (j + 1))
                    for g in range(2):
                        if not (isinstance(b, int) and b * 4 + q < 2):
                            pe.wait_ge(silu_done if g == 0 else mult_done, b * 4 + (q - 1))
                        dst = core.bank[:, 2 * (q % 2) + g, :]
                        for k in range(KD):
                            if start and isinstance(b, int) and b == 0 and j == 0 and g == 0:
                                pe.wait_ge(start.h_lo_done, h * KD + k + 1)
                            w_hi, w_lo = in_hi[:, j, k, g, :], in_lo[:, j, k, g, :]
                            pe.matmul(dst, w_hi, core.h_hi[:, k, half], start=(k == 0), stop=False)
                            pe.matmul(dst, w_hi, core.h_lo[:, k, half], start=False, stop=False)
                            mm = pe.matmul(dst, w_lo, core.h_hi[:, k, half], start=False, stop=(k == KD - 1))
                        mm.then_inc(u_ready if g else g_ready, 1)

                def group(b, g):
                    t, dh = g // 2, g % 2
                    tok, cols = slice(t * P, (t + 1) * P), slice(dh * BANK, (dh + 1) * BANK)
                    if g == 0:
                        pe.wait_ge(out_lo_done, b * TPS + TPS)
                    if g in (0, NG // 2):
                        pe.wait_ge(act_lo_done, b * 4 + (2 if g == 0 else 4))
                    if not (isinstance(b, int) and b == 0 and g < 4):
                        pe.wait_ge(y_added, b * NG + (g - 3))
                    if start and g == 0:
                        if isinstance(b, int) and b == 0:
                            pe.wait_ge(start.gate_made, 2)
                        elif isinstance(b, int) and b == STEPS - 2:
                            pe.wait_ge(start.rows_kept, 1)
                        elif not isinstance(b, int):
                            pe.wait_ge(start.rest_kept, b - 1)
                    dst = core.bank[:, 4 + g % 4, :]
                    for j in range(TPS):
                        a_hi, a_lo = act_hi[:, j, tok], act_lo[:, j, tok]
                        pe.matmul(dst, a_hi, out_hi[:, j, cols], start=(j == 0), stop=False)
                        pe.matmul(dst, a_hi, out_lo[:, j, cols], start=False, stop=False)
                        mm = pe.matmul(dst, a_lo, out_hi[:, j, cols], start=False, stop=(j == TPS - 1))
                    mm.then_inc(y_ready, 1)

                def body(b, first, last):
                    for q in range(4):
                        quarter(b, q)
                        if start and first and q == 1:
                            start.pe_gate(pe)
                        if start and isinstance(b, int) and b == STEPS - 2 and q == 2:
                            pe.wait_ge(y_added, b * NG)
                            start.pe_finish(pe)
                    for g in range(NG):
                        group(b, g)
                        if last and next_mod is not None and g % 2 and g >= 9:
                            norm.turn(pe, (g - 9) // 2)
                    if start and not isinstance(b, int):
                        pe.wait_ge(y_added, b * NG + (NG - 3))
                        start.pe_rest(pe, b)

                if start:
                    start.pe_part(pe)
                steps(pe, body)
                if next_mod is not None:
                    for t in range(4, NS):
                        norm.turn(pe, t)


class Chain:

    def __init__(self, eng, sem):
        self.eng, self.sem, self.base, self.done, self.per = eng, sem, 0, 0, 0

    def at(self, i):
        if isinstance(i, int) and i == 0:
            self.start, self.per = self.done, 0
        elif self.per == 0:
            self.per = self.done - self.start
        if not (isinstance(i, int) and i == 0):
            self.base, self.done = i * self.per, self.start

    def leave(self, n):
        self.base, self.done = 0, self.start + n * self.per

    def __call__(self, ins):
        ins.then_inc(self.sem, 1)
        self.done += 1
        self.eng.wait_ge(self.sem, self.base + self.done)


def mixer(core, w_mix_in, b_fox_f, b_m_i, b_m_f, w_conv, b_conv, g_mhn, w_mix_out, gate_row, next_mod):
    nc, KD, D, S, NS = core.nc, core.KD, core.D, core.S, core.NS
    FH, MH = b_fox_f.shape[1], b_m_i.shape[1]
    FW = D // 2
    HD = FW // FH
    MW = D - FW
    PAIRS = FH // 2
    TAPS = w_conv.shape[1]
    COL_Q, COL_K, COL_V, COL_F = 0, FW, 2 * FW, 3 * FW
    COL_MQ = COL_F + FH
    COL_MK, COL_MV, COL_MO, COL_MG = COL_MQ + MW, COL_MQ + 2 * MW, COL_MQ + 3 * MW, COL_MQ + 4 * MW
    NG = FH + 2 * MH
    NR = FH + MH
    V1 = P + 1
    K_SCALE = float(P) ** -0.5
    w_in = w_mix_in.rearrange("a (k p) n -> (a p) k n", p=P)
    w_out = w_mix_out.rearrange("a (k p) n -> (a p) k n", p=P)
    gate_rows = nc.dram_tensor("gate_rows", (NR * S,), F32, kind="Internal").ap()

    with ExitStack() as ctx:
        sb = lambda n, *a: core.sb(f"mx_{n}", *a, ctx=ctx)
        raw_w = sb("raw_w", [P, 2, KD * P])
        w_hi = sb("w_hi", [P, 2, KD * P], F32R)
        w_lo = sb("w_lo", [P, 2, KD * P], F32R)
        yT_fox = sb("yT_fox", [P, PAIRS, S])
        NCONST = (TAPS + 1) * 2 * MH + MH
        consts = sb("consts", [P, NCONST])
        mask_m = sb("mask_m", [P, P])
        m_total = sb("m_total", [P, MH, NS])
        m_cum = sb("m_cum", [P, MH, NS])
        m_b = sb("m_b", [P, MH, NS])

        s = lambda n: core.sem(f"mx_{n}")
        w_loaded = [s("w_loaded0"), s("w_loaded1")]
        w_hi_done = [s("w_hi_done0"), s("w_hi_done1")]
        w_lo_done = [s("w_lo_done0"), s("w_lo_done1")]
        w_used = [s("w_used0"), s("w_used1")]
        small_loaded = s("small_loaded")
        pool_set = s("pool_set")
        gw_cut = s("gw_cut")
        gw_hi_done = s("gw_hi_done")
        z_ready, z_done = s("z_ready"), s("z_done")
        neg_done, exp_done, ln_done = s("neg_done"), s("exp_done"), s("ln_done")
        logf_done = s("logf_done")
        sums_ready, rows_ready = s("sums_ready"), s("rows_ready")
        rows_turned, rows_kept, rows_stored = s("rows_turned"), s("rows_kept"), s("rows_stored")
        const_turned, const_kept = s("const_turned"), s("const_kept")
        dve_step, act_step, pool_step = s("dve_step"), s("act_step"), s("pool_step")
        v_ready, v_kept_even, v_kept_odd = s("v_ready"), s("v_kept_even"), s("v_kept_odd")
        fq_ready, fq_kept = s("fq_ready"), s("fq_kept")
        cum_loaded = s("cum_loaded")
        score_ready, logit_done, prob_done = s("score_ready"), s("logit_done"), s("prob_done")
        pt_ready, pt_act, pt_dve = s("pt_ready"), s("pt_act"), s("pt_dve")
        pv_ready, y_done = s("pv_ready"), s("y_done")
        yt_ready, yt_kept = s("yt_ready"), s("yt_kept")
        x_ready, x_kept = s("x_ready"), s("x_kept")
        b_loaded = s("b_loaded")
        max_done, args_done, weights_done = s("max_done"), s("args_done"), s("weights_done")
        conv_done, silu_done = s("conv_done"), s("silu_done")
        sig_done, sg_done = s("sig_done"), s("sg_done")
        kt_ready, kw_done = s("kt_ready"), s("kw_done")
        qk_ready, sp_done = s("qk_ready"), s("sp_done")
        u_ready, state_done = s("u_ready"), s("state_done")
        spt_ready, spt_kept = s("spt_ready"), s("spt_kept")
        num_ready, inter_kept, o_done = s("num_ready"), s("inter_kept"), s("o_done")
        sq_done, var_done, rpow_done = s("sq_done"), s("var_done"), s("rpow_done")
        yb_done, ybt_ready, ybt_kept = s("yb_done"), s("ybt_ready"), s("ybt_kept")
        gate_loaded, gated = s("gate_loaded"), s("gated")
        y_hi, y_lo = s("y_hi"), s("y_lo")
        out_ready, out_added = s("out_ready"), s("out_added")

        fox = ExitStack()
        fsb = lambda n, *a: core.sb(f"mx_{n}", *a, ctx=fox)
        gw_raw = fsb("gw_raw", [P, KD, NG])
        gw_hi, gw_lo = fsb("gw_hi", [P, KD, NG], F32R), fsb("gw_lo", [P, KD, NG], F32R)
        gbias = fsb("gbias", [P, NG])
        z = fsb("z", [P, NS, NG])
        zneg = fsb("zneg", [P, NS, NG])
        logf = fsb("logf", [P, NS, NG])
        cum_in = fsb("cum_in", [P, NS, NG])
        total = fsb("total", [P, NS, NG])
        before = fsb("before", [P, NS, FH])
        rows_in = fsb("rows_in", [P, NR, NS])
        rows_out = fsb("rows_out", [NR * NS, P])
        upper = fsb("upper", [P, P])
        ones = fsb("ones", [P, P])
        const_rows = fsb("const_rows", [(TAPS + 1) * 2 * MH + MH, P])
        mask_f = fsb("mask_f", [P, P], BF16)
        ident_b = fsb("ident_b", [P, P], BF16)
        v_fox = fsb("v_fox", [P, NS, FW])
        fqT, fkT = fsb("fqT", [P, S]), fsb("fkT", [P, S])
        cum_bc = fsb("cum_bc", [P, 2, S])
        RP = 3
        prob = fsb("prob", [P, RP, S])
        probT = fsb("probT", [P, 2, S])
        y_tok = fsb("y_tok", [P, NS, 2 * HD])
        low = fsb("low", [P, 4 * NS])
        rowsum = fsb("rowsum", [P, 2 * NS])
        rinv = fsb("rinv", [P, 2 * NS])
        wait_tile = fsb("wait_tile", [P, 2 * NS])
        fox.close()
        late = ExitStack()
        yT_ml = core.sb("mx_yT_ml", [P, MH, S], ctx=late)
        ml = ExitStack()
        msb = lambda n, *a: core.sb(f"mx_{n}", *a, ctx=ml)
        v_ml = msb("v_ml", [P, NS, MH, V1])
        pre_q = msb("pre_q", [P, TAPS - 1 + S])
        pre_k = msb("pre_k", [P, TAPS - 1 + S])
        mo = msb("mo", [P, S])
        sg = msb("sg", [P, S])
        mqT = msb("mqT", [P, S])
        mkT = msb("mkT", [P, NS * V1])
        kw = msb("kw", [P, NS * V1])
        dec = msb("dec", [P, S])
        arg = msb("arg", [P, 4, NS])
        mst = msb("mst", [P, NS + 1])
        tiny = msb("tiny", [P, 8, NS])
        sq_junk = msb("sq_junk", [P, P])
        ml.close()
        fin = ExitStack()
        gate = core.sb("mx_gate", [P, D], ctx=fin)
        shift, scale1 = core.sb("mx_shift", [P, D], ctx=fin), core.sb("mx_scale1", [P, D], ctx=fin)
        junk = core.sb("mx_junk", [P, D], ctx=fin)
        xn3 = core.sb("mx_xn", [P, 4, D], ctx=fin)
        fin.close()
        late.close()
        states = mkT[:, :].rearrange("p (c v) -> p c v", v=V1)
        o_all = kw[:, :].rearrange("p (c v) -> p c v", v=V1)
        kw_c = kw[:, 0:S]
        norm = Norm(core, "mxn", shift[:, :], scale1[:, :], junk[:, :], [xn3[:, i, :] for i in range(4)], 0)

        C_V = (0, 0)
        C_F = (2, 2)
        C_MV = (2 + PAIRS, 2 + PAIRS)
        C_M = (4 + PAIRS, 4 + PAIRS)
        C_O = (C_M[0] + 2 * MH, C_M[1] + MH)
        X_PER = 6

        def w_load(sp, slot, c, src):
            if not (isinstance(c, int) and c == 0):
                sp.wait_ge(w_lo_done[slot], c)
            dst = raw_w[:, slot, :].rearrange("p (k n) -> p k n", n=src.shape[2])
            sp.dma_start(dst, src).then_inc(w_loaded[slot], 16)

        def w_cut_hi(act, slot, c, freed=None, is_gated=None):
            if is_gated is None:
                act.wait_ge(w_loaded[slot], c * 16 + 16)
            else:
                act.wait_ge(gated, is_gated)
            if freed is not None:
                act.wait_ge(*freed)
            act.copy(w_hi[:, slot, :], raw_w[:, slot, :]).then_inc(w_hi_done[slot], 1)

        def w_cut_lo(pool, slot, c):
            pool.wait_ge(w_hi_done[slot], c + 1)
            pool.tensor_tensor(w_lo[:, slot, :], raw_w[:, slot, :], w_hi[:, slot, :].bitcast(F32),
                               ALU.subtract).then_inc(w_lo_done[slot], 1)

        def three(pe, dst, a_hi, a_lo, b_hi, b_lo, start, stop):
            pe.matmul(dst, a_hi, b_hi, start=start, stop=False)
            pe.matmul(dst, a_hi, b_lo, start=False, stop=False)
            return pe.matmul(dst, a_lo, b_hi, start=False, stop=stop)

        def by_token(pe, c, ready, before):
            for k in range(KD):
                slot = k // 2 % 2
                if k % 2 == 0:
                    pe.wait_ge(w_lo_done[slot], c[slot] + k // 4 + 1)
                cols = slice(k % 2 * BANK, (k % 2 + 1) * BANK)
                for t in range(NS):
                    before(k, t)
                    tok = slice(t * P, (t + 1) * P)
                    mm = three(pe, core.bank[:, t, :], core.h_hi[:, k, tok], core.h_lo[:, k, tok],
                               w_hi[:, slot, cols], w_lo[:, slot, cols], k == 0, k == KD - 1)
                    if k == KD - 1:
                        mm.then_inc(ready, 1)
                if k % 2 and k < KD - 1:
                    mm.then_inc(w_used[slot], 1)

        def by_feature(pe, dst, slot, half):
            tok = slice(half * BANK, (half + 1) * BANK)
            for k in range(KD):
                cols = slice(k * P, (k + 1) * P)
                mm = three(pe, dst, w_hi[:, slot, cols], w_lo[:, slot, cols],
                           core.h_hi[:, k, tok], core.h_lo[:, k, tok], k == 0, k == KD - 1)
            return mm

        def repeat(eng, n, body):
            body(0, True, False)
            with eng.Fori(1, n - 1) as i:
                body(i, False, False)
            body(n - 1, False, True)

        PER = 2 * NS
        STEP = lambda p, n: p * PER + n

        with nc.Block() as block:

            @block.sync
            def _(sp):
                with nc.allow_non_contiguous_dma(reason="16 gate columns"):
                    sp.dma_start(gw_raw[:, :, 0:FH], w_in[:, :, COL_F:COL_F + FH]).then_inc(small_loaded, 16)
                    sp.dma_start(gw_raw[:, :, FH:NG], w_in[:, :, COL_MG:COL_MG + 2 * MH]).then_inc(small_loaded, 16)
                for lo, hi, src in ((0, FH, b_fox_f), (FH, FH + MH, b_m_i), (FH + MH, NG, b_m_f)):
                    sp.dma_start(gbias[:, lo:hi], src.rearrange("a n -> (a n)").partition_broadcast(P))\
                        .then_inc(small_loaded, 16)
                R0, R1 = TAPS * 2 * MH, (TAPS + 1) * 2 * MH
                sp.dma_start(const_rows[0:R0, :], w_conv.rearrange("a w (c p) -> (a w c) p", p=P)).then_inc(small_loaded, 16)
                sp.dma_start(const_rows[R0:R1, :], b_conv.rearrange("a (c p) -> (a c) p", p=P)).then_inc(small_loaded, 16)
                sp.dma_start(const_rows[R1:, :], g_mhn.rearrange("a (c p) -> (a c) p", p=P)).then_inc(small_loaded, 16)
                for piece in range(4):
                    w_load(sp, piece % 2, C_V[0] + piece // 2, w_in[:, 2 * piece:2 * piece + 2, COL_V:COL_V + FW])
                for slot, col in ((0, COL_Q), (1, COL_K)):
                    w_load(sp, slot, C_F[slot], w_in[:, :, col:col + P])
                sp.wait_ge(rows_kept, 1)
                sp.dma_start(gate_rows.rearrange("(r n) -> r n", n=P), rows_out[:, :]).then_inc(rows_stored, 16)
                sp.wait_ge(rows_stored, 16)

                def fox_loads(p, first, last):
                    if not first:
                        sp.wait_ge(logit_done, p * PER)
                    sp.dma_start(cum_bc[:, :, :], gate_rows[bass.ds(p * (2 * S), 2 * S)]
                                 .rearrange("(e s) -> e s", e=2).partition_broadcast(P)).then_inc(cum_loaded, 16)
                    if not last:
                        for slot, col in ((0, COL_Q), (1, COL_K)):
                            w_load(sp, slot, p + (C_F[slot] + 1), w_in[:, :, bass.ds(p * P + (col + P), P)])

                repeat(sp, PAIRS, fox_loads)
                for piece in range(4):
                    w_load(sp, piece % 2, C_MV[0] + piece // 2, w_in[:, 2 * piece:2 * piece + 2, COL_MV:COL_MV + MW])

                def ml_w(h, c, col):
                    w_load(sp, c % 2, c // 2 + (h * 2 + C_M[0] if c % 2 == 0 else h + C_M[1]),
                           w_in[:, :, bass.ds(h * P + col, P)])

                def ml_loads(h, first, last):
                    if not last:
                        ml_w(h + 1, 0, COL_MQ)
                        ml_w(h + 1, 1, COL_MK)
                    if first:
                        sp.wait_ge(yt_kept, 2 * PAIRS)
                        sp.wait_ge(y_done, PAIRS * PER)
                    else:
                        sp.wait_ge(num_ready, h * 3)
                    sp.dma_start(dec[:, :], gate_rows[bass.ds(h * S + FH * S, S)].partition_broadcast(P))\
                        .then_inc(b_loaded, 16)
                    if not last:
                        ml_w(h + 1, 2, COL_MO)

                for c, col in ((0, COL_MQ), (1, COL_MK), (2, COL_MO)):
                    ml_w(0, c, col)
                repeat(sp, MH, ml_loads)
                sp.wait_ge(ybt_kept, 2 * MH)
                sp.dma_start(gate[:, :], core.mod(gate_row)).then_inc(gate_loaded, 16)
                norm.load(sp, next_mod)
                for n in range(8):
                    dh, piece = n // 4, n % 4
                    w_load(sp, n % 2, C_O[n % 2] + n // 2,
                           w_out[:, 2 * piece:2 * piece + 2, dh * BANK:(dh + 1) * BANK])

            @block.gpsimd
            def _(pool):
                link = Chain(pool, pool_step)
                link(pool.memset(ones[:, :], 1.0))
                link(pool.affine_select(out=upper[:, :], in_=ones[:, :], compare_op=ALU.is_ge, fill=0.0,
                                        base=0, pattern=[[1, P]], channel_multiplier=-1))
                link(pool.memset(mask_m[:, :], 0.0))
                link(pool.affine_select(out=mask_m[:, :], in_=mask_m[:, :], compare_op=ALU.is_ge, fill=NEG,
                                        base=0, pattern=[[-1, P]], channel_multiplier=1))
                link(pool.tensor_scalar(mask_f[:, :], mask_m[:, :], -1.0, None, ALU.mult))
                pool.tensor_copy(ident_b[:, :], core.ident[:, :]).then_inc(pool_set, 1)
                pool.wait_ge(pool_set, 1)
                pool.wait_ge(gw_hi_done, 1)
                flat = lambda t: t[:, :, :].rearrange("p k n -> p (k n)")
                pool.tensor_tensor(flat(gw_lo), flat(gw_raw), flat(gw_hi).bitcast(F32), ALU.subtract)\
                    .then_inc(gw_cut, 1)
                for piece in range(4):
                    w_cut_lo(pool, piece % 2, C_V[0] + piece // 2)
                w_cut_lo(pool, 0, C_F[0])
                w_cut_lo(pool, 1, C_F[1])

                def fox_cut(p, first, last):
                    if not last:
                        w_cut_lo(pool, 0, p + (C_F[0] + 1))
                        w_cut_lo(pool, 1, p + (C_F[1] + 1))

                repeat(pool, PAIRS, fox_cut)
                for piece in range(4):
                    w_cut_lo(pool, piece % 2, C_MV[0] + piece // 2)
                w_cut_lo(pool, 0, C_M[0])
                w_cut_lo(pool, 1, C_M[1])
                w_cut_lo(pool, 0, C_M[0] + 1)

                def ml_cut(h, first, last):
                    if not last:
                        w_cut_lo(pool, 0, h * 2 + (C_M[0] + 2))
                        w_cut_lo(pool, 1, h + (C_M[1] + 1))
                        w_cut_lo(pool, 0, h * 2 + (C_M[0] + 3))
                    pool.wait_ge(var_done, h + 1)
                    pool.tensor_tensor(tiny[:, 5, :], tiny[:, 4, :], core.neg_half[:, :], ALU.pow)\
                        .then_inc(rpow_done, 1)

                repeat(pool, MH, ml_cut)
                pool.wait_ge(gate_loaded, 16)
                for n in range(8):
                    slot, c, dh = n % 2, C_O[n % 2] + n // 2, n // 4
                    pool.wait_ge(w_loaded[slot], 16 * (c + 1))
                    for kk in range(2):
                        piece = raw_w[:, slot, kk * BANK:(kk + 1) * BANK]
                        pool.tensor_tensor(piece, piece, gate[:, dh * BANK:(dh + 1) * BANK], ALU.mult)\
                            .then_inc(gated, 1)
                    w_cut_lo(pool, slot, c)
                for t in range(NS + 1):
                    if t < NS:
                        norm.inverse(pool, t)
                    if t >= 1:
                        norm.add_shift(pool, t - 1)

            @block.scalar
            def _(act):
                link = Chain(act, act_step)
                flat = lambda t: t[:, :, :].rearrange("p k n -> p (k n)")
                act.wait_ge(small_loaded, 16 * 8)
                act.copy(flat(gw_hi), flat(gw_raw)).then_inc(gw_hi_done, 1)
                w_cut_hi(act, 0, 0)
                w_cut_hi(act, 1, 0)
                act.wait_ge(neg_done, 1)
                act.activation(flat(zneg), flat(zneg), ACT.Exp).then_inc(exp_done, 1)
                act.wait_ge(exp_done, 1)
                act.activation(flat(zneg), flat(zneg), ACT.Ln, bias=1.0).then_inc(ln_done, 1)
                w_cut_hi(act, 0, 1, freed=(w_used[0], 1))
                w_cut_hi(act, 1, 1, freed=(w_used[1], 1))
                w_cut_hi(act, 0, C_F[0], freed=(w_used[0], 2))
                for t in range(0, NS, 2):
                    act.wait_ge(v_ready, t + 1)
                    act.copy(v_fox[:, t, :], core.bank[:, t, :]).then_inc(v_kept_even, 1)
                w_cut_hi(act, 1, C_F[1], freed=(v_ready, NS))

                def keep_qk(p, g):
                    half = slice((g % 2) * BANK, (g % 2 + 1) * BANK)
                    act.wait_ge(fq_ready, p * 4 + (g + 1))
                    if g < 2:
                        act.mul(fqT[:, half], core.bank[:, g, :], -float(HD) ** -0.5).then_inc(fq_kept, 1)
                    else:
                        act.copy(fkT[:, half], core.bank[:, g, :]).then_inc(fq_kept, 1)

                for g in range(4):
                    keep_qk(0, g)

                def exp_rows(p, n):
                    w = (n % NS + 1) * P
                    act.wait_ge(logit_done, p * PER + (n + 1))
                    rows = prob[:, n % RP, 0:w]
                    act.activation(rows, rows, ACT.Exp, bias=low[:, n:n + 1], scale=-1.0,
                                   accum_out=rowsum[:, n:n + 1]).then_inc(prob_done, 1)

                def keep_pt(p, n, first):
                    w = min((n % NS + 1) * P, BANK)
                    act.wait_ge(pt_ready, p * PER + (n + 1))
                    if not (first and n < 2):
                        act.wait_ge(pv_ready, p * PER + (n - 1))
                    act.copy(probT[:, n % 2, 0:w], core.bank[:, 4, 0:w]).then_inc(pt_act, 1)

                def fox_body(p, first, last):
                    for m in range(PER + 2):
                        if 1 <= m <= PER:
                            exp_rows(p, m - 1)
                        if m == 3 and not last:
                            w_cut_hi(act, 0, p + (C_F[0] + 1), freed=(fq_ready, p * 4 + 2))
                            w_cut_hi(act, 1, p + (C_F[1] + 1), freed=(fq_ready, p * 4 + 4))
                        if m >= 2:
                            keep_pt(p, m - 2, first)
                    if not last:
                        for g in range(4):
                            keep_qk(p + 1, g)
                    for half in range(2):
                        act.wait_ge(yt_ready, p * 2 + (half + 1))
                        act.copy(yT_fox[:, bass.ds(p, 1), half * BANK:(half + 1) * BANK].rearrange("p a s -> p (a s)"),
                                 core.bank[:, 4 + half, :]).then_inc(yt_kept, 1)

                repeat(act, PAIRS, fox_body)
                w_cut_hi(act, 0, C_MV[0], freed=(fq_ready, 4 * PAIRS - 2))
                w_cut_hi(act, 1, C_MV[1], freed=(fq_ready, 4 * PAIRS))
                w_cut_hi(act, 0, C_MV[0] + 1, freed=(w_used[0], 3))
                w_cut_hi(act, 1, C_MV[1] + 1, freed=(w_used[1], 2))
                w_cut_hi(act, 0, C_M[0], freed=(w_used[0], 4))
                act.wait_ge(y_done, PAIRS * PER)
                for t in range(0, NS, 2):
                    act.wait_ge(v_ready, NS + t + 1)
                    act.copy(v_ml[:, t, :, 0:P], core.bank[:, t, :].rearrange("p (h v) -> p h v", v=P))\
                        .then_inc(v_kept_even, 1)
                w_cut_hi(act, 1, C_M[1], freed=(v_ready, 2 * NS))

                def keep_x(h, g, first):
                    off = (TAPS - 1 if g < 4 else 0) + (g % 2) * BANK
                    act.wait_ge(x_ready, h * X_PER + (g + 1))
                    if not first and g in (0, 2):
                        act.wait_ge(conv_done, h * 2 + (-1 if g == 0 else 0))
                    act.copy((pre_q, pre_k, mo)[g // 2][:, off:off + BANK], core.bank[:, g % 4, :])\
                        .then_inc(x_kept, 1)
                    if g == 1:
                        w_cut_hi(act, 0, h * 2 + (C_M[0] + 1), freed=(x_ready, h * X_PER + 2))

                for g in range(X_PER):
                    keep_x(0, g, True)

                def ml_body(h, first, last):
                    link.at(h)
                    bias = lambda c: consts[:, bass.ds(h + (TAPS * 2 * MH + c), 1)]
                    if not last:
                        w_cut_hi(act, 0, h * 2 + (C_M[0] + 2), freed=(x_ready, h * X_PER + 6))
                        w_cut_hi(act, 1, h + (C_M[1] + 1), freed=(x_ready, h * X_PER + 4))
                    if not first:
                        act.wait_ge(ybt_kept, h * 2)
                    act.wait_ge(x_kept, h * X_PER + X_PER)
                    act.activation(sg[:, :], mo[:, :], ACT.Sigmoid).then_inc(sig_done, 1)
                    for i, buf in enumerate((mqT[:, :], mkT[:, 0:S])):
                        act.wait_ge(conv_done, h * 2 + (i + 1))
                        act.activation(buf, buf, ACT.Silu, bias=bias(i * MH)).then_inc(silu_done, 1)
                        if not last:
                            keep_x(h + 1, 2 * i, False)
                            keep_x(h + 1, 2 * i + 1, False)
                    act.wait_ge(args_done, h + 1)
                    act.activation(arg[:, :, :], arg[:, :, :], ACT.Exp).then_inc(weights_done, 1)
                    act.activation(dec[:, :], dec[:, :], ACT.Exp).then_inc(weights_done, 1)
                    if not last:
                        act.wait_ge(sig_done, h + 1)
                        keep_x(h + 1, 4, False)
                    for half in range(2):
                        act.wait_ge(spt_ready, h * 2 + 2)
                        act.copy(dec[:, half * BANK:(half + 1) * BANK], core.bank[:, (7, 4)[half], :])\
                            .then_inc(spt_kept, 1)
                    if not last:
                        keep_x(h + 1, 5, False)
                    for j in range(NS):
                        r, jj = j // 3, j % 3
                        act.wait_ge(num_ready, h * 3 + (r + 1))
                        act.mul(o_all[:, j, :], core.bank[:, (6, 4, 6)[r], jj * V1:(jj + 1) * V1],
                                arg[:, 2, j:j + 1]).then_inc(inter_kept, 1)
                    for j in range(NS):
                        act.wait_ge(o_done, h * 3 + (j // 3 + 1))
                        link(act.activation(sq_junk[:, :], o_all[:, j, 0:P], ACT.Square,
                                            accum_out=tiny[:, 0, j:j + 1]))
                    act.activation(sq_junk[:, 0:NS], tiny[:, 0, :], ACT.Copy).then_inc(sq_done, 1)

                repeat(act, MH, ml_body)
                for k in range(KD):
                    src = yT_fox[:, k, :] if k < PAIRS else yT_ml[:, k - PAIRS, :]
                    if k in (0, PAIRS):
                        act.wait_ge(*((yt_kept, 2 * PAIRS) if k == 0 else (ybt_kept, 2 * MH)))
                    act.copy(core.h_hi[:, k, :], src).then_inc(y_hi, 1)
                    if k < 2:
                        w_cut_hi(act, k, C_O[k], freed=(x_ready, MH * X_PER - 2 * k), is_gated=2 * k + 2)
                for n, freed in ((2, (w_used[0], 5)), (3, (w_used[1], 3)), (4, (w_used[0], 6)),
                                 (5, (out_ready, NS)), (6, (w_used[0], 7)), (7, (w_used[1], 4))):
                    w_cut_hi(act, n % 2, C_O[n % 2] + n // 2, freed=freed, is_gated=2 * n + 2)
                for t in range(NS + 2):
                    if t < NS:
                        act.wait_ge(out_added, NS + t + 1)
                        norm.square(act, t)
                    if t >= 2:
                        norm.keep_hi(act, t - 2)

            @block.vector
            def _(dve):
                link = Chain(dve, dve_step)
                gates = lambda t, a, b: t[:, :, a:b].rearrange("p t g -> p g t")
                dve.wait_ge(small_loaded, 16 * 8)
                dve.wait_ge(const_turned, 1)
                dve.tensor_copy(consts[:, :], core.bank[:, 1, 0:NCONST]).then_inc(const_kept, 1)
                dve.wait_ge(z_ready, 1)
                dve.tensor_tensor(z[:, :, :], core.bank[:, 0, 0:NS * NG].rearrange("p (t g) -> p t g", g=NG),
                                  gbias[:, :].unsqueeze(1).to_broadcast([P, NS, NG]), ALU.add).then_inc(z_done, 1)
                dve.wait_ge(z_done, 1)
                link(dve.tensor_scalar(logf[:, :, :], z[:, :, :], 0.0, None, ALU.min))
                dve.scalar_tensor_tensor(zneg[:, :, :], logf[:, :, :], 2.0, z[:, :, :], ALU.mult, ALU.subtract)\
                    .then_inc(neg_done, 1)
                dve.wait_ge(ln_done, 1)
                dve.tensor_tensor(logf[:, :, :], logf[:, :, :], zneg[:, :, :], ALU.subtract).then_inc(logf_done, 1)
                for t in range(1, NS, 2):
                    dve.wait_ge(v_ready, t + 1)
                    dve.tensor_copy(v_fox[:, t, :], core.bank[:, t, :]).then_inc(v_kept_odd, 1)
                dve.wait_ge(sums_ready, 1)
                tg = lambda b: core.bank[:, b, 0:NS * NG].rearrange("p (t g) -> p t g", g=NG)
                link(dve.tensor_copy(cum_in[:, :, :], tg(4)))
                link(dve.tensor_copy(total[:, :, :], tg(5)))
                link(dve.memset(before[:, 0, :], 0.0))
                for t in range(1, NS):
                    link(dve.tensor_tensor(before[:, t, :], before[:, t - 1, :], total[:, t - 1, 0:FH], ALU.add))
                link(dve.tensor_tensor(rows_in[:, 0:FH, :], gates(cum_in, 0, FH), gates(before, 0, FH), ALU.add))
                link(dve.tensor_tensor(rows_in[:, FH:NR, :], gates(z, FH, FH + MH), gates(cum_in, FH + MH, NG),
                                       ALU.subtract))
                link(dve.tensor_copy(m_b[:, :, :], rows_in[:, FH:NR, :]))
                link(dve.tensor_copy(m_total[:, :, :], gates(total, FH + MH, NG)))
                dve.tensor_copy(m_cum[:, :, :], gates(cum_in, FH + MH, NG)).then_inc(rows_ready, 1)
                dve.wait_ge(rows_turned, 1)
                dve.tensor_copy(rows_out[:, :], core.bank[0:NR * NS, 6, 0:P]).then_inc(rows_kept, 1)

                def logits(p, n, first):
                    w = (n % NS + 1) * P
                    if n == 0:
                        dve.wait_ge(cum_loaded, p * 16 + 16)
                    dve.wait_ge(score_ready, p * PER + (n + 1))
                    if not (first and n < RP):
                        dve.wait_ge(pt_ready, p * PER + (n - RP + 1))
                    b = 2 * (n % 2)
                    dve.memset(wait_tile[:, n:n + 1], 0.0)
                    dve.tensor_tensor_reduce(prob[:, n % RP, 0:w],
                                             core.bank[:, b:b + 2, :].rearrange("p b n -> p (b n)")[:, 0:w],
                                             cum_bc[:, n // NS, 0:w], 1.0, 3e38, ALU.add, ALU.min,
                                             low[:, n:n + 1]).then_inc(logit_done, 1)

                def keep_pt(p, n, first):
                    w = (n % NS + 1) * P
                    if w <= BANK:
                        return
                    dve.wait_ge(pt_ready, p * PER + (n + 1))
                    dve.wait_ge(pv_ready, p * PER + (n - 1))
                    dve.tensor_copy(probT[:, n % 2, BANK:w], core.bank[:, 5, 0:w - BANK]).then_inc(pt_dve, 1)

                def normalise(p, n, first):
                    dve.wait_ge(pv_ready, p * PER + (n + 1))
                    if not first and n == 0:
                        dve.wait_ge(yt_ready, p * 2)
                    link(dve.reciprocal(rinv[:, n:n + 1], rowsum[:, n:n + 1]))
                    dve.tensor_scalar(y_tok[:, n % NS, (n // NS) * HD:(n // NS + 1) * HD],
                                      core.bank[:, 6 + n % 2, 0:HD], rinv[:, n:n + 1], None, ALU.mult)\
                        .then_inc(y_done, 1)

                def fox_body(p, first, last):
                    link.at(p)
                    for m in range(PER + 3):
                        if m < PER:
                            logits(p, m, first)
                        if 2 <= m < PER + 2:
                            keep_pt(p, m - 2, first)
                        if m >= 3:
                            normalise(p, m - 3, first)

                repeat(dve, PAIRS, fox_body)
                link.leave(PAIRS)
                dve.wait_ge(yt_kept, 2 * PAIRS)
                link(dve.memset(v_ml[:, :, :, P:V1], 1.0))
                link(dve.memset(pre_q[:, 0:TAPS - 1], 0.0))
                link(dve.memset(pre_k[:, 0:TAPS - 1], 0.0))
                link(dve.memset(mst[:, 0:1], 0.0))
                for t in range(1, NS, 2):
                    dve.wait_ge(v_ready, NS + t + 1)
                    dve.tensor_copy(v_ml[:, t, :, 0:P], core.bank[:, t, :].rearrange("p (h v) -> p h v", v=P))\
                        .then_inc(v_kept_odd, 1)

                chunks = lambda t: t.rearrange("p (c s) -> p c s", s=P)

                def ml_body(h, first, last):
                    link.at(h)
                    if not first:
                        dve.wait_ge(num_ready, h * 3)
                    for i, (src, dst) in enumerate(((pre_q, mqT[:, :]), (pre_k, mkT[:, 0:S]))):
                        dve.wait_ge(x_kept, h * X_PER + (2 * i + 2))
                        for w in range(TAPS):
                            tap = consts[:, bass.ds(h + (w * 2 * MH + i * MH), 1)]
                            if w == 0:
                                link(dve.tensor_scalar(dst, src[:, 0:S], tap, None, ALU.mult))
                            elif w < TAPS - 1:
                                link(dve.scalar_tensor_tensor(dst, src[:, w:w + S], tap, dst, ALU.mult, ALU.add))
                            else:
                                dve.scalar_tensor_tensor(dst, src[:, w:w + S], tap, dst, ALU.mult, ALU.add)\
                                    .then_inc(conv_done, 1)
                    head = lambda t: t[:, bass.ds(h, 1), :].rearrange("p a c -> p (a c)")
                    prev = mst[:, 0:NS]
                    dve.wait_ge(b_loaded, h * 16 + 16)
                    link(dve.tensor_reduce(tiny[:, 1, :], chunks(dec[:, :]), AX.X, ALU.max))
                    link(dve.tensor_tensor_scan(mst[:, 1:NS + 1], tiny[:, 1, :], head(m_total), 0.0, ALU.max, ALU.add))
                    link(dve.tensor_tensor(tiny[:, 1, :], tiny[:, 1, :], prev, ALU.max))
                    link(dve.tensor_tensor(arg[:, 0, :], prev, tiny[:, 1, :], ALU.subtract))
                    link(dve.tensor_tensor(arg[:, 1, :], head(m_b), tiny[:, 1, :], ALU.subtract))
                    link(dve.tensor_tensor(chunks(dec[:, :]), chunks(dec[:, :]),
                                           mask_m[:, :].unsqueeze(1).to_broadcast([P, NS, P]), ALU.add))
                    link(dve.tensor_reduce(tiny[:, 2, :], chunks(dec[:, :]), AX.X, ALU.max))
                    link(dve.tensor_tensor(tiny[:, 2, :], tiny[:, 2, :], prev, ALU.max))
                    link(dve.tensor_tensor(arg[:, 2, :], prev, tiny[:, 2, :], ALU.subtract))
                    link(dve.scalar_tensor_tensor(arg[:, 3, :], head(m_cum), -1.0, tiny[:, 2, :],
                                                  ALU.mult, ALU.subtract))
                    dve.tensor_tensor(chunks(dec[:, :]), chunks(dec[:, :]),
                                      tiny[:, 2, :].unsqueeze(2).to_broadcast([P, NS, P]), ALU.subtract)\
                        .then_inc(args_done, 1)
                    dve.wait_ge(sig_done, h + 1)
                    dve.tensor_scalar(sg[:, :], sg[:, :], consts[:, bass.ds(h + (TAPS + 1) * 2 * MH, 1)], None,
                                      ALU.mult).then_inc(sg_done, 1)
                    dve.wait_ge(weights_done, h * 2 + 2)
                    link(dve.tensor_scalar(arg[:, 1, :], arg[:, 1, :], K_SCALE, None, ALU.mult))
                    for half in range(2):
                        c4 = slice(4 * half, 4 * half + 4)
                        dve.wait_ge(kt_ready, h * 2 + (half + 1))
                        dve.tensor_tensor(chunks(kw_c)[:, c4, :], chunks(core.bank[:, 4 + half, :]),
                                          arg[:, 1, c4].unsqueeze(2).to_broadcast([P, 4, P]), ALU.mult)\
                            .then_inc(kw_done, 1)
                    for half in range(2):
                        part = dec[:, half * BANK:(half + 1) * BANK]
                        dve.wait_ge(qk_ready, h * 2 + (half + 1))
                        dve.scalar_tensor_tensor(part, core.bank[:, 6 + half, :], K_SCALE, part, ALU.mult, ALU.mult)\
                            .then_inc(sp_done, 1)
                    dve.memset(states[:, 0, :], 0.0).then_inc(state_done, 1)
                    for j in range(NS - 1):
                        dve.wait_ge(u_ready, h * 3 + (j // 3 + 1))
                        dve.wait_ge(state_done, h * NS + (j + 1))
                        dve.scalar_tensor_tensor(states[:, j + 1, :], states[:, j, :], arg[:, 0, j:j + 1],
                                                 core.bank[:, 4 + j // 3, (j % 3) * V1:(j % 3 + 1) * V1],
                                                 ALU.mult, ALU.add).then_inc(state_done, 1)
                    for r in range(3):
                        j0, j1 = 3 * r, min(3 * r + 3, NS)
                        dve.wait_ge(inter_kept, h * NS + j1)
                        dve.tensor_tensor(o_all[:, j0:j1, :], o_all[:, j0:j1, :],
                                          core.bank[:, (5, 7, 5)[r], 0:(j1 - j0) * V1]
                                          .rearrange("p (c v) -> p c v", v=V1), ALU.add).then_inc(o_done, 1)
                    den = o_all[:, :, P:V1].rearrange("p c v -> p (c v)")
                    dve.wait_ge(o_done, h * 3 + 3)
                    link(dve.scalar_tensor_tensor(tiny[:, 1, :], den, -1.0, den, ALU.mult, ALU.max))
                    link(dve.tensor_tensor(tiny[:, 1, :], tiny[:, 1, :], arg[:, 3, :], ALU.max))
                    link(dve.reciprocal(tiny[:, 2, :], tiny[:, 1, :]))
                    dve.wait_ge(sq_done, h + 1)
                    link(dve.tensor_tensor(tiny[:, 3, :], tiny[:, 0, :], tiny[:, 2, :], ALU.mult))
                    link(dve.tensor_tensor(tiny[:, 3, :], tiny[:, 3, :], tiny[:, 2, :], ALU.mult))
                    dve.tensor_scalar(tiny[:, 4, :], tiny[:, 3, :], 1.0 / P, EPS, ALU.mult, ALU.add)\
                        .then_inc(var_done, 1)
                    dve.wait_ge(rpow_done, h + 1)
                    link(dve.tensor_tensor(tiny[:, 6, :], tiny[:, 5, :], tiny[:, 2, :], ALU.mult))
                    dve.tensor_tensor(o_all[:, :, 0:P], o_all[:, :, 0:P],
                                      tiny[:, 6, :].unsqueeze(2).to_broadcast([P, NS, P]), ALU.mult)\
                        .then_inc(yb_done, 1)
                    for half in range(2):
                        dve.wait_ge(ybt_ready, h * 2 + (half + 1))
                        cols = slice(half * BANK, (half + 1) * BANK)
                        dve.tensor_tensor(yT_ml[:, bass.ds(h, 1), cols].rearrange("p a s -> p (a s)"),
                                          core.bank[:, (7, 4)[half], :], sg[:, cols], ALU.mult)\
                            .then_inc(ybt_kept, 1)

                repeat(dve, MH, ml_body)
                link.leave(MH)
                for k in range(KD):
                    src = yT_fox[:, k, :] if k < PAIRS else yT_ml[:, k - PAIRS, :]
                    dve.wait_ge(y_hi, k + 1)
                    dve.tensor_tensor(core.h_lo[:, k, :], src, core.h_hi[:, k, :].bitcast(F32), ALU.subtract)\
                        .then_inc(y_lo, 1)
                for n in range(2 * NS):
                    t, dh = n % NS, n // NS
                    part = core.xres[:, t, dh * BANK:(dh + 1) * BANK]
                    dve.wait_ge(out_ready, n + 1)
                    dve.tensor_tensor(part, core.bank[:, t, :], part, ALU.add).then_inc(out_added, 1)
                for t in range(NS + 2):
                    if t < NS:
                        norm.scale(dve, t)
                    if t >= 2:
                        norm.keep_lo(dve, t - 2)

            @block.tensor
            def _(pe):
                pe.wait_ge(small_loaded, 16 * 8)
                pe.transpose(core.bank[:, 1, 0:NCONST], const_rows[:, :], core.ident[0:NCONST, 0:NCONST])\
                    .then_inc(const_turned, 1)
                pe.wait_ge(gw_cut, 1)
                for t in range(NS):
                    tok = slice(t * P, (t + 1) * P)
                    for k in range(KD):
                        mm = three(pe, core.bank[:, 0, t * NG:(t + 1) * NG], core.h_hi[:, k, tok],
                                   core.h_lo[:, k, tok], gw_hi[:, k, :], gw_lo[:, k, :], k == 0, k == KD - 1)
                mm.then_inc(z_ready, 1)

                def v_waits(k, t):
                    if k == 0 and t < 2:
                        pe.wait_ge((z_done, const_kept)[t], 1)

                by_token(pe, C_V, v_ready, v_waits)
                pe.wait_ge(logf_done, 1)
                pe.wait_ge(pool_set, 1)
                pe.wait_ge(v_kept_even, NS // 2)
                pe.wait_ge(v_kept_odd, NS // 2)
                flat = lambda t: t[:, :, :].rearrange("p k n -> p (k n)")
                pe.matmul(core.bank[:, 4, 0:NS * NG], upper[:, :], flat(logf), start=True, stop=True)
                pe.matmul(core.bank[:, 5, 0:NS * NG], ones[:, :], flat(logf), start=True, stop=True)\
                    .then_inc(sums_ready, 1)

                def project_qk(p, g):
                    if g % 2 == 0:
                        pe.wait_ge(w_lo_done[g // 2], p + (C_F[g // 2] + 1))
                    by_feature(pe, core.bank[:, g, :], g // 2, g % 2).then_inc(fq_ready, 1)

                project_qk(0, 0)
                project_qk(0, 1)
                pe.wait_ge(rows_ready, 1)
                pe.transpose(core.bank[0:NR * NS, 6, 0:P], rows_in[:, :, :].rearrange("p r t -> p (r t)"),
                             core.ident[:, :]).then_inc(rows_turned, 1)
                project_qk(0, 2)
                project_qk(0, 3)

                def scores(p, n, first):
                    e, i = n // NS, n % NS
                    heads = slice(e * HD, (e + 1) * HD)
                    w = (i + 1) * P
                    if n == 0:
                        pe.wait_ge(fq_kept, p * 4 + 4)
                        if first:
                            pe.wait_ge(rows_kept, 1)
                    if not (first and n < 2):
                        pe.wait_ge(logit_done, p * PER + (n - 1))
                    for b in range((w + BANK - 1) // BANK):
                        k0, k1 = b * BANK, min((b + 1) * BANK, w)
                        pe.matmul(core.bank[:, 2 * (n % 2) + b, 0:k1 - k0], fqT[heads, i * P:(i + 1) * P],
                                  fkT[heads, k0:k1], start=True, stop=(k1 < w))
                    mm = pe.matmul(core.bank[:, 2 * (n % 2) + b, k1 - k0 - P:k1 - k0], ident_b[:, :], mask_f[:, :],
                                   start=False, stop=True)
                    mm.then_inc(score_ready, 1)

                def turn_prob(p, n, first):
                    i = n % NS
                    pe.wait_ge(prob_done, p * PER + (n + 1))
                    if n >= 1:
                        pe.wait_ge(pt_act, p * PER + n)
                        hi = 4 * ((n - 1) // NS) + max(0, (n - 1) % NS - 3)
                        if hi:
                            pe.wait_ge(pt_dve, p * NS + hi)
                    elif not first:
                        pe.wait_ge(yt_kept, p * 2)
                    for j in range(i + 1):
                        mm = pe.transpose(core.bank[:, 4 + j // 4, (j % 4) * P:(j % 4 + 1) * P],
                                          prob[:, n % RP, j * P:(j + 1) * P], core.ident[:, :])
                    mm.then_inc(pt_ready, 1)

                def values(p, n, first):
                    e, i = n // NS, n % NS
                    pe.wait_ge(pt_act, p * PER + (n + 1))
                    hi = 4 * e + max(0, i - 3)
                    if hi:
                        pe.wait_ge(pt_dve, p * NS + hi)
                    if not (first and n < 2):
                        pe.wait_ge(y_done, p * PER + (n - 1))
                    for j in range(i + 1):
                        mm = pe.matmul(core.bank[:, 6 + n % 2, 0:HD], probT[:, n % 2, j * P:(j + 1) * P],
                                       v_fox[:, j, bass.ds(p * (2 * HD) + e * HD, HD)], start=(j == 0), stop=(j == i))
                    mm.then_inc(pv_ready, 1)

                def fox_body(p, first, last):
                    for m in range(PER + 3):
                        if m < PER:
                            scores(p, m, first)
                        if 2 <= m < PER + 2:
                            turn_prob(p, m - 2, first)
                        if m >= 3:
                            values(p, m - 3, first)
                        if m in (PER, PER + 1) and not last:
                            pe.wait_ge(logit_done, p * PER + (m - 1))
                            project_qk(p + 1, 2 * (m - PER))
                            project_qk(p + 1, 2 * (m - PER) + 1)
                    pe.wait_ge(y_done, p * PER + PER)
                    pe.wait_ge(pt_act, p * PER + PER)
                    for t in range(NS):
                        mm = pe.transpose(core.bank[:, 4 + t // 4, (t % 4) * P:(t % 4 + 1) * P], y_tok[:, t, :],
                                          core.ident[:, :])
                        if t % 4 == 3:
                            mm.then_inc(yt_ready, 1)

                repeat(pe, PAIRS, fox_body)

                def mv_waits(k, t):
                    if k == 0 and t in (0, 4):
                        if t == 0:
                            pe.wait_ge(logit_done, PAIRS * PER)
                        else:
                            pe.wait_ge(yt_kept, 2 * PAIRS)

                by_token(pe, C_MV, v_ready, mv_waits)

                def project(h, g):
                    slot = g // 2 % 2
                    if g % 2 == 0:
                        pe.wait_ge(w_lo_done[slot], h + (C_M[1] + 1) if slot else h * 2 + (C_M[0] + g // 4 + 1))
                    if g < 4:
                        if not (isinstance(h, int) and h == 0):
                            pe.wait_ge(x_kept, h * X_PER)
                    else:
                        pe.wait_ge(x_kept, h * X_PER + (g - 3))
                    by_feature(pe, core.bank[:, g % 4, :], slot, g % 2).then_inc(x_ready, 1)

                pe.wait_ge(v_kept_even, NS)
                pe.wait_ge(v_kept_odd, NS)
                for g in range(X_PER):
                    project(0, g)

                def ml_body(h, first, last):
                    c_of = lambda j: slice(j * P, (j + 1) * P)
                    if not last:
                        for g in range(4):
                            project(h + 1, g)
                    pe.wait_ge(silu_done, h * 2 + 2)
                    if not first:
                        pe.wait_ge(ybt_kept, h * 2)
                    for j in range(NS):
                        mm = pe.transpose(core.bank[:, 4 + j // 4, c_of(j % 4)], mkT[:, c_of(j)], core.ident[:, :])
                        if j % 4 == 3:
                            mm.then_inc(kt_ready, 1)
                    for j in range(NS):
                        mm = pe.matmul(core.bank[:, 6 + j // 4, c_of(j % 4)], mqT[:, c_of(j)], mkT[:, c_of(j)],
                                       start=True, stop=True)
                        if j % 4 == 3:
                            mm.then_inc(qk_ready, 1)
                    if not last:
                        project(h + 1, 4)
                    for j in range(NS - 1):
                        if j in (0, 3):
                            pe.wait_ge(kw_done, h * 2 + 2)
                        if j == 6:
                            pe.wait_ge(sp_done, h * 2 + 1)
                        mm = pe.matmul(core.bank[:, 4 + j // 3, (j % 3) * V1:(j % 3 + 1) * V1], kw_c[:, c_of(j)],
                                       v_ml[:, j, bass.ds(h, 1), :].rearrange("p a v -> p (a v)"),
                                       start=True, stop=True)
                        if j in (2, 5, 6):
                            mm.then_inc(u_ready, 1)
                    pe.wait_ge(sp_done, h * 2 + 2)
                    pe.wait_ge(state_done, h * NS + 4)
                    for j in range(NS):
                        mm = pe.transpose(core.bank[:, (7, 4)[j // 4], c_of(j % 4)], dec[:, c_of(j)],
                                          core.ident[:, :])
                        if j % 4 == 3:
                            mm.then_inc(spt_ready, 1)
                    if not last:
                        project(h + 1, 5)
                    pe.wait_ge(state_done, h * NS + NS)
                    for r in range(3):
                        num_b, int_b = ((5, 6), (7, 4), (5, 6))[r]
                        if r == 0:
                            pe.wait_ge(spt_kept, h * 2 + 2)
                        if r == 2:
                            pe.wait_ge(o_done, h * 3 + 1)
                        for j in range(3 * r, min(3 * r + 3, NS)):
                            cols = slice((j % 3) * V1, (j % 3 + 1) * V1)
                            pe.matmul(core.bank[:, num_b, cols], dec[:, c_of(j)],
                                      v_ml[:, j, bass.ds(h, 1), :].rearrange("p a v -> p (a v)"),
                                      start=True, stop=True)
                            mm = pe.matmul(core.bank[:, int_b, cols], mqT[:, c_of(j)], states[:, j, :],
                                           start=True, stop=True)
                        mm.then_inc(num_ready, 1)
                    pe.wait_ge(yb_done, h + 1)
                    for j in range(NS):
                        mm = pe.transpose(core.bank[:, (7, 4)[j // 4], c_of(j % 4)], o_all[:, j, 0:P],
                                          core.ident[:, :])
                        if j % 4 == 3:
                            mm.then_inc(ybt_ready, 1)

                repeat(pe, MH, ml_body)

                def out_waits(k, t, dh):
                    if t == 0 and dh == 0:
                        pe.wait_ge(y_lo, k + 1)
                        if k == 0:
                            pe.wait_ge(ybt_kept, 2 * MH)
                    if k == 0 and dh == 1:
                        pe.wait_ge(out_added, t + 1)

                for dh in range(2):
                    by_token(pe, (C_O[0] + 2 * dh, C_O[1] + 2 * dh), out_ready, lambda k, t: out_waits(k, t, dh))
                pe.wait_ge(out_added, 2 * NS)
                for t in range(NS):
                    norm.turn(pe, t)


def program(nc, x, c, w_ada, b_ada, w_ffn1_in, w_ffn1_out, w_mix_in, b_fox_f, b_m_i, b_m_f,
            w_conv, b_conv, g_mhn, w_mix_out, w_ffn2_in, w_ffn2_out, g_final, out):
    with ExitStack() as ctx:
        core = Core(nc, ctx, x)
        ffn(core, "f1", w_ffn1_in, w_ffn1_out, next_mod=3, start_in=(x, c, w_ada, b_ada))
        core.end_part()
        mixer(core, w_mix_in, b_fox_f, b_m_i, b_m_f, w_conv, b_conv, g_mhn, w_mix_out, 5, 6)
        core.end_part()
        ffn(core, "f2", w_ffn2_in, w_ffn2_out, gate_row=8, g_final=g_final, out=out)


_INS = ['x', 'c', 'w_ada', 'b_ada', 'w_ffn1_in', 'w_ffn1_out', 'w_mix_in', 'b_fox_f', 'b_m_i', 'b_m_f',
        'w_conv', 'b_conv', 'g_mhn', 'w_mix_out', 'w_ffn2_in', 'w_ffn2_out', 'g_final']


def kernel(**inputs):
    import numpy as np
    import concourse.bacc as bacc
    from concourse.bass_utils import run_bass_kernel_spmd

    nc = bacc.Bacc("TRN2", target_bir_lowering=False, num_devices=1)
    arrays, args = {}, []
    for name in _INS:
        a = np.ascontiguousarray(inputs[name])
        arrays[f"in_{name}"] = a
        args.append(nc.dram_tensor(f"in_{name}", a.shape, mybir.dt.from_np(a.dtype), kind="ExternalInput").ap())
    shape = inputs['x'].shape
    args.append(nc.dram_tensor("out_y", shape, F32, kind="ExternalOutput").ap())
    program(nc, *args)
    r = run_bass_kernel_spmd(nc, [arrays], core_ids=[0])
    return r.results[0]["out_y"]
```

```python
from contextlib import ExitStack

import concourse.bass as bass
from concourse import mybir

F32 = mybir.dt.float32
F32R = mybir.dt.float32r
BF16 = mybir.dt.bfloat16
ALU = mybir.AluOpType
ACT = mybir.ActivationFunctionType
AX = mybir.AxisListType

P = 128
BANK = 512
EPS = 1e-6
NEG = -1e30


class Core:

    def __init__(self, nc, ctx, x):
        self.nc, self.ctx, self.sems = nc, ctx, []
        self.S, self.D = x.shape[1], x.shape[2]
        self.KD = self.D // P
        self.NS = self.S // P
        self.NH = self.S // BANK
        self.xres = self.sb("xres", [P, self.NS, self.D])
        self.h_hi = self.sb("h_hi", [P, self.KD, self.S], F32R)
        with ExitStack() as early:
            self.x_turned = self.sb("x_turned", [P, self.KD, self.S], ctx=early)
        self.h_lo = self.sb("h_lo", [P, self.KD, self.S], F32R)
        self.ident = self.sb("ident", [P, P])
        self.rms = self.sb("rms", [P, 3, self.NS])
        self.neg_half = self.sb("neg_half", [P, self.NS])
        self.bank = ctx.enter_context(nc.psum_tensor("bank", [P, 8, BANK], F32))
        self.mod_rows = nc.dram_tensor("mod_rows", (9 * self.D,), F32, kind="Internal").ap()

    def sb(self, name, shape, dt=F32, ctx=None):
        return (ctx or self.ctx).enter_context(self.nc.sbuf_tensor(name, shape, dt))

    def sem(self, name):
        self.sems.append(self.nc.alloc_semaphore(name=name))
        return self.sems[-1]

    def kept_sem(self, name):
        return self.nc.alloc_semaphore(name=name)

    def end_part(self):
        self.nc.clear_and_free_semaphores(self.sems)
        self.nc.all_engine_barrier()
        self.sems = []

    def mod(self, m):
        return self.mod_rows[m * self.D:(m + 1) * self.D].partition_broadcast(P)


class Norm:
    DVE_TILES = (5, 7)

    def __init__(self, core, tag, shift, scale1, junk, xn, first_bank):
        self.c, self.shift, self.scale1, self.junk, self.xn = core, shift, scale1, junk, xn
        self.first_bank = first_bank
        s = core.sem
        self.loaded = s(f"{tag}_mod_loaded")
        self.squared = s(f"{tag}_squared")
        self.mean_done = s(f"{tag}_mean_done")
        self.rms_done = s(f"{tag}_rms_done")
        self.scaled = s(f"{tag}_scaled")
        self.shifted = [s(f"{tag}_shifted_pool"), s(f"{tag}_shifted_dve")]
        self.turned = s(f"{tag}_turned")
        self.hi_done = s(f"{tag}_hi_done")
        self.lo_done = s(f"{tag}_lo_done")

    def load(self, sp, m):
        sp.dma_start(self.shift, self.c.mod(m)).then_inc(self.loaded, 16)
        sp.dma_start(self.scale1, self.c.mod(m + 1)).then_inc(self.loaded, 16)

    def bank_of(self, t):
        return self.first_bank + 2 * (t % 2)

    def square(self, act, t):
        if t:
            act.wait_ge(self.squared, t)
        act.activation(self.junk, self.c.xres[:, t, :], ACT.Square,
                       accum_out=self.c.rms[:, 0, t:t + 1]).then_inc(self.squared, 1)

    def inverse(self, pool, t):
        c = self.c
        pool.wait_ge(self.squared, t + 1)
        pool.tensor_scalar(c.rms[:, 1, t:t + 1], c.rms[:, 0, t:t + 1], 1.0 / c.D, EPS,
                           ALU.mult, ALU.add).then_inc(self.mean_done, 1)
        pool.wait_ge(self.mean_done, t + 1)
        pool.tensor_tensor(c.rms[:, 2, t:t + 1], c.rms[:, 1, t:t + 1], c.neg_half[:, t:t + 1],
                           ALU.pow).then_inc(self.rms_done, 1)

    def scale(self, dve, t):
        c, n = self.c, len(self.xn)
        if t == 0:
            dve.wait_ge(self.loaded, 32)
        dve.wait_ge(self.rms_done, t + 1)
        if t >= n:
            dve.wait_ge(self.turned, 2 * (t - n) + 2)
        dve.scalar_tensor_tensor(self.xn[t % n], c.xres[:, t, :], c.rms[:, 2, t:t + 1], self.scale1,
                                 ALU.mult, ALU.mult).then_inc(self.scaled, 1)
        if t in self.DVE_TILES:
            dve.wait_ge(self.scaled, t + 1)
            dve.tensor_tensor(self.xn[t % n], self.xn[t % n], self.shift, ALU.add).then_inc(self.shifted[1], 1)

    def add_shift(self, pool, t):
        n = len(self.xn)
        if t in self.DVE_TILES:
            return
        if t == 0:
            pool.wait_ge(self.loaded, 32)
        pool.wait_ge(self.scaled, t + 1)
        pool.tensor_tensor(self.xn[t % n], self.xn[t % n], self.shift, ALU.add).then_inc(self.shifted[0], 1)

    def turn(self, pe, t):
        c, n = self.c, len(self.xn)
        on_dve = t in self.DVE_TILES
        pe.wait_ge(self.shifted[on_dve], sum((i in self.DVE_TILES) == on_dve for i in range(t + 1)))
        if t >= 2:
            pe.wait_ge(self.lo_done, 2 * (t - 2) + 2)
        for half in range(2):
            for k in range(4):
                mm = pe.transpose(c.bank[:, self.bank_of(t) + half, k * P:(k + 1) * P],
                                  self.xn[t % n][:, (4 * half + k) * P:(4 * half + k + 1) * P], c.ident[:, :])
            mm.then_inc(self.turned, 1)

    def _h(self, which, t, half):
        return which[:, 4 * half:4 * half + 4, t * P:(t + 1) * P]

    def _turned(self, t, half):
        return self.c.bank[:, self.bank_of(t) + half, :].rearrange("p (k s) -> p k s", k=4)

    def keep_hi(self, act, t):
        for half in range(2):
            act.wait_ge(self.turned, 2 * t + half + 1)
            act.copy(self._h(self.c.h_hi, t, half), self._turned(t, half)).then_inc(self.hi_done, 1)

    def keep_lo(self, dve, t):
        for half in range(2):
            dve.wait_ge(self.hi_done, 2 * t + half + 1)
            dve.tensor_tensor(self._h(self.c.h_lo, t, half), self._turned(t, half),
                              self._h(self.c.h_hi, t, half).bitcast(F32),
                              ALU.subtract).then_inc(self.lo_done, 1)


class Start:
    RING = 4

    def __init__(self, core, x, c_vec, w_ada, b_ada, steps, buf):
        self.c, self.x, self.c_vec, self.w_ada, self.b_ada = core, x, c_vec, w_ada, b_ada
        D = core.D
        self.M = w_ada.shape[2] // D
        self.COLS = (self.M - 3) * D // steps
        self.TILES = self.COLS // P
        self.LEAD = core.KD + 1
        self.acc, self.gate = buf.shift_scale[:, :], buf.gate[:, :]
        self.ring = [buf.ada_ring[:, r, :] for r in range(self.RING)]
        self.xn = [buf.raw_out[:, i, :] for i in range(2)]
        self.junk = buf.act_f[:, :, :].rearrange("p j n -> p (j n)")
        self.c_act, self.brow, self.bcol, self.mcol, self.mrow = buf.c_act, buf.brow, buf.bcol, buf.mcol, buf.mrow
        self.ones, self.halves = buf.ones, buf.halves
        s = core.sem
        self.small_loaded, self.bias_loaded = s("small_loaded"), s("gate_bias_loaded")
        self.x_loaded = [s(f"x_loaded{t}") for t in range(core.NS)]
        self.ring_loaded = [s(f"ada_loaded{i}") for i in range(self.RING)]
        self.ident_zero, self.consts = s("ident_zero"), s("consts")
        self.b_turned, self.b_kept, self.c_act_done = s("b_turned"), s("b_kept"), s("c_act_done")
        self.squared, self.mean_done, self.rms_done = s("squared"), s("mean_done"), s("rms_done")
        self.xn_done, self.turned = s("xn_done"), s("turned")
        self.kept_low, self.kept_high = s("turned_kept_low"), s("turned_kept_high")
        self.summed, self.cols_ready, self.cols_kept = s("ada_summed"), s("mod_cols_ready"), s("mod_cols_kept")
        self.h_made, self.h_hi_done, self.h_lo_done = s("h_made"), s("h_hi_done"), s("h_lo_done")
        self.gate_spread, self.gate_made = s("gate_spread"), s("gate_made")
        self.rest_loaded = s("rest_loaded")
        self.rest_final, self.rows_turned = s("rest_final"), s("rows_turned")
        self.rows_kept, self.rows_stored = s("rows_kept"), s("rows_stored")

    def load(self, sp, first_weights):
        KD, D = self.c.KD, self.c.D
        sp.dma_start(self.brow[self.M * KD:, :], self.c_vec.rearrange("a (k p) -> (a k) p", p=P))\
            .then_inc(self.small_loaded, 16)
        sp.dma_start(self.brow[0:self.M * KD, :], self.b_ada.rearrange("a (r n) -> (a r) n", n=P))\
            .then_inc(self.small_loaded, 16)
        for k in range(KD):
            if k >= self.RING:
                sp.wait_ge(self.summed, k - self.RING + 1)
            sp.dma_start(self.ring[k % self.RING], self.w_ada[0, k * P:(k + 1) * P, 0:2 * D])\
                .then_inc(self.ring_loaded[k % self.RING], 16)
            if k < self.RING:
                for t in (2 * k, 2 * k + 1):
                    sp.dma_start(self.c.xres[:, t, :], self.x[0, t * P:(t + 1) * P, :])\
                        .then_inc(self.x_loaded[t], 16)
            if k == KD - 3:
                first_weights(0)
        first_weights(1)
        sp.dma_start(self.gate, self.b_ada[0, 2 * D:3 * D].partition_broadcast(P)).then_inc(self.bias_loaded, 16)
        for r in range(self.RING):
            sp.wait_ge(self.summed, KD - self.RING + r + 1 + (r == self.RING - 1))
            sp.dma_start(self.ring[r].rearrange("p (k d) -> p k d", k=2),
                         self.w_ada[0, 2 * r * P:(2 * r + 2) * P, 2 * D:3 * D].rearrange("(k p) d -> p k d", p=P))\
                .then_inc(self.ring_loaded[r], 16)

    def load_rest(self, sp, b):
        KD, D = self.c.KD, self.c.D
        for k in range(KD):
            sp.wait_ge(self.summed, b * KD + (self.LEAD + k))
            sp.dma_start(self.acc[:, self.COLS:2 * self.COLS],
                         self.w_ada[0, k * P:(k + 1) * P, bass.ds((b - 1) * self.COLS + 3 * D, self.COLS)])\
                .then_inc(self.rest_loaded, 16)

    def store_rows(self, sp):
        sp.wait_ge(self.rows_kept, 1)
        sp.dma_start(self.c.mod_rows[3 * self.c.D:].rearrange("(r n) -> r n", n=P), self.mrow[:, :])\
            .then_inc(self.rows_stored, 16)
        sp.wait_ge(self.rows_stored, 16)

    def pool_part(self, pool):
        c = self.c
        pool.memset(c.ident[:, :], 0.0).then_inc(self.ident_zero, 1)
        pool.wait_ge(self.ident_zero, 1)
        pool.affine_select(out=c.ident[:, :], in_=c.ident[:, :], compare_op=ALU.not_equal,
                           fill=1.0, base=0, pattern=[[-1, P]], channel_multiplier=1).then_inc(self.consts, 1)
        pool.memset(self.ones[:, :], 1.0).then_inc(self.consts, 1)
        pool.memset(self.halves[:, :], 0.5).then_inc(self.consts, 1)
        pool.memset(c.neg_half[:, :], -0.5).then_inc(self.consts, 1)
        pool.wait_ge(self.consts, 4)
        for t in range(c.NS):
            pool.wait_ge(self.squared, t + 1)
            pool.tensor_scalar(c.rms[:, 1, t:t + 1], c.rms[:, 0, t:t + 1], 1.0 / c.D, EPS,
                               ALU.mult, ALU.add).then_inc(self.mean_done, 1)
            pool.wait_ge(self.mean_done, t + 1)
            pool.tensor_tensor(c.rms[:, 2, t:t + 1], c.rms[:, 1, t:t + 1], c.neg_half[:, t:t + 1],
                               ALU.pow).then_inc(self.rms_done, 1)

    def _turned_dst(self, t, half):
        return self.c.x_turned[:, 4 * half:4 * half + 4, t * P:(t + 1) * P]

    def _turned_src(self, t, half):
        return self.c.bank[:, 4 + 2 * (t % 2) + half, :].rearrange("p (k s) -> p k s", k=4)

    def act_part(self, act):
        c, KD = self.c, self.c.KD
        act.wait_ge(self.b_turned, 1)
        act.activation(self.c_act[:, :], c.bank[:, 0, self.M * KD:(self.M + 1) * KD], ACT.Silu)\
            .then_inc(self.c_act_done, 1)
        for t in range(c.NS + 2):
            if t < c.NS:
                act.wait_ge(self.x_loaded[t], 16)
                if t:
                    act.wait_ge(self.squared, t)
                act.activation(self.junk, c.xres[:, t, :], ACT.Square,
                               accum_out=c.rms[:, 0, t:t + 1]).then_inc(self.squared, 1)
            if 1 <= t <= c.NS:
                act.wait_ge(self.rms_done, t)
                if t >= 3:
                    act.wait_ge(self.turned, 2 * (t - 3) + 2)
                act.activation(self.xn[(t - 1) % 2], c.xres[:, t - 1, :], ACT.Copy,
                               scale=c.rms[:, 2, t - 1:t]).then_inc(self.xn_done, 1)
            if t >= 2:
                act.wait_ge(self.turned, 2 * (t - 2) + 2)
                act.copy(self._turned_dst(t - 2, 1), self._turned_src(t - 2, 1)).then_inc(self.kept_high, 1)

    def pe_part(self, pe):
        c, KD = self.c, self.c.KD
        pe.wait_ge(self.consts, 4)
        pe.wait_ge(self.small_loaded, 32)
        pe.transpose(c.bank[:, 0, 0:(self.M + 1) * KD], self.brow[:, :],
                     c.ident[0:(self.M + 1) * KD, 0:(self.M + 1) * KD]).then_inc(self.b_turned, 1)
        for t in range(c.NS):
            pe.wait_ge(self.xn_done, t + 1)
            if t >= 2:
                pe.wait_ge(self.kept_low, t - 1)
                pe.wait_ge(self.kept_high, t - 1)
            for half in range(2):
                for k in range(4):
                    mm = pe.transpose(c.bank[:, 4 + 2 * (t % 2) + half, k * P:(k + 1) * P],
                                      self.xn[t % 2][:, (4 * half + k) * P:(4 * half + k + 1) * P], c.ident[:, :])
                mm.then_inc(self.turned, 1)
        for half in range(2):
            pe.wait_ge(self.summed, KD + half)
            for v in range(2):
                for k in range(half * KD // 2, (half + 1) * KD // 2):
                    r = v * KD + k
                    mm = pe.matmul(c.bank[:, 1 + half, r:r + 1], self.acc[:, r * P:(r + 1) * P], self.ones[:, :],
                                   start=True, stop=True)
            mm.then_inc(self.cols_ready, 1)

    def dve_lead(self, dve):
        c, KD, D = self.c, self.c.KD, self.c.D
        dve.wait_ge(self.c_act_done, 1)
        dve.wait_ge(self.b_turned, 1)
        dve.tensor_copy(self.bcol[:, :], c.bank[:, 0, 0:self.M * KD]).then_inc(self.b_kept, 1)
        tiles_after = {1: (0,), 2: (1,), 3: (2, 3), 4: (4, 5), 5: (6,), 6: (7,)}
        for k in range(KD):
            dve.wait_ge(self.ring_loaded[k % self.RING], 16 * (k // self.RING + 1))
            piece, c_k = self.ring[k % self.RING], self.c_act[:, k:k + 1]
            if k == 0:
                dve.tensor_scalar(self.acc, piece, c_k, None, ALU.mult).then_inc(self.summed, 1)
            elif k < KD - 1:
                dve.wait_ge(self.summed, k)
                dve.scalar_tensor_tensor(self.acc, piece, c_k, self.acc, ALU.mult, ALU.add)\
                    .then_inc(self.summed, 1)
            else:
                dve.wait_ge(self.summed, k)
                for half in range(2):
                    part, acc = [t.rearrange("p (v d) -> p v d", v=2)[:, :, half * D // 2:(half + 1) * D // 2]
                                 for t in (piece, self.acc)]
                    dve.scalar_tensor_tensor(acc, part, c_k, acc, ALU.mult, ALU.add).then_inc(self.summed, 1)
            for t in tiles_after.get(k, ()):
                dve.wait_ge(self.turned, 2 * t + 1)
                dve.tensor_copy(self._turned_dst(t, 0), self._turned_src(t, 0)).then_inc(self.kept_low, 1)
        dve.wait_ge(self.b_kept, 1)

    def dve_lead_cols(self, dve, half):
        c, KD = self.c, self.c.KD
        dve.wait_ge(self.cols_ready, half + 1)
        for v in range(2):
            at = slice(v * KD + half * KD // 2, v * KD + (half + 1) * KD // 2)
            dve.scalar_tensor_tensor(self.mcol[:, at], c.bank[:, 1 + half, at], float(v), self.bcol[:, at],
                                     ALU.add, ALU.add).then_inc(self.cols_kept, 1)
        dve.wait_ge(self.cols_kept, 2 * half + 2)

    def _piece(self, which, n):
        half, k = n // self.c.KD, n % self.c.KD
        return which[:, k, half * BANK:(half + 1) * BANK]

    def dve_h(self, dve):
        c, KD = self.c, self.c.KD
        dve.wait_ge(self.kept_high, c.NS)
        dve.wait_ge(self.kept_low, c.NS)
        for n in range(c.NH * KD + 1):
            if n in (0, KD // 2):
                self.dve_lead_cols(dve, n // (KD // 2))
            if n < c.NH * KD:
                x_n, k = self._piece(c.x_turned, n), n % KD
                dve.tensor_scalar(x_n, x_n, self.mcol[:, KD + k:KD + k + 1], self.mcol[:, k:k + 1],
                                  ALU.mult, ALU.add).then_inc(self.h_made, 1)
            if n:
                dve.wait_ge(self.h_hi_done, n)
                dve.wait_ge(self.h_made, n)
                dve.tensor_tensor(self._piece(c.h_lo, n - 1), self._piece(c.x_turned, n - 1),
                                  self._piece(c.h_hi, n - 1).bitcast(F32), ALU.subtract).then_inc(self.h_lo_done, 1)

    def act_h(self, act, pieces):
        c = self.c
        for n in pieces:
            act.wait_ge(self.h_made, n + 1)
            act.copy(self._piece(c.h_hi, n), self._piece(c.x_turned, n)).then_inc(self.h_hi_done, 1)

    def dve_gate(self, dve):
        KD, D = self.c.KD, self.c.D
        acc = self.acc[:, 0:D]
        for k in range(KD):
            dve.wait_ge(self.ring_loaded[k // 2], 48)
            piece, c_k = self.ring[k // 2][:, (k % 2) * D:(k % 2 + 1) * D], self.c_act[:, k:k + 1]
            if k == 0:
                dve.wait_ge(self.cols_ready, 2)
                dve.tensor_scalar(acc, piece, c_k, None, ALU.mult).then_inc(self.summed, 1)
            else:
                dve.wait_ge(self.summed, self.LEAD + k)
                dve.scalar_tensor_tensor(acc, piece, c_k, acc, ALU.mult, ALU.add).then_inc(self.summed, 1)

    def pe_gate(self, pe):
        pe.wait_ge(self.summed, self.LEAD + self.c.KD)
        for i in range(2):
            pe.matmul(self.c.bank[:, 4 + i, :], self.halves[:, :], self.acc[:, i * BANK:(i + 1) * BANK],
                      start=True, stop=True).then_inc(self.gate_spread, 1)

    def dve_gate_done(self, dve):
        dve.wait_ge(self.bias_loaded, 16)
        for i in range(2):
            half = self.gate[:, i * BANK:(i + 1) * BANK]
            dve.wait_ge(self.gate_spread, i + 1)
            dve.scalar_tensor_tensor(half, half, 0.5, self.c.bank[:, 4 + i, :], ALU.mult, ALU.add)\
                .then_inc(self.gate_made, 1)

    def dve_rest(self, dve, b, k):
        dve.wait_ge(self.rest_loaded, (b - 1) * (16 * self.c.KD) + 16 * (k + 1))
        acc, piece = self.acc[:, 0:self.COLS], self.acc[:, self.COLS:2 * self.COLS]
        c_k = self.c_act[:, k:k + 1]
        if k == 0:
            dve.wait_ge(self.cols_ready, b + 1)
            dve.tensor_scalar(acc, piece, c_k, None, ALU.mult).then_inc(self.summed, 1)
        else:
            dve.wait_ge(self.summed, b * self.c.KD + (self.LEAD + k))
            dve.scalar_tensor_tensor(acc, piece, c_k, acc, ALU.mult, ALU.add).then_inc(self.summed, 1)

    def pe_rest(self, pe, b):
        pe.wait_ge(self.summed, b * self.c.KD + (self.LEAD + self.c.KD))
        for r in range(self.TILES):
            mm = pe.matmul(self.c.bank[:, 4, r:r + 1], self.acc[:, r * P:(r + 1) * P], self.ones[:, :],
                           start=True, stop=True)
        mm.then_inc(self.cols_ready, 1)

    def dve_rest_kept(self, dve, b):
        at = bass.ds((b - 1) * self.TILES + 3 * self.c.KD, self.TILES)
        dve.wait_ge(self.cols_ready, b + 2)
        dve.tensor_tensor(self.mcol[:, at], self.c.bank[:, 4, 0:self.TILES], self.bcol[:, at], ALU.add)\
            .then_inc(self.cols_kept, 1)

    def dve_finish(self, dve, steps):
        KD = self.c.KD
        dve.wait_ge(self.cols_kept, steps + 4)
        for m in (4, 7):
            v = self.mcol[:, m * KD:(m + 1) * KD]
            dve.tensor_scalar(v, v, 1.0, None, ALU.add).then_inc(self.rest_final, 1)
        v = self.mcol[:, 8 * KD:9 * KD]
        dve.tensor_scalar(v, v, 0.5, None, ALU.mult).then_inc(self.rest_final, 1)

    def pe_finish(self, pe):
        pe.wait_ge(self.rest_final, 3)
        pe.transpose(self.c.bank[0:(self.M - 3) * self.c.KD, 4, 0:P], self.mcol[:, 3 * self.c.KD:], self.c.ident[:, :])\
            .then_inc(self.rows_turned, 1)

    def dve_rows(self, dve):
        dve.wait_ge(self.rows_turned, 1)
        dve.tensor_copy(self.mrow[:, :], self.c.bank[0:(self.M - 3) * self.c.KD, 4, 0:P]).then_inc(self.rows_kept, 1)


class FfnBuffers:
    TPS = 2

    def __init__(self, core, w_ada):
        KD, D, TPS = core.KD, core.D, self.TPS
        with ExitStack() as ctx:
            sb = lambda n, *a: core.sb(f"ffn_{n}", *a, ctx=ctx)
            self.in_hi = sb("in_hi", [P, TPS, KD, 2, P], F32R)
            self.in_lo = sb("in_lo", [P, TPS, KD, 2, P], F32R)
            self.raw_in = sb("raw_in", [P, TPS, KD, 2, P])
            self.raw_out = sb("raw_out", [P, TPS, D])
            with ExitStack() as early:
                self.ada_ring = core.sb("ada_ring", [P, Start.RING, 2 * D], ctx=early)
            self.out_hi = sb("out_hi", [P, TPS, D], F32R)
            self.out_lo = sb("out_lo", [P, TPS, D], F32R)
            self.act_hi = sb("act_hi", [P, TPS, core.S], F32R)
            self.act_lo = sb("act_lo", [P, TPS, core.S], F32R)
            self.silu_g = sb("silu_g", [P, 2, BANK])
            self.act_f = sb("act_f", [P, 2, BANK])
            self.gate = sb("gate", [P, D])
            self.shift_scale = sb("shift_scale", [P, 2 * D])
            M = w_ada.shape[2] // D
            self.c_act = sb("c_act", [P, KD])
            self.brow = sb("b_ada_rows", [(M + 1) * KD, P])
            self.bcol = sb("b_ada_cols", [P, M * KD])
            self.mcol = sb("mod_cols", [P, M * KD])
            self.mrow = sb("mod_row_tiles", [(M - 3) * KD, P])
            self.ones = sb("ada_ones", [P, 1])
            self.halves = sb("ada_halves", [P, P])


def flat_tile(t, j):
    return t[:, j].rearrange("p k g n -> p (k g n)")


class InWeights:

    def __init__(self, core, tag, buf, w_in):
        self.buf, self.TPS = buf, buf.TPS
        self.src = w_in.rearrange("a (k p) (g n) -> (a p) k g n", p=P, g=2)
        self.loaded = [core.kept_sem(f"{tag}_in_loaded{j}") for j in range(self.TPS)]
        self.hi_done, self.lo_done = core.kept_sem(f"{tag}_in_hi_done"), core.kept_sem(f"{tag}_in_lo_done")

    def load(self, sp, b, j):
        for g in range(2):
            sp.dma_start(self.buf.raw_in[:, j, :, g, :], self.src[:, :, g, bass.ts(b * self.TPS + j, P)])\
                .then_inc(self.loaded[j], 16)

    def cut_hi(self, act, b, j):
        act.copy(flat_tile(self.buf.in_hi, j), flat_tile(self.buf.raw_in, j)).then_inc(self.hi_done, 1)

    def cut_lo(self, pool, b, j):
        pool.tensor_tensor(flat_tile(self.buf.in_lo, j), flat_tile(self.buf.raw_in, j),
                           flat_tile(self.buf.in_hi, j).bitcast(F32), ALU.subtract).then_inc(self.lo_done, 1)


def ffn(core, tag, buf, weights, w_out, gate_row=None, next_mod=None, g_final=None, out=None, start_in=None,
        after=None):
    nc, KD, D, F, NS = core.nc, core.KD, core.D, w_out.shape[1], core.NS
    TPS = buf.TPS
    STEPS = F // (TPS * P)
    NG = 2 * NS
    src_out = w_out.rearrange("a f d -> (a f) d")
    raw_in, in_hi, in_lo, raw_out, out_hi, out_lo = (buf.raw_in, buf.in_hi, buf.in_lo, buf.raw_out, buf.out_hi,
                                                     buf.out_lo)
    act_hi, act_lo, silu_g, act_f, gate = buf.act_hi, buf.act_lo, buf.silu_g, buf.act_f, buf.gate
    shift, scale1 = buf.shift_scale[:, 0:D], buf.shift_scale[:, D:2 * D]
    in_loaded, in_hi_done, in_lo_done = weights.loaded, weights.hi_done, weights.lo_done
    s = lambda n: core.sem(f"{tag}_{n}")
    out_loaded = [s(f"out_loaded{j}") for j in range(TPS)]
    gate_loaded = s("gate_loaded")
    out_gated, out_hi_done, out_lo_done = s("out_gated"), s("out_hi_done"), s("out_lo_done")
    g_ready, u_ready = s("g_ready"), s("u_ready")
    silu_done, mult_done = s("silu_done"), s("mult_done")
    act_hi_done, act_lo_done = s("act_hi_done"), s("act_lo_done")
    y_ready, y_added = s("y_ready"), s("y_added")
    xn = [flat_tile(raw_in, j)[:, i * D:(i + 1) * D] for i in range(2) for j in range(TPS)]
    norm = Norm(core, tag + "n", shift, scale1, raw_out[:, 0, :], xn, 0)
    stored = s("stored")
    LOOP = STEPS - 3
    start = Start(core, *start_in, LOOP, buf) if start_in else None

    def steps(eng, body):
        body(0, True, False)
        with eng.Fori(1, LOOP + 1) as b:
            body(b, False, False)
        body(STEPS - 2, False, False)
        body(STEPS - 1, False, True)

    with nc.Block() as block:

        @block.sync
        def _(sp):
            def load_in(b, first):
                for j in range(TPS):
                    if not first:
                        sp.wait_ge(in_lo_done, b * TPS + (j - TPS + 1))
                    weights.load(sp, b, j)

            def load_out(b, first):
                for j in range(TPS):
                    if not first:
                        sp.wait_ge(out_lo_done, b * TPS + (j - TPS + 1))
                    sp.dma_start(raw_out[:, j, :], src_out[bass.ts(b * TPS + j, P), :])\
                        .then_inc(out_loaded[j], 16)

            def load(b):
                load_in(b, False)
                load_out(b, False)

            if start:
                start.load(sp, lambda j: weights.load(sp, 0, j))
                sp.wait_ge(start.turned, 2 * NS)
            else:
                sp.dma_start(gate[:, :], core.mod(gate_row)).then_inc(gate_loaded, 16)
            load_out(0, True)
            load(1)
            if start:
                sp.wait_ge(start.gate_made, 2)
            with sp.Fori(1, LOOP + 1) as b:
                load(b + 1)
                if start:
                    start.load_rest(sp, b)
            load(STEPS - 1)
            if start:
                start.store_rows(sp)
            if next_mod is not None:
                norm.load(sp, next_mod)
                sp.wait_ge(u_ready, STEPS * 4)
                after.load(sp)
            else:
                sp.dma_start(scale1, g_final.partition_broadcast(P)).then_inc(norm.loaded, 16)
                for t in range(NS):
                    sp.wait_ge(norm.scaled, t + 1)
                    sp.dma_start(out[0, t * P:(t + 1) * P, :], core.xres[:, t, :]).then_inc(stored, 16)
                sp.wait_ge(stored, 16 * NS)

        @block.gpsimd
        def _(pool):
            def cut_in(b, first):
                for j in range(TPS):
                    pool.wait_ge(in_hi_done, b * TPS + (j + 1))
                    if not first:
                        pool.wait_ge(u_ready, b * 4 + (j - 1))
                    weights.cut_lo(pool, b, j)

            def cut_out(b, first, last):
                for j in range(TPS):
                    pool.wait_ge(out_loaded[j], b * 16 + 16)
                    pool.tensor_tensor(raw_out[:, j, :], raw_out[:, j, :], gate[:, :], ALU.mult)\
                        .then_inc(out_gated, 1)
                for j in range(TPS):
                    pool.wait_ge(out_hi_done, b * TPS + (j + 1))
                    if not first:
                        pool.wait_ge(y_ready, b * NG)
                    pool.tensor_tensor(out_lo[:, j, :], raw_out[:, j, :], out_hi[:, j, :].bitcast(F32),
                                       ALU.subtract).then_inc(out_lo_done, 1)

            def body(b, first, last):
                cut_out(b, first, last)
                if not last:
                    cut_in(b + 1, False)

            if start:
                start.pool_part(pool)
                cut_in(0, True)
                pool.wait_ge(start.gate_made, 2)
            else:
                pool.wait_ge(gate_loaded, 16)
            steps(pool, body)
            for t in range(NS + 1):
                if t < NS:
                    norm.inverse(pool, t)
                if t >= 1 and next_mod is not None:
                    norm.add_shift(pool, t - 1)

        @block.scalar
        def _(act):
            def cut_in(b, first):
                for j in range(TPS):
                    act.wait_ge(in_loaded[j], b * 32 + 32)
                    if not first:
                        act.wait_ge(u_ready, b * 4 + (j - 1))
                    weights.cut_hi(act, b, j)

            def silu(b, q):
                act.wait_ge(g_ready, b * 4 + (q + 1))
                if not (isinstance(b, int) and b * 4 + q < 2):
                    act.wait_ge(mult_done, b * 4 + (q - 1))
                act.activation(silu_g[:, q % 2, :], core.bank[:, 2 * (q % 2), :], ACT.Silu)\
                    .then_inc(silu_done, 1)

            def hidden_hi(b, q, first):
                h, j = q // 2, q % 2
                act.wait_ge(mult_done, b * 4 + (q + 1))
                if not first:
                    act.wait_ge(y_ready, b * NG + (h - 1) * (NG // 2))
                act.copy(act_hi[:, j, h * BANK:(h + 1) * BANK], act_f[:, q % 2, :]).then_inc(act_hi_done, 1)

            def cut_out(b, first):
                for j in range(TPS):
                    act.wait_ge(out_gated, b * TPS + (j + 1))
                    if not first:
                        act.wait_ge(y_ready, b * NG)
                    act.copy(out_hi[:, j, :], raw_out[:, j, :]).then_inc(out_hi_done, 1)

            def body(b, first, last):
                if not first:
                    cut_out(b, first)
                for q in range(5):
                    if q < 4:
                        silu(b, q)
                    if q >= 1:
                        hidden_hi(b, q - 1, first)
                    if first and q == 2:
                        cut_out(b, first)
                if not last:
                    cut_in(b + 1, False)

            if start:
                start.act_part(act)
                act.wait_ge(in_loaded[0], 32)
                weights.cut_hi(act, 0, 0)
                start.act_h(act, range(0, core.KD // 2))
                act.wait_ge(in_loaded[1], 32)
                weights.cut_hi(act, 0, 1)
                start.act_h(act, range(core.KD // 2, core.NH * KD))
            steps(act, body)
            for t in range(NS + 2):
                if t < NS:
                    act.wait_ge(y_added, (STEPS - 1) * NG + 2 * t + 2)
                    if t == 0:
                        act.wait_ge(out_lo_done, STEPS * TPS)
                    norm.square(act, t)
                if t >= 2 and next_mod is not None:
                    norm.keep_hi(act, t - 2)
                if t == NS - 1 and next_mod is not None:
                    after.cut_hi(act)

        @block.vector
        def _(dve):
            def hidden(b, q):
                h, j = q // 2, q % 2
                dve.wait_ge(silu_done, b * 4 + (q + 1))
                dve.wait_ge(u_ready, b * 4 + (q + 1))
                if not (isinstance(b, int) and b * 4 + q < 2):
                    dve.wait_ge(act_lo_done, b * 4 + (q - 1))
                dve.tensor_tensor(act_f[:, q % 2, :], core.bank[:, 2 * (q % 2) + 1, :], silu_g[:, q % 2, :],
                                  ALU.mult).then_inc(mult_done, 1)
                dve.wait_ge(act_hi_done, b * 4 + (q + 1))
                half = slice(h * BANK, (h + 1) * BANK)
                dve.tensor_tensor(act_lo[:, j, half], act_f[:, q % 2, :], act_hi[:, j, half].bitcast(F32),
                                  ALU.subtract).then_inc(act_lo_done, 1)

            def add(b, g):
                part = core.xres[:, g // 2, (g % 2) * BANK:(g % 2 + 1) * BANK]
                dve.wait_ge(y_ready, b * NG + (g + 1))
                dve.tensor_tensor(part, core.bank[:, 4 + g % 4, :], part, ALU.add).then_inc(y_added, 1)

            def body(b, first, last):
                in_loop = start and not isinstance(b, int)
                if start and first:
                    start.dve_lead(dve)
                    start.dve_h(dve)
                    start.dve_gate(dve)
                if start and isinstance(b, int) and b == STEPS - 2:
                    start.dve_finish(dve, LOOP)
                for q in range(4):
                    hidden(b, q)
                    if in_loop:
                        start.dve_rest(dve, b, q)
                    if start and first and q == 0:
                        start.dve_gate_done(dve)
                    if start and isinstance(b, int) and b == STEPS - 2 and q == 2:
                        start.dve_rows(dve)
                if not last:
                    for g in range(NG):
                        add(b, g)
                        if in_loop and g % 4 == 2:
                            start.dve_rest(dve, b, 4 + g // 4)
                    if in_loop:
                        start.dve_rest_kept(dve, b)

            steps(dve, body)
            for t in range(NS + 4):
                if t < NS:
                    add(STEPS - 1, 2 * t)
                    add(STEPS - 1, 2 * t + 1)
                if 2 <= t < NS + 2:
                    if next_mod is not None:
                        if t == 2:
                            dve.wait_ge(in_lo_done, STEPS * TPS)
                        norm.scale(dve, t - 2)
                    else:
                        if t == 2:
                            dve.wait_ge(norm.loaded, 16)
                        dve.wait_ge(norm.rms_done, t - 1)
                        dve.scalar_tensor_tensor(core.xres[:, t - 2, :], core.xres[:, t - 2, :],
                                                 core.rms[:, 2, t - 2:t - 1], scale1[:, :],
                                                 ALU.mult, ALU.mult).then_inc(norm.scaled, 1)
                if 4 <= t and next_mod is not None:
                    norm.keep_lo(dve, t - 4)

        @block.tensor
        def _(pe):
            def quarter(b, q):
                h, j = q // 2, q % 2
                half = slice(h * BANK, (h + 1) * BANK)
                if h == 0:
                    pe.wait_ge(in_lo_done, b * TPS + (j + 1))
                for g in range(2):
                    if not (isinstance(b, int) and b * 4 + q < 2):
                        pe.wait_ge(silu_done if g == 0 else mult_done, b * 4 + (q - 1))
                    dst = core.bank[:, 2 * (q % 2) + g, :]
                    for k in range(KD):
                        if start and isinstance(b, int) and b == 0 and j == 0 and g == 0:
                            pe.wait_ge(start.h_lo_done, h * KD + k + 1)
                        w_hi, w_lo = in_hi[:, j, k, g, :], in_lo[:, j, k, g, :]
                        pe.matmul(dst, w_hi, core.h_hi[:, k, half], start=(k == 0), stop=False)
                        pe.matmul(dst, w_hi, core.h_lo[:, k, half], start=False, stop=False)
                        mm = pe.matmul(dst, w_lo, core.h_hi[:, k, half], start=False, stop=(k == KD - 1))
                    mm.then_inc(u_ready if g else g_ready, 1)
                    if start and isinstance(b, int) and b == 0 and q == 2 and g == 0:
                        start.pe_gate(pe)

            def group(b, g):
                t, dh = g // 2, g % 2
                tok, cols = slice(t * P, (t + 1) * P), slice(dh * BANK, (dh + 1) * BANK)
                if g == 0:
                    pe.wait_ge(out_lo_done, b * TPS + TPS)
                if g in (0, NG // 2):
                    pe.wait_ge(act_lo_done, b * 4 + (2 if g == 0 else 4))
                if not (isinstance(b, int) and b == 0 and g < 4):
                    pe.wait_ge(y_added, b * NG + (g - 3))
                if start and g == 0:
                    if isinstance(b, int) and b == 0:
                        pe.wait_ge(start.gate_made, 2)
                    elif isinstance(b, int) and b == STEPS - 2:
                        pe.wait_ge(start.rows_kept, 1)
                    elif not isinstance(b, int):
                        pe.wait_ge(start.cols_kept, b + 3)
                dst = core.bank[:, 4 + g % 4, :]
                for j in range(TPS):
                    a_hi, a_lo = act_hi[:, j, tok], act_lo[:, j, tok]
                    pe.matmul(dst, a_hi, out_hi[:, j, cols], start=(j == 0), stop=False)
                    pe.matmul(dst, a_hi, out_lo[:, j, cols], start=False, stop=False)
                    mm = pe.matmul(dst, a_lo, out_hi[:, j, cols], start=False, stop=(j == TPS - 1))
                mm.then_inc(y_ready, 1)

            def body(b, first, last):
                for q in range(4):
                    quarter(b, q)
                    if start and isinstance(b, int) and b == STEPS - 2 and q == 2:
                        pe.wait_ge(y_added, b * NG)
                        start.pe_finish(pe)
                for g in range(NG):
                    group(b, g)
                    if last and next_mod is not None and g % 2 and g >= 9:
                        norm.turn(pe, (g - 9) // 2)
                if start and not isinstance(b, int):
                    pe.wait_ge(y_added, b * NG + (NG - 3))
                    start.pe_rest(pe, b)

            if start:
                start.pe_part(pe)
            steps(pe, body)
            if next_mod is not None:
                for t in range(4, NS):
                    norm.turn(pe, t)


class Chain:

    def __init__(self, eng, sem):
        self.eng, self.sem, self.base, self.done, self.per = eng, sem, 0, 0, 0

    def at(self, i):
        if isinstance(i, int) and i == 0:
            self.start, self.per = self.done, 0
        elif self.per == 0:
            self.per = self.done - self.start
        if not (isinstance(i, int) and i == 0):
            self.base, self.done = i * self.per, self.start

    def leave(self, n):
        self.base, self.done = 0, self.start + n * self.per

    def __call__(self, ins):
        ins.then_inc(self.sem, 1)
        self.done += 1
        self.eng.wait_ge(self.sem, self.base + self.done)


class MixerStart:

    def __init__(self, core, w_mix_in, b_fox_f, b_m_i, b_m_f, w_conv, b_conv, g_mhn):
        KD = core.KD
        FH, MH, TAPS = b_fox_f.shape[1], b_m_i.shape[1], w_conv.shape[1]
        NG = FH + 2 * MH
        self.core, self.biases, self.w_conv, self.b_conv, self.g_mhn = (core, (b_fox_f, b_m_i, b_m_f), w_conv,
                                                                        b_conv, g_mhn)
        self.w_in = w_mix_in.rearrange("a (k p) n -> (a p) k n", p=P)
        self.NG, self.FH, self.MH, self.TAPS, self.FW = NG, FH, MH, TAPS, core.D // 2
        sb = lambda n, *a: core.sb(f"mx_{n}", *a, ctx=self.ctx)
        self.ctx = ExitStack()
        self.raw_w = sb("raw_w", [P, 2, KD * P])
        self.w_hi = sb("w_hi", [P, 2, KD * P], F32R)
        self.w_lo = sb("w_lo", [P, 2, KD * P], F32R)
        self.gw_raw = sb("gw_raw", [P, KD, NG])
        self.gw = sb("gw", [P, KD, 2, NG], F32R)
        self.gbias = sb("gbias", [P, NG])
        self.const_rows = sb("const_rows", [(TAPS + 1) * 2 * MH + MH, P])
        s = lambda n: core.kept_sem(f"mx_{n}")
        self.w_loaded = [s("w_loaded0"), s("w_loaded1")]
        self.w_hi_done = [s("w_hi_done0"), s("w_hi_done1")]
        self.w_lo_done = [s("w_lo_done0"), s("w_lo_done1")]
        self.w_used = [s("w_used0"), s("w_used1")]
        self.small_loaded, self.gw_hi_done = s("small_loaded"), s("gw_hi_done")

    def close(self):
        self.ctx.close()

    def w_load(self, sp, slot, c, src):
        if not (isinstance(c, int) and c == 0):
            sp.wait_ge(self.w_lo_done[slot], c)
        dst = self.raw_w[:, slot, :].rearrange("p (k n) -> p k n", n=src.shape[2])
        sp.dma_start(dst, src).then_inc(self.w_loaded[slot], 16)

    def w_cut_hi(self, act, slot, c, freed=None, is_gated=None, dst=None):
        if is_gated is None:
            act.wait_ge(self.w_loaded[slot], c * 16 + 16)
        else:
            act.wait_ge(*is_gated)
        if freed is not None:
            act.wait_ge(*freed)
        dst = self.w_hi[:, slot, :] if dst is None else dst
        act.copy(dst, self.raw_w[:, slot, :]).then_inc(self.w_hi_done[slot], 1)

    def load(self, sp):
        FH, MH, NG, TAPS, FW, w_in = self.FH, self.MH, self.NG, self.TAPS, self.FW, self.w_in
        COL_F = 3 * FW
        COL_MG = COL_F + FH + 4 * (self.core.D - FW)
        with self.core.nc.allow_non_contiguous_dma(reason="16 gate columns"):
            sp.dma_start(self.gw_raw[:, :, 0:FH], w_in[:, :, COL_F:COL_F + FH]).then_inc(self.small_loaded, 16)
            sp.dma_start(self.gw_raw[:, :, FH:NG], w_in[:, :, COL_MG:COL_MG + 2 * MH]).then_inc(self.small_loaded, 16)
        for lo, hi, src in zip((0, FH, FH + MH), (FH, FH + MH, NG), self.biases):
            sp.dma_start(self.gbias[:, lo:hi], src.rearrange("a n -> (a n)").partition_broadcast(P))\
                .then_inc(self.small_loaded, 16)
        R0, R1 = TAPS * 2 * MH, (TAPS + 1) * 2 * MH
        for lo, hi, src in ((0, R0, self.w_conv.rearrange("a w (c p) -> (a w c) p", p=P)),
                            (R0, R1, self.b_conv.rearrange("a (c p) -> (a c) p", p=P)),
                            (R1, R1 + MH, self.g_mhn.rearrange("a (c p) -> (a c) p", p=P))):
            sp.dma_start(self.const_rows[lo:hi, :], src).then_inc(self.small_loaded, 16)
        for piece in range(2):
            self.w_load(sp, piece, 0, w_in[:, 2 * piece:2 * piece + 2, 2 * FW:3 * FW])

    def cut_hi(self, act):
        act.wait_ge(self.small_loaded, 16 * 8)
        act.copy(self.gw[:, :, 0, :], self.gw_raw[:, :, :]).then_inc(self.gw_hi_done, 1)
        self.w_cut_hi(act, 0, 0)
        self.w_cut_hi(act, 1, 0)


def mixer(core, ms, ffn_weights, w_mix_in, b_fox_f, b_m_i, b_m_f, w_conv, b_conv, g_mhn, w_mix_out,
          gate_row, next_mod):
    nc, KD, D, S, NS = core.nc, core.KD, core.D, core.S, core.NS
    FH, MH = b_fox_f.shape[1], b_m_i.shape[1]
    FW = D // 2
    HD = FW // FH
    MW = D - FW
    PAIRS = FH // 2
    TAPS = w_conv.shape[1]
    COL_Q, COL_K, COL_V, COL_F = 0, FW, 2 * FW, 3 * FW
    COL_MQ = COL_F + FH
    COL_MK, COL_MV, COL_MO, COL_MG = COL_MQ + MW, COL_MQ + 2 * MW, COL_MQ + 3 * MW, COL_MQ + 4 * MW
    NG = FH + 2 * MH
    NR = FH + MH
    V1 = P + 1
    K_SCALE = float(P) ** -0.5
    w_in = w_mix_in.rearrange("a (k p) n -> (a p) k n", p=P)
    w_out = w_mix_out.rearrange("a (k p) n -> (a p) k n", p=P)
    gate_rows = nc.dram_tensor("gate_rows", (NR * S,), F32, kind="Internal").ap()

    raw_w, w_hi, w_lo, gw_raw, gw = ms.raw_w, ms.w_hi, ms.w_lo, ms.gw_raw, ms.gw
    gbias, const_rows = ms.gbias, ms.const_rows
    w_loaded, w_hi_done, w_lo_done, w_used = ms.w_loaded, ms.w_hi_done, ms.w_lo_done, ms.w_used
    small_loaded, gw_hi_done = ms.small_loaded, ms.gw_hi_done
    w_load, w_cut_hi = ms.w_load, ms.w_cut_hi
    sb = lambda n, *a: core.sb(f"mx_{n}", *a, ctx=ms.ctx)
    NCONST = (TAPS + 1) * 2 * MH + MH
    consts = sb("consts", [P, NCONST])
    mask_m = sb("mask_m", [P, P])
    m_total = sb("m_total", [P, MH, NS])
    m_cum = sb("m_cum", [P, MH, NS])
    m_b = sb("m_b", [P, MH, NS])
    yT_fox = sb("yT_fox", [P, PAIRS, S])

    s = lambda n: core.sem(f"mx_{n}")
    pool_set = s("pool_set")
    gw_cut = s("gw_cut")
    zrow_ready, zrow_kept = s("zrow_ready"), s("zrow_kept")
    z_ready, z_done = s("z_ready"), s("z_done")
    neg_done, exp_done, ln_done = s("neg_done"), s("exp_done"), s("ln_done")
    logf_done = s("logf_done")
    sums_ready, rows_ready = s("sums_ready"), s("rows_ready")
    rows_turned, rows_kept, rows_stored = s("rows_turned"), s("rows_kept"), s("rows_stored")
    const_turned, const_kept = s("const_turned"), s("const_kept")
    dve_step, act_step, pool_step = s("dve_step"), s("act_step"), s("pool_step")
    v_ready, v_kept_even, v_kept_odd = s("v_ready"), s("v_kept_even"), s("v_kept_odd")
    fq_ready, fq_kept, fq_cut = s("fq_ready"), s("fq_kept"), s("fq_cut")
    cum_loaded = s("cum_loaded")
    score_ready, logit_done, prob_done = s("score_ready"), s("logit_done"), s("prob_done")
    pt_ready, pt_act, pt_dve = s("pt_ready"), s("pt_act"), s("pt_dve")
    pv_ready, y_done = s("pv_ready"), s("y_done")
    yt_ready, yt_kept = s("yt_ready"), s("yt_kept")
    x_ready, x_kept = s("x_ready"), s("x_kept")
    b_loaded = s("b_loaded")
    max_done, args_done, weights_done = s("max_done"), s("args_done"), s("weights_done")
    conv_done, silu_done = s("conv_done"), s("silu_done")
    sig_done, sg_done = s("sig_done"), s("sg_done")
    kt_ready, kw_done = s("kt_ready"), s("kw_done")
    qk_ready, sp_done = s("qk_ready"), s("sp_done")
    u_ready, state_done = s("u_ready"), s("state_done")
    spt_ready, spt_kept = s("spt_ready"), s("spt_kept")
    num_ready, inter_kept, o_done = s("num_ready"), s("inter_kept"), s("o_done")
    sq_done, var_done, rpow_done = s("sq_done"), s("var_done"), s("rpow_done")
    yb_done, ybt_ready, ybt_kept = s("yb_done"), s("ybt_ready"), s("ybt_kept")
    gate_loaded, gated = s("gate_loaded"), [s("gated_pool"), s("gated_dve")]
    y_hi, y_lo_pool, y_lo = s("y_hi"), s("y_lo_pool"), s("y_lo")
    out_ready, out_added = s("out_ready"), s("out_added")

    fox = ExitStack()
    fsb = lambda n, *a: core.sb(f"mx_{n}", *a, ctx=fox)
    mask_f = fsb("mask_f", [P, P], BF16)
    ident_b = fsb("ident_b", [P, P], BF16)
    v_fox = fsb("v_fox", [P, NS, FW])
    fq_hi, fq_lo = fsb("fq_hi", [P, S], F32R), fsb("fq_lo", [P, S], F32R)
    fk_hi, fk_lo = fsb("fk_hi", [P, S], F32R), fsb("fk_lo", [P, S], F32R)
    cum_bc = fsb("cum_bc", [P, 2, S])
    RP = 3
    prob = fsb("prob", [P, RP, S])
    probT = fsb("probT", [P, 2, S])
    early = ExitStack()
    esb = lambda n, *a: core.sb(f"mx_{n}", *a, ctx=early)
    z = esb("z", [P, NS, NG])
    zneg = esb("zneg", [P, NS, NG])
    logf = esb("logf", [P, NS, NG])
    cum_in = esb("cum_in", [P, NS, NG])
    total = esb("total", [P, NS, NG])
    before = esb("before", [P, NS, FH])
    rows_in = esb("rows_in", [P, NR, NS])
    rows_out = esb("rows_out", [NR * NS, P])
    upper = esb("upper", [P, P])
    ones = esb("ones", [P, P])
    early.close()
    zrows = prob[:, 0, :]
    y_tok = fsb("y_tok", [P, NS, 2 * HD])
    low = fsb("low", [P, 4 * NS])
    rowsum = fsb("rowsum", [P, 2 * NS])
    rinv = fsb("rinv", [P, 2 * NS])
    wait_tile = fsb("wait_tile", [P, 2 * NS])
    fox.close()
    late = ExitStack()
    yT_ml = core.sb("mx_yT_ml", [P, MH, S], ctx=late)
    mo = core.sb("mx_mo", [P, S], ctx=late)
    ml = ExitStack()
    msb = lambda n, *a: core.sb(f"mx_{n}", *a, ctx=ml)
    v_ml = msb("v_ml", [P, NS, MH, V1])
    pre_q = msb("pre_q", [P, TAPS - 1 + S])
    pre_k = msb("pre_k", [P, TAPS - 1 + S])
    sg = msb("sg", [P, S])
    mqT = msb("mqT", [P, S])
    mkT = msb("mkT", [P, NS * V1])
    kw = msb("kw", [P, NS * V1])
    dec = msb("dec", [P, S])
    arg = msb("arg", [P, 4, NS])
    mst = msb("mst", [P, NS + 1])
    tiny = msb("tiny", [P, 8, NS])
    sq_junk = msb("sq_junk", [P, P])
    ml.close()
    fin = ExitStack()
    out_w_hi = core.sb("mx_out_w_hi", [P, KD, BANK], F32R, ctx=fin)
    out_w_lo = core.sb("mx_out_w_lo", [P, KD, BANK], F32R, ctx=fin)
    shift, scale1 = core.sb("mx_shift", [P, D], ctx=fin), core.sb("mx_scale1", [P, D], ctx=fin)
    junk = core.sb("mx_junk", [P, D], ctx=fin)
    fin.close()
    late.close()
    over = ExitStack()
    RX = 3
    pad = core.sb("mx_pad", [P, MH * S - RX * D], ctx=over)
    xn3 = core.sb("mx_xn", [P, RX, D], ctx=over)
    over.close()
    gate = mo
    states = mkT[:, :].rearrange("p (c v) -> p c v", v=V1)
    o_all = kw[:, :].rearrange("p (c v) -> p c v", v=V1)
    kw_c = kw[:, 0:S]
    norm = Norm(core, "mxn", shift[:, :], scale1[:, :], junk[:, :], [xn3[:, i, :] for i in range(RX)], 4)

    C_V = (0, 0)
    C_F = (2, 2)
    C_MV = (2 + PAIRS, 2 + PAIRS)
    C_M = (4 + PAIRS, 4 + PAIRS)
    C_O = (C_M[0] + MH, C_M[1] + 2 * MH)
    X_PER = 6

    def w_cut_lo(pool, slot, c, hi=None, lo=None):
        hi, lo = (w_hi[:, slot, :], w_lo[:, slot, :]) if hi is None else (hi, lo)
        pool.wait_ge(w_hi_done[slot], c + 1)
        pool.tensor_tensor(lo, raw_w[:, slot, :], hi.bitcast(F32), ALU.subtract).then_inc(w_lo_done[slot], 1)

    def out_w(n):
        pieces = slice(2 * (n - 4), 2 * (n - 4) + 2)
        return [t[:, pieces, :].rearrange("p k n -> p (k n)") for t in (out_w_hi, out_w_lo)]

    def cut_y_lo(eng, k, done):
        src = yT_fox[:, k, :] if k < PAIRS else yT_ml[:, k - PAIRS, :]
        eng.tensor_tensor(core.h_lo[:, k, :], src, core.h_hi[:, k, :].bitcast(F32), ALU.subtract)\
            .then_inc(done, 1)

    def gate_out(eng, n):
        slot, c, dh = n % 2, C_O[n % 2] + n // 2, n // 4
        eng.wait_ge(w_loaded[slot], 16 * (c + 1))
        piece = raw_w[:, slot, :].rearrange("p (k n) -> p k n", k=2)
        cols = gate[:, dh * BANK:(dh + 1) * BANK]
        eng.tensor_tensor(piece, piece, cols.unsqueeze(1).to_broadcast([P, 2, BANK]), ALU.mult)\
            .then_inc(gated[n >= 2], 1)

    def three(pe, dst, a_hi, a_lo, b_hi, b_lo, start, stop):
        pe.matmul(dst, a_hi, b_hi, start=start, stop=False)
        pe.matmul(dst, a_hi, b_lo, start=False, stop=False)
        return pe.matmul(dst, a_lo, b_hi, start=False, stop=stop)

    def token_product(pe, k, t):
        slot, cols = k // 2 % 2, slice(k % 2 * BANK, (k % 2 + 1) * BANK)
        tok = slice(t * P, (t + 1) * P)
        return three(pe, core.bank[:, t, :], core.h_hi[:, k, tok], core.h_lo[:, k, tok],
                     w_hi[:, slot, cols], w_lo[:, slot, cols], k == 0, k == KD - 1)

    def by_token(pe, c, ready, before, done_already=lambda k, t: False):
        for k in range(KD):
            slot = k // 2 % 2
            if k % 2 == 0:
                pe.wait_ge(w_lo_done[slot], c[slot] + k // 4 + 1)
            for t in range(NS):
                if done_already(k, t):
                    continue
                before(k, t)
                mm = token_product(pe, k, t)
                if k == KD - 1:
                    mm.then_inc(ready, 1)
            if k % 2 and k < KD - 1:
                mm.then_inc(w_used[slot], 1)

    def by_feature(pe, dst, slot, half):
        tok = slice(half * BANK, (half + 1) * BANK)
        for k in range(KD):
            cols = slice(k * P, (k + 1) * P)
            mm = three(pe, dst, w_hi[:, slot, cols], w_lo[:, slot, cols],
                       core.h_hi[:, k, tok], core.h_lo[:, k, tok], k == 0, k == KD - 1)
        return mm

    def repeat(eng, n, body):
        body(0, True, False)
        with eng.Fori(1, n - 1) as i:
            body(i, False, False)
        body(n - 1, False, True)

    PER = 2 * NS
    HEAD = [n % 2 for n in range(PER)]
    UP = [(n // 2 + NS // 2 - 1) % NS for n in range(PER)]
    BLOCK = [(UP[n], NS - 1 - UP[n])[n % 2] for n in range(PER)]
    LONG = [sum((BLOCK[m] + 1) * P > BANK for m in range(n + 1)) for n in range(PER)]

    with nc.Block() as block:

        @block.sync
        def _(sp):
            for piece in range(2, 4):
                w_load(sp, piece % 2, C_V[0] + piece // 2, w_in[:, 2 * piece:2 * piece + 2, COL_V:COL_V + FW])
            for slot, col in ((0, COL_Q), (1, COL_K)):
                w_load(sp, slot, C_F[slot], w_in[:, :, col:col + P])
            sp.wait_ge(rows_kept, 1)
            sp.dma_start(gate_rows.rearrange("(r n) -> r n", n=P), rows_out[:, :]).then_inc(rows_stored, 16)
            sp.wait_ge(rows_stored, 16)

            def fox_loads(p, first, last):
                if not first:
                    sp.wait_ge(logit_done, p * PER)
                sp.dma_start(cum_bc[:, :, :], gate_rows[bass.ds(p * (2 * S), 2 * S)]
                             .rearrange("(e s) -> e s", e=2).partition_broadcast(P)).then_inc(cum_loaded, 16)
                if not last:
                    for slot, col in ((0, COL_Q), (1, COL_K)):
                        w_load(sp, slot, p + (C_F[slot] + 1), w_in[:, :, bass.ds(p * P + (col + P), P)])

            repeat(sp, PAIRS, fox_loads)
            for piece in range(4):
                w_load(sp, piece % 2, C_MV[0] + piece // 2, w_in[:, 2 * piece:2 * piece + 2, COL_MV:COL_MV + MW])

            def ml_w(h, c, col):
                w_load(sp, min(c, 1), h + C_M[0] if c == 0 else h * 2 + (C_M[1] + c - 1),
                       w_in[:, :, bass.ds(h * P + col, P)])

            def ml_loads(h, first, last):
                if not last:
                    ml_w(h + 1, 0, COL_MK)
                if first:
                    sp.wait_ge(yt_kept, 2 * PAIRS)
                    sp.wait_ge(y_done, PAIRS * PER)
                else:
                    sp.wait_ge(num_ready, h * 3)
                sp.dma_start(dec[:, :], gate_rows[bass.ds(h * S + FH * S, S)].partition_broadcast(P))\
                    .then_inc(b_loaded, 16)
                if not last:
                    ml_w(h + 1, 1, COL_MQ)
                    ml_w(h + 1, 2, COL_MO)

            for c, col in ((0, COL_MK), (1, COL_MQ), (2, COL_MO)):
                ml_w(0, c, col)
            repeat(sp, MH, ml_loads)
            sp.wait_ge(sig_done, MH)
            sp.dma_start(gate[:, :], core.mod(gate_row)).then_inc(gate_loaded, 16)
            for n in range(8):
                dh, piece = n // 4, n % 4
                w_load(sp, n % 2, C_O[n % 2] + n // 2,
                       w_out[:, 2 * piece:2 * piece + 2, dh * BANK:(dh + 1) * BANK])
            sp.wait_ge(ybt_kept, 2 * MH)
            norm.load(sp, next_mod)
            sp.wait_ge(y_lo_pool, 2)
            sp.wait_ge(y_lo, KD - 2)
            for j in range(ffn_weights.TPS):
                ffn_weights.load(sp, 0, j)

        @block.gpsimd
        def _(pool):
            link = Chain(pool, pool_step)
            pool.wait_ge(gw_hi_done, 1)
            pool.tensor_tensor(gw[:, :, 1, :], gw_raw[:, :, :], gw[:, :, 0, :].bitcast(F32), ALU.subtract)\
                .then_inc(gw_cut, 1)
            w_cut_lo(pool, 0, 0)
            link(pool.memset(ones[:, :], 1.0))
            link(pool.affine_select(out=upper[:, :], in_=ones[:, :], compare_op=ALU.is_ge, fill=0.0,
                                    base=0, pattern=[[1, P]], channel_multiplier=-1))
            link(pool.memset(mask_m[:, :], 0.0))
            link(pool.affine_select(out=mask_m[:, :], in_=mask_m[:, :], compare_op=ALU.is_ge, fill=NEG,
                                    base=0, pattern=[[-1, P]], channel_multiplier=1))
            link(pool.tensor_scalar(mask_f[:, :], mask_m[:, :], -1.0, None, ALU.mult))
            pool.tensor_copy(ident_b[:, :], core.ident[:, :]).then_inc(pool_set, 1)
            pool.wait_ge(pool_set, 1)
            for piece in range(1, 4):
                w_cut_lo(pool, piece % 2, C_V[0] + piece // 2)
            w_cut_lo(pool, 0, C_F[0])
            w_cut_lo(pool, 1, C_F[1])

            def fox_cut(p, first, last):
                w_cut_lo(pool, 0, p + (C_F[0] + 1))
                w_cut_lo(pool, 1, p + (C_F[1] + 1))

            repeat(pool, PAIRS, fox_cut)
            for piece in range(2, 4):
                w_cut_lo(pool, piece % 2, C_MV[0] + piece // 2)
            w_cut_lo(pool, 0, C_M[0])
            w_cut_lo(pool, 1, C_M[1])
            w_cut_lo(pool, 1, C_M[1] + 1)

            def ml_cut(h, first, last):
                if not last:
                    w_cut_lo(pool, 0, h + (C_M[0] + 1))
                    w_cut_lo(pool, 1, h * 2 + (C_M[1] + 2))
                else:
                    for k in range(2):
                        pool.wait_ge(y_hi, k + 1)
                        cut_y_lo(pool, k, y_lo_pool)
                    pool.wait_ge(gate_loaded, 16)
                    gate_out(pool, 0)
                    gate_out(pool, 1)
                    w_cut_lo(pool, 0, C_O[0])
                pool.wait_ge(var_done, h + 1)
                pool.tensor_tensor(tiny[:, 5, :], tiny[:, 4, :], core.neg_half[:, :], ALU.pow)\
                    .then_inc(rpow_done, 1)
                if not last:
                    w_cut_lo(pool, 1, h * 2 + (C_M[1] + 3))

            repeat(pool, MH, ml_cut)
            for n in range(1, 8):
                w_cut_lo(pool, n % 2, C_O[n % 2] + n // 2, *(out_w(n) if n >= 4 else ()))
            pool.wait_ge(out_ready, NS)
            for j in range(ffn_weights.TPS):
                pool.wait_ge(ffn_weights.hi_done, j + 1)
                ffn_weights.cut_lo(pool, 0, j)
            for t in range(NS + 1):
                if t < NS:
                    norm.inverse(pool, t)
                if t >= 1:
                    norm.add_shift(pool, t - 1)

        @block.scalar
        def _(act):
            link = Chain(act, act_step)
            flat = lambda t: t[:, :, :].rearrange("p k n -> p (k n)")
            for half in range(core.NH):
                act.wait_ge(zrow_ready, half + 1)
                act.copy(zrows[0:2 * NG, half * BANK:(half + 1) * BANK], core.bank[0:2 * NG, 6 + half, :])\
                    .then_inc(zrow_kept, 1)
            act.wait_ge(neg_done, 1)
            act.activation(flat(zneg), flat(zneg), ACT.Exp).then_inc(exp_done, 1)
            act.wait_ge(exp_done, 1)
            act.activation(flat(zneg), flat(zneg), ACT.Ln, bias=1.0).then_inc(ln_done, 1)
            w_cut_hi(act, 0, 1, freed=(w_used[0], 1))
            w_cut_hi(act, 1, 1, freed=(w_used[1], 1))
            w_cut_hi(act, 0, C_F[0], freed=(w_used[0], 2))
            for t in range(0, NS, 2):
                act.wait_ge(v_ready, t + 1)
                act.copy(v_fox[:, t, :], core.bank[:, t, :]).then_inc(v_kept_even, 1)
            w_cut_hi(act, 1, C_F[1], freed=(v_ready, NS))

            def keep_qk(p, g):
                half = slice((g % 2) * BANK, (g % 2 + 1) * BANK)
                act.wait_ge(fq_ready, p * 4 + (g + 1))
                if g < 2:
                    act.mul(fq_hi[:, half], core.bank[:, g, :], -float(HD) ** -0.5).then_inc(fq_kept, 1)
                else:
                    act.copy(fk_hi[:, half], core.bank[:, g, :]).then_inc(fq_kept, 1)

            for g in range(4):
                keep_qk(0, g)

            def exp_rows(p, n):
                w = (BLOCK[n] + 1) * P
                act.wait_ge(logit_done, p * PER + (n + 1))
                rows = prob[:, n % RP, 0:w]
                act.activation(rows, rows, ACT.Exp, bias=low[:, n:n + 1], scale=-1.0,
                               accum_out=rowsum[:, n:n + 1]).then_inc(prob_done, 1)

            def keep_pt(p, n, first):
                w = min((BLOCK[n] + 1) * P, BANK)
                act.wait_ge(pt_ready, p * PER + (n + 1))
                if not (first and n < 2):
                    act.wait_ge(pv_ready, p * PER + (n - 1))
                act.copy(probT[:, n % 2, 0:w], core.bank[:, 4, 0:w]).then_inc(pt_act, 1)

            def fox_body(p, first, last):
                for m in range(2, PER + 2):
                    if m <= PER:
                        exp_rows(p, m - 1)
                    if m == 3:
                        w_cut_hi(act, 0, p + (C_F[0] + 1), freed=(fq_ready, p * 4 + 2))
                        w_cut_hi(act, 1, p + (C_F[1] + 1), freed=(fq_ready, p * 4 + 4))
                    keep_pt(p, m - 2, first)
                if not last:
                    for g in range(4):
                        keep_qk(p + 1, g)
                    exp_rows(p + 1, 0)
                for half in range(2):
                    act.wait_ge(yt_ready, p * 2 + (half + 1))
                    act.copy(yT_fox[:, bass.ds(p, 1), half * BANK:(half + 1) * BANK].rearrange("p a s -> p (a s)"),
                             core.bank[:, 4 + half, :]).then_inc(yt_kept, 1)

            exp_rows(0, 0)
            repeat(act, PAIRS, fox_body)
            w_cut_hi(act, 0, C_MV[0] + 1, freed=(w_used[0], 3))
            w_cut_hi(act, 1, C_MV[1] + 1, freed=(w_used[1], 2))
            w_cut_hi(act, 0, C_M[0], freed=(w_used[0], 4))
            act.wait_ge(y_done, PAIRS * PER)
            for t in range(0, NS, 2):
                act.wait_ge(v_ready, NS + t + 1)
                act.copy(v_ml[:, t, :, 0:P], core.bank[:, t, :].rearrange("p (h v) -> p h v", v=P))\
                    .then_inc(v_kept_even, 1)
            w_cut_hi(act, 1, C_M[1], freed=(v_ready, 2 * NS))

            def keep_x(h, g, first):
                off = (TAPS - 1 if g < 4 else 0) + (g % 2) * BANK
                act.wait_ge(x_ready, h * X_PER + (g + 1))
                if not first and g in (0, 2):
                    act.wait_ge(conv_done, h * 2 + (-1 if g == 0 else 0))
                if not first and g == 4:
                    act.wait_ge(sig_done, h)
                act.copy((pre_k, pre_q, mo)[g // 2][:, off:off + BANK], core.bank[:, g % 4, :])\
                    .then_inc(x_kept, 1)

            for g in range(4):
                keep_x(0, g, True)
            w_cut_hi(act, 1, C_M[1] + 1, freed=(x_ready, 4))

            def ml_body(h, first, last):
                link.at(h)
                bias = lambda c: consts[:, bass.ds(h + (TAPS * 2 * MH + c), 1)]
                if not last:
                    w_cut_hi(act, 0, h + (C_M[0] + 1), freed=(x_ready, h * X_PER + 2))
                keep_x(h, 4, first)
                for i, buf in ((1, mkT[:, 0:S]), (0, mqT[:, :])):
                    act.wait_ge(conv_done, h * 2 + (2 - i))
                    act.activation(buf, buf, ACT.Silu, bias=bias(i * MH)).then_inc(silu_done, 1)
                keep_x(h, 5, first)
                if not last:
                    w_cut_hi(act, 1, h * 2 + (C_M[1] + 2), freed=(x_ready, h * X_PER + 6))
                if not first:
                    act.wait_ge(ybt_kept, h * 2)
                act.wait_ge(x_kept, h * X_PER + X_PER)
                act.activation(sg[:, :], mo[:, :], ACT.Sigmoid).then_inc(sig_done, 1)
                if last:
                    act.wait_ge(x_ready, MH * X_PER)
                    for k in range(2):
                        act.copy(core.h_hi[:, k, :], yT_fox[:, k, :]).then_inc(y_hi, 1)
                act.wait_ge(args_done, h + 1)
                act.activation(arg[:, :, :], arg[:, :, :], ACT.Exp).then_inc(weights_done, 1)
                act.activation(dec[:, :], dec[:, :], ACT.Exp).then_inc(weights_done, 1)
                if not last:
                    keep_x(h + 1, 0, False)
                    keep_x(h + 1, 1, False)
                for half in range(2):
                    act.wait_ge(spt_ready, h * 2 + 2)
                    act.copy(dec[:, half * BANK:(half + 1) * BANK], core.bank[:, (7, 4)[half], :])\
                        .then_inc(spt_kept, 1)
                if not last:
                    keep_x(h + 1, 2, False)
                if last:
                    w_cut_hi(act, 0, C_O[0], freed=(x_ready, MH * X_PER), is_gated=(gated[0], 1))
                for j in range(NS):
                    r, jj = j // 3, j % 3
                    act.wait_ge(num_ready, h * 3 + (r + 1))
                    act.mul(o_all[:, j, :], core.bank[:, (6, 4, 6)[r], jj * V1:(jj + 1) * V1],
                            arg[:, 2, j:j + 1]).then_inc(inter_kept, 1)
                for j in range(NS):
                    act.wait_ge(o_done, h * 3 + (j // 3 + 1))
                    link(act.activation(sq_junk[:, :], o_all[:, j, 0:P], ACT.Square,
                                        accum_out=tiny[:, 0, j:j + 1]))
                act.activation(sq_junk[:, 0:NS], tiny[:, 0, :], ACT.Copy).then_inc(sq_done, 1)
                if last:
                    w_cut_hi(act, 1, C_O[1], freed=(x_ready, MH * X_PER), is_gated=(gated[0], 2))
                    for k in range(2, PAIRS):
                        act.copy(core.h_hi[:, k, :], yT_fox[:, k, :]).then_inc(y_hi, 1)
                if not last:
                    keep_x(h + 1, 3, False)
                    w_cut_hi(act, 1, h * 2 + (C_M[1] + 3), freed=(x_ready, h * X_PER + (X_PER + 4)))

            repeat(act, MH, ml_body)
            act.wait_ge(ybt_kept, 2 * MH)
            for k in range(PAIRS, KD):
                act.copy(core.h_hi[:, k, :], yT_ml[:, k - PAIRS, :]).then_inc(y_hi, 1)
            for n, freed in ((2, (w_used[0], 5)), (3, (w_used[1], 3))):
                w_cut_hi(act, n % 2, C_O[n % 2] + n // 2, freed=freed, is_gated=(gated[1], n - 1))
            for n in range(4, 8):
                w_cut_hi(act, n % 2, C_O[n % 2] + n // 2, is_gated=(gated[1], n - 1), dst=out_w(n)[0])
            act.wait_ge(out_ready, NS)
            act.wait_ge(w_lo_done[0], C_O[0] + 4)
            act.wait_ge(w_lo_done[1], C_O[1] + 4)
            for j in range(ffn_weights.TPS):
                act.wait_ge(ffn_weights.loaded[j], 32)
                ffn_weights.cut_hi(act, 0, j)
            for t in range(NS + 2):
                if t < NS:
                    act.wait_ge(out_added, NS + t + 1)
                    norm.square(act, t)
                if t >= 2:
                    norm.keep_hi(act, t - 2)

        @block.vector
        def _(dve):
            link = Chain(dve, dve_step)
            gates = lambda t, a, b: t[:, :, a:b].rearrange("p t g -> p g t")
            dve.wait_ge(small_loaded, 16 * 8)
            dve.wait_ge(const_turned, 1)
            dve.tensor_copy(consts[:, :], core.bank[:, 1, 0:NCONST]).then_inc(const_kept, 1)
            dve.wait_ge(z_ready, 1)
            z_parts = core.bank[:, 5, 0:NS * 2 * NG].rearrange("p (t a g) -> p t a g", a=2, g=NG)
            dve.tensor_tensor(z[:, :, :], z_parts[:, :, 0, :],
                              gbias[:, :].unsqueeze(1).to_broadcast([P, NS, NG]), ALU.add).then_inc(z_done, 1)
            dve.wait_ge(z_done, 1)
            dve.tensor_tensor(z[:, :, :], z[:, :, :], z_parts[:, :, 1, :], ALU.add).then_inc(z_done, 1)
            dve.wait_ge(z_done, 2)
            link(dve.tensor_scalar(logf[:, :, :], z[:, :, :], 0.0, None, ALU.min))
            dve.scalar_tensor_tensor(zneg[:, :, :], logf[:, :, :], 2.0, z[:, :, :], ALU.mult, ALU.subtract)\
                .then_inc(neg_done, 1)
            dve.wait_ge(ln_done, 1)
            dve.tensor_tensor(logf[:, :, :], logf[:, :, :], zneg[:, :, :], ALU.subtract).then_inc(logf_done, 1)
            for t in range(1, NS, 2):
                dve.wait_ge(v_ready, t + 1)
                dve.tensor_copy(v_fox[:, t, :], core.bank[:, t, :]).then_inc(v_kept_odd, 1)
            dve.wait_ge(sums_ready, 1)
            tg = lambda b: core.bank[:, b, 0:NS * NG].rearrange("p (t g) -> p t g", g=NG)
            link(dve.tensor_copy(cum_in[:, :, :], tg(4)))
            link(dve.tensor_copy(total[:, :, :], tg(5)))
            link(dve.memset(before[:, 0, :], 0.0))
            for t in range(1, NS):
                link(dve.tensor_tensor(before[:, t, :], before[:, t - 1, :], total[:, t - 1, 0:FH], ALU.add))
            link(dve.tensor_tensor(rows_in[:, 0:FH, :], gates(cum_in, 0, FH), gates(before, 0, FH), ALU.add))
            link(dve.tensor_tensor(rows_in[:, FH:NR, :], gates(z, FH, FH + MH), gates(cum_in, FH + MH, NG),
                                   ALU.subtract))
            link(dve.tensor_copy(m_b[:, :, :], rows_in[:, FH:NR, :]))
            link(dve.tensor_copy(m_total[:, :, :], gates(total, FH + MH, NG)))
            dve.tensor_copy(m_cum[:, :, :], gates(cum_in, FH + MH, NG)).then_inc(rows_ready, 1)
            dve.wait_ge(rows_turned, 1)
            dve.tensor_copy(rows_out[:, :], core.bank[0:NR * NS, 6, 0:P]).then_inc(rows_kept, 1)

            def cut_qk(p, g):
                half = slice((g % 2) * BANK, (g % 2 + 1) * BANK)
                hi, lo = ((fq_hi, fq_lo), (fk_hi, fk_lo))[g // 2]
                dve.wait_ge(fq_kept, p * 4 + (g + 1))
                dve.scalar_tensor_tensor(lo[:, half], core.bank[:, g, :], (-float(HD) ** -0.5, 1.0)[g // 2],
                                         hi[:, half].bitcast(F32), ALU.mult, ALU.subtract).then_inc(fq_cut, 1)

            for g in range(4):
                cut_qk(0, g)

            def logits(p, n, first):
                w = (BLOCK[n] + 1) * P
                if n == 0:
                    dve.wait_ge(cum_loaded, p * 16 + 16)
                dve.wait_ge(score_ready, p * PER + (n + 1))
                if not (first and n < RP):
                    dve.wait_ge(pt_ready, p * PER + (n - RP + 1))
                b = 2 * (n % 2)
                dve.memset(wait_tile[:, n:n + 1], 0.0)
                dve.tensor_tensor_reduce(prob[:, n % RP, 0:w],
                                         core.bank[:, b:b + 2, :].rearrange("p b n -> p (b n)")[:, 0:w],
                                         cum_bc[:, HEAD[n], 0:w], 1.0, 3e38, ALU.add, ALU.min,
                                         low[:, n:n + 1]).then_inc(logit_done, 1)

            def keep_pt(p, n, first):
                w = (BLOCK[n] + 1) * P
                if w <= BANK:
                    return
                dve.wait_ge(pt_ready, p * PER + (n + 1))
                if not (first and n < 2):
                    dve.wait_ge(pv_ready, p * PER + (n - 1))
                dve.tensor_copy(probT[:, n % 2, BANK:w], core.bank[:, 5, 0:w - BANK]).then_inc(pt_dve, 1)

            def normalise(p, n, first):
                dve.wait_ge(pv_ready, p * PER + (n + 1))
                if not first and n == 0:
                    dve.wait_ge(yt_ready, p * 2)
                link(dve.reciprocal(rinv[:, n:n + 1], rowsum[:, n:n + 1]))
                dve.tensor_scalar(y_tok[:, BLOCK[n], HEAD[n] * HD:(HEAD[n] + 1) * HD],
                                  core.bank[:, 6 + n % 2, 0:HD], rinv[:, n:n + 1], None, ALU.mult)\
                    .then_inc(y_done, 1)

            def fox_body(p, first, last):
                link.at(p)
                for m in range(2, PER + 2):
                    if m < PER:
                        logits(p, m, first)
                    keep_pt(p, m - 2, first)
                    if 3 <= m <= PER:
                        normalise(p, m - 3, first)
                if not last:
                    for g in range(4):
                        cut_qk(p + 1, g)
                normalise(p, PER - 2, first)
                normalise(p, PER - 1, first)
                if not last:
                    logits(p + 1, 0, False)
                    logits(p + 1, 1, False)

            logits(0, 0, True)
            logits(0, 1, True)
            repeat(dve, PAIRS, fox_body)
            link.leave(PAIRS)
            dve.wait_ge(yt_kept, 2 * PAIRS)
            link(dve.memset(v_ml[:, :, :, P:V1], 1.0))
            link(dve.memset(pre_q[:, 0:TAPS - 1], 0.0))
            link(dve.memset(pre_k[:, 0:TAPS - 1], 0.0))
            link(dve.memset(mst[:, 0:1], 0.0))
            for t in range(1, NS, 2):
                dve.wait_ge(v_ready, NS + t + 1)
                dve.tensor_copy(v_ml[:, t, :, 0:P], core.bank[:, t, :].rearrange("p (h v) -> p h v", v=P))\
                    .then_inc(v_kept_odd, 1)

            chunks = lambda t: t.rearrange("p (c s) -> p c s", s=P)

            def cut_y(ks):
                for k in ks:
                    dve.wait_ge(y_hi, k + 1)
                    cut_y_lo(dve, k, y_lo)

            def ml_body(h, first, last):
                link.at(h)
                if not first:
                    dve.wait_ge(num_ready, h * 3)
                for i, src, dst in ((1, pre_k, mkT[:, 0:S]), (0, pre_q, mqT[:, :])):
                    dve.wait_ge(x_kept, h * X_PER + (4 - 2 * i))
                    for w in range(TAPS):
                        tap = consts[:, bass.ds(h + (w * 2 * MH + i * MH), 1)]
                        if w == 0:
                            link(dve.tensor_scalar(dst, src[:, 0:S], tap, None, ALU.mult))
                        elif w < TAPS - 1:
                            link(dve.scalar_tensor_tensor(dst, src[:, w:w + S], tap, dst, ALU.mult, ALU.add))
                        else:
                            dve.scalar_tensor_tensor(dst, src[:, w:w + S], tap, dst, ALU.mult, ALU.add)\
                                .then_inc(conv_done, 1)
                head = lambda t: t[:, bass.ds(h, 1), :].rearrange("p a c -> p (a c)")
                prev = mst[:, 0:NS]
                dve.wait_ge(b_loaded, h * 16 + 16)
                link(dve.tensor_reduce(tiny[:, 1, :], chunks(dec[:, :]), AX.X, ALU.max))
                link(dve.tensor_tensor_scan(mst[:, 1:NS + 1], tiny[:, 1, :], head(m_total), 0.0, ALU.max, ALU.add))
                link(dve.tensor_tensor(tiny[:, 1, :], tiny[:, 1, :], prev, ALU.max))
                link(dve.tensor_tensor(arg[:, 0, :], prev, tiny[:, 1, :], ALU.subtract))
                link(dve.tensor_tensor(arg[:, 1, :], head(m_b), tiny[:, 1, :], ALU.subtract))
                link(dve.tensor_tensor(chunks(dec[:, :]), chunks(dec[:, :]),
                                       mask_m[:, :].unsqueeze(1).to_broadcast([P, NS, P]), ALU.add))
                link(dve.tensor_reduce(tiny[:, 2, :], chunks(dec[:, :]), AX.X, ALU.max))
                link(dve.tensor_tensor(tiny[:, 2, :], tiny[:, 2, :], prev, ALU.max))
                link(dve.tensor_tensor(arg[:, 2, :], prev, tiny[:, 2, :], ALU.subtract))
                link(dve.scalar_tensor_tensor(arg[:, 3, :], head(m_cum), -1.0, tiny[:, 2, :],
                                              ALU.mult, ALU.subtract))
                dve.tensor_tensor(chunks(dec[:, :]), chunks(dec[:, :]),
                                  tiny[:, 2, :].unsqueeze(2).to_broadcast([P, NS, P]), ALU.subtract)\
                    .then_inc(args_done, 1)
                dve.wait_ge(sig_done, h + 1)
                dve.tensor_scalar(sg[:, :], sg[:, :], consts[:, bass.ds(h + (TAPS + 1) * 2 * MH, 1)], None,
                                  ALU.mult).then_inc(sg_done, 1)
                dve.wait_ge(weights_done, h * 2 + 2)
                link(dve.tensor_scalar(arg[:, 1, :], arg[:, 1, :], K_SCALE, None, ALU.mult))
                for half in range(2):
                    c4 = slice(4 * half, 4 * half + 4)
                    dve.wait_ge(kt_ready, h * 2 + (half + 1))
                    dve.tensor_tensor(chunks(kw_c)[:, c4, :], chunks(core.bank[:, 4 + half, :]),
                                      arg[:, 1, c4].unsqueeze(2).to_broadcast([P, 4, P]), ALU.mult)\
                        .then_inc(kw_done, 1)
                for half in range(2):
                    part = dec[:, half * BANK:(half + 1) * BANK]
                    dve.wait_ge(qk_ready, h * 2 + (half + 1))
                    dve.scalar_tensor_tensor(part, core.bank[:, 6 + half, :], K_SCALE, part, ALU.mult, ALU.mult)\
                        .then_inc(sp_done, 1)
                dve.memset(states[:, 0, :], 0.0).then_inc(state_done, 1)
                for j in range(NS - 1):
                    dve.wait_ge(u_ready, h * 3 + (j // 3 + 1))
                    dve.wait_ge(state_done, h * NS + (j + 1))
                    dve.scalar_tensor_tensor(states[:, j + 1, :], states[:, j, :], arg[:, 0, j:j + 1],
                                             core.bank[:, 4 + j // 3, (j % 3) * V1:(j % 3 + 1) * V1],
                                             ALU.mult, ALU.add).then_inc(state_done, 1)
                for r in range(3):
                    j0, j1 = 3 * r, min(3 * r + 3, NS)
                    dve.wait_ge(inter_kept, h * NS + j1)
                    dve.tensor_tensor(o_all[:, j0:j1, :], o_all[:, j0:j1, :],
                                      core.bank[:, (5, 7, 5)[r], 0:(j1 - j0) * V1]
                                      .rearrange("p (c v) -> p c v", v=V1), ALU.add).then_inc(o_done, 1)
                den = o_all[:, :, P:V1].rearrange("p c v -> p (c v)")
                dve.wait_ge(o_done, h * 3 + 3)
                link(dve.scalar_tensor_tensor(tiny[:, 1, :], den, -1.0, den, ALU.mult, ALU.max))
                link(dve.tensor_tensor(tiny[:, 1, :], tiny[:, 1, :], arg[:, 3, :], ALU.max))
                link(dve.reciprocal(tiny[:, 2, :], tiny[:, 1, :]))
                dve.wait_ge(sq_done, h + 1)
                link(dve.tensor_tensor(tiny[:, 3, :], tiny[:, 0, :], tiny[:, 2, :], ALU.mult))
                link(dve.tensor_tensor(tiny[:, 3, :], tiny[:, 3, :], tiny[:, 2, :], ALU.mult))
                dve.tensor_scalar(tiny[:, 4, :], tiny[:, 3, :], 1.0 / P, EPS, ALU.mult, ALU.add)\
                    .then_inc(var_done, 1)
                dve.wait_ge(rpow_done, h + 1)
                link(dve.tensor_tensor(tiny[:, 6, :], tiny[:, 5, :], tiny[:, 2, :], ALU.mult))
                for half in range(2):
                    c4 = slice(4 * half, 4 * half + 4)
                    dve.tensor_tensor(o_all[:, c4, 0:P], o_all[:, c4, 0:P],
                                      tiny[:, 6, c4].unsqueeze(2).to_broadcast([P, 4, P]), ALU.mult)\
                        .then_inc(yb_done, 1)
                if last:
                    cut_y(range(2, PAIRS))
                for half in range(2):
                    dve.wait_ge(ybt_ready, h * 2 + (half + 1))
                    cols = slice(half * BANK, (half + 1) * BANK)
                    dve.tensor_tensor(yT_ml[:, bass.ds(h, 1), cols].rearrange("p a s -> p (a s)"),
                                      core.bank[:, (7, 4)[half], :], sg[:, cols], ALU.mult)\
                        .then_inc(ybt_kept, 1)

            repeat(dve, MH, ml_body)
            link.leave(MH)
            cut_y(range(PAIRS, KD))
            dve.wait_ge(gate_loaded, 16)
            for n in range(2, 8):
                gate_out(dve, n)

            def add_out(n):
                t, dh = n % NS, n // NS
                part = core.xres[:, t, dh * BANK:(dh + 1) * BANK]
                dve.wait_ge(out_ready, n + 1)
                dve.tensor_tensor(part, core.bank[:, t if dh == 0 else t % 4, :], part, ALU.add)\
                    .then_inc(out_added, 1)

            for n in range(NS):
                add_out(n)
            for t in range(NS + 2):
                if t < NS:
                    add_out(NS + t)
                if 1 <= t <= NS:
                    norm.scale(dve, t - 1)
                if t >= 2:
                    norm.keep_lo(dve, t - 2)

        @block.tensor
        def _(pe):
            pe.wait_ge(small_loaded, 16 * 8)
            pe.transpose(core.bank[:, 1, 0:NCONST], const_rows[:, :], core.ident[0:NCONST, 0:NCONST])\
                .then_inc(const_turned, 1)
            pe.wait_ge(gw_cut, 1)
            for half in range(core.NH):
                tok = slice(half * BANK, (half + 1) * BANK)
                for k in range(KD):
                    pe.matmul(core.bank[0:2 * NG, 6 + half, :], gw[:, k, :, :].rearrange("p a n -> p (a n)"),
                              core.h_hi[:, k, tok], start=(k == 0), stop=False)
                    mm = pe.matmul(core.bank[0:NG, 6 + half, :], gw[:, k, 0, :], core.h_lo[:, k, tok],
                                   start=False, stop=(k == KD - 1))
                mm.then_inc(zrow_ready, 1)
            for t in range(NS):
                if t % 4 == 0:
                    pe.wait_ge(zrow_kept, t // 4 + 1)
                mm = pe.transpose(core.bank[:, 5, t * 2 * NG:(t + 1) * 2 * NG], zrows[0:2 * NG, t * P:(t + 1) * P],
                                  core.ident[0:2 * NG, 0:2 * NG])
            mm.then_inc(z_ready, 1)

            def v_waits(k, t):
                if k == 0 and t == 1:
                    pe.wait_ge(const_kept, 1)
                if k == 0 and t == 5:
                    pe.wait_ge(z_done, 2)

            by_token(pe, C_V, v_ready, v_waits)
            pe.wait_ge(logf_done, 1)
            pe.wait_ge(pool_set, 1)
            pe.wait_ge(v_kept_even, NS // 2)
            pe.wait_ge(v_kept_odd, NS // 2)
            flat = lambda t: t[:, :, :].rearrange("p k n -> p (k n)")
            pe.matmul(core.bank[:, 4, 0:NS * NG], upper[:, :], flat(logf), start=True, stop=True)
            pe.matmul(core.bank[:, 5, 0:NS * NG], ones[:, :], flat(logf), start=True, stop=True)\
                .then_inc(sums_ready, 1)

            def project_qk(p, g):
                if g % 2 == 0:
                    pe.wait_ge(w_lo_done[g // 2], p + (C_F[g // 2] + 1))
                by_feature(pe, core.bank[:, g, :], g // 2, g % 2).then_inc(fq_ready, 1)

            project_qk(0, 0)
            project_qk(0, 1)
            pe.wait_ge(rows_ready, 1)
            pe.transpose(core.bank[0:NR * NS, 6, 0:P], rows_in[:, :, :].rearrange("p r t -> p (r t)"),
                         core.ident[:, :]).then_inc(rows_turned, 1)
            project_qk(0, 2)
            project_qk(0, 3)

            def scores(p, n, first):
                e, i = HEAD[n], BLOCK[n]
                heads = slice(e * HD, (e + 1) * HD)
                w = (i + 1) * P
                if n == 0:
                    pe.wait_ge(fq_cut, p * 4 + 4)
                    if first:
                        pe.wait_ge(rows_kept, 1)
                if not (first and n < 2):
                    pe.wait_ge(logit_done, p * PER + (n - 1))
                for b in range((w + BANK - 1) // BANK):
                    k0, k1 = b * BANK, min((b + 1) * BANK, w)
                    k2 = max(k1, k0 + 2 * P)
                    three(pe, core.bank[:, 2 * (n % 2) + b, 0:k2 - k0], fq_hi[heads, i * P:(i + 1) * P],
                          fq_lo[heads, i * P:(i + 1) * P], fk_hi[heads, k0:k2], fk_lo[heads, k0:k2],
                          True, k1 < w)
                mm = pe.matmul(core.bank[:, 2 * (n % 2) + b, k1 - k0 - P:k1 - k0], ident_b[:, :], mask_f[:, :],
                               start=False, stop=True)
                mm.then_inc(score_ready, 1)

            def turn_prob(p, n, first):
                i = BLOCK[n]
                pe.wait_ge(prob_done, p * PER + (n + 1))
                if n >= 1:
                    pe.wait_ge(pt_act, p * PER + n)
                    if LONG[n - 1]:
                        pe.wait_ge(pt_dve, p * LONG[-1] + LONG[n - 1])
                elif not first:
                    pe.wait_ge(yt_kept, p * 2)
                for j in range(i + 1):
                    mm = pe.transpose(core.bank[:, 4 + j // 4, (j % 4) * P:(j % 4 + 1) * P],
                                      prob[:, n % RP, j * P:(j + 1) * P], core.ident[:, :])
                mm.then_inc(pt_ready, 1)

            def values(p, n, first):
                e, i = HEAD[n], BLOCK[n]
                pe.wait_ge(pt_act, p * PER + (n + 1))
                if LONG[n]:
                    pe.wait_ge(pt_dve, p * LONG[-1] + LONG[n])
                if not (first and n < 2):
                    pe.wait_ge(y_done, p * PER + (n - 1))
                for j in range(i + 1):
                    mm = pe.matmul(core.bank[:, 6 + n % 2, 0:HD], probT[:, n % 2, j * P:(j + 1) * P],
                                   v_fox[:, j, bass.ds(p * (2 * HD) + e * HD, HD)], start=(j == 0), stop=(j == i))
                mm.then_inc(pv_ready, 1)

            def fox_body(p, first, last):
                for m in range(2, PER + 2):
                    if m < PER:
                        scores(p, m, first)
                    turn_prob(p, m - 2, first)
                    if 3 <= m <= PER:
                        values(p, m - 3, first)
                    if m >= PER and not last:
                        pe.wait_ge(logit_done, p * PER + (m - 1))
                        project_qk(p + 1, 2 * (m - PER))
                        project_qk(p + 1, 2 * (m - PER) + 1)
                values(p, PER - 2, first)
                values(p, PER - 1, first)
                if not last:
                    scores(p + 1, 0, False)
                    scores(p + 1, 1, False)
                pe.wait_ge(y_done, p * PER + PER)
                pe.wait_ge(pt_act, p * PER + PER)
                for t in range(NS):
                    mm = pe.transpose(core.bank[:, 4 + t // 4, (t % 4) * P:(t % 4 + 1) * P], y_tok[:, t, :],
                                      core.ident[:, :])
                    if t % 4 == 3:
                        mm.then_inc(yt_ready, 1)

            scores(0, 0, True)
            scores(0, 1, True)
            repeat(pe, PAIRS, fox_body)

            def mv_waits(k, t):
                if k == 0 and t in (0, 4):
                    if t == 0:
                        pe.wait_ge(logit_done, PAIRS * PER)
                    else:
                        pe.wait_ge(yt_kept, 2 * PAIRS)

            by_token(pe, C_MV, v_ready, mv_waits)

            def project(h, g):
                slot = min(g // 2, 1)
                if g % 2 == 0:
                    pe.wait_ge(w_lo_done[slot], h * 2 + (C_M[1] + g // 2) if slot else h + (C_M[0] + 1))
                if g >= 4:
                    pe.wait_ge(x_kept, h * X_PER + (g - 3))
                elif not (isinstance(h, int) and h == 0):
                    pe.wait_ge(x_kept, h * X_PER - (g == 0))
                by_feature(pe, core.bank[:, g % 4, :], slot, g % 2).then_inc(x_ready, 1)

            pe.wait_ge(v_kept_even, NS)
            pe.wait_ge(v_kept_odd, NS)
            for g in range(4):
                project(0, g)

            def ml_body(h, first, last):
                c_of = lambda j: slice(j * P, (j + 1) * P)
                project(h, 4)
                project(h, 5)
                if not last:
                    project(h + 1, 0)
                pe.wait_ge(silu_done, h * 2 + 2)
                if not first:
                    pe.wait_ge(ybt_kept, h * 2)
                for j in range(NS):
                    mm = pe.transpose(core.bank[:, 4 + j // 4, c_of(j % 4)], mkT[:, c_of(j)], core.ident[:, :])
                    if j % 4 == 3:
                        mm.then_inc(kt_ready, 1)
                for j in range(NS):
                    mm = pe.matmul(core.bank[:, 6 + j // 4, c_of(j % 4)], mqT[:, c_of(j)], mkT[:, c_of(j)],
                                   start=True, stop=True)
                    if j % 4 == 3:
                        mm.then_inc(qk_ready, 1)
                if not last:
                    project(h + 1, 1)
                for j in range(NS - 1):
                    if j in (0, 3):
                        pe.wait_ge(kw_done, h * 2 + 2)
                    if j == 6:
                        pe.wait_ge(sp_done, h * 2 + 1)
                    mm = pe.matmul(core.bank[:, 4 + j // 3, (j % 3) * V1:(j % 3 + 1) * V1], kw_c[:, c_of(j)],
                                   v_ml[:, j, bass.ds(h, 1), :].rearrange("p a v -> p (a v)"),
                                   start=True, stop=True)
                    if j in (2, 5, 6):
                        mm.then_inc(u_ready, 1)
                pe.wait_ge(sp_done, h * 2 + 2)
                pe.wait_ge(state_done, h * NS + 4)
                for j in range(NS):
                    mm = pe.transpose(core.bank[:, (7, 4)[j // 4], c_of(j % 4)], dec[:, c_of(j)],
                                      core.ident[:, :])
                    if j % 4 == 3:
                        mm.then_inc(spt_ready, 1)
                if not last:
                    project(h + 1, 2)
                pe.wait_ge(state_done, h * NS + NS)
                for r in range(3):
                    num_b, int_b = ((5, 6), (7, 4), (5, 6))[r]
                    if r == 0:
                        pe.wait_ge(spt_kept, h * 2 + 2)
                    if r == 2:
                        pe.wait_ge(o_done, h * 3 + 1)
                    for j in range(3 * r, min(3 * r + 3, NS)):
                        cols = slice((j % 3) * V1, (j % 3 + 1) * V1)
                        pe.matmul(core.bank[:, num_b, cols], dec[:, c_of(j)],
                                  v_ml[:, j, bass.ds(h, 1), :].rearrange("p a v -> p (a v)"),
                                  start=True, stop=True)
                        mm = pe.matmul(core.bank[:, int_b, cols], mqT[:, c_of(j)], states[:, j, :],
                                       start=True, stop=True)
                    mm.then_inc(num_ready, 1)
                if not last:
                    project(h + 1, 3)
                else:
                    pe.wait_ge(x_kept, MH * X_PER)
                    pe.wait_ge(w_lo_done[0], C_O[0] + 1)
                    for k in range(2):
                        pe.wait_ge(y_lo_pool, k + 1)
                        for t in range(NS // 2):
                            token_product(pe, k, t)
                for j in range(NS):
                    if j % 4 == 0:
                        pe.wait_ge(yb_done, h * 2 + (j // 4 + 1))
                    mm = pe.transpose(core.bank[:, (7, 4)[j // 4], c_of(j % 4)], o_all[:, j, 0:P],
                                      core.ident[:, :])
                    if j % 4 == 3:
                        mm.then_inc(ybt_ready, 1)

            repeat(pe, MH, ml_body)

            def out_waits(k, t):
                if t == 0:
                    pe.wait_ge(y_lo, k - 1)
                if k == 0 and t == 4:
                    pe.wait_ge(ybt_kept, 2 * MH)

            by_token(pe, C_O, out_ready, out_waits, lambda k, t: k < 2 and t < NS // 2)
            for t in range(NS + 2):
                if t < NS:
                    tok = slice(t * P, (t + 1) * P)
                    if t == 0:
                        pe.wait_ge(w_lo_done[0], C_O[0] + 4)
                        pe.wait_ge(w_lo_done[1], C_O[1] + 4)
                    pe.wait_ge(out_added, t + 1 if t < 4 else NS + t - 3)
                    for k in range(KD):
                        mm = three(pe, core.bank[:, t % 4, :], core.h_hi[:, k, tok], core.h_lo[:, k, tok],
                                   out_w_hi[:, k, :], out_w_lo[:, k, :], k == 0, k == KD - 1)
                    mm.then_inc(out_ready, 1)
                if t == 1:
                    pe.wait_ge(out_added, NS)
                if t >= 2:
                    norm.turn(pe, t - 2)
    ms.close()


def program(nc, x, c, w_ada, b_ada, w_ffn1_in, w_ffn1_out, w_mix_in, b_fox_f, b_m_i, b_m_f,
            w_conv, b_conv, g_mhn, w_mix_out, w_ffn2_in, w_ffn2_out, g_final, out):
    with ExitStack() as ctx:
        core = Core(nc, ctx, x)
        buf = FfnBuffers(core, w_ada)
        ffn1_weights = InWeights(core, "f1", buf, w_ffn1_in)
        ffn2_weights = InWeights(core, "f2", buf, w_ffn2_in)
        ms = MixerStart(core, w_mix_in, b_fox_f, b_m_i, b_m_f, w_conv, b_conv, g_mhn)
        ffn(core, "f1", buf, ffn1_weights, w_ffn1_out, next_mod=3, start_in=(x, c, w_ada, b_ada), after=ms)
        core.end_part()
        mixer(core, ms, ffn2_weights, w_mix_in, b_fox_f, b_m_i, b_m_f, w_conv, b_conv, g_mhn, w_mix_out, 5, 6)
        core.end_part()
        ffn(core, "f2", buf, ffn2_weights, w_ffn2_out, gate_row=8, g_final=g_final, out=out)


_INS = ['x', 'c', 'w_ada', 'b_ada', 'w_ffn1_in', 'w_ffn1_out', 'w_mix_in', 'b_fox_f', 'b_m_i', 'b_m_f',
        'w_conv', 'b_conv', 'g_mhn', 'w_mix_out', 'w_ffn2_in', 'w_ffn2_out', 'g_final']


def kernel(**inputs):
    import numpy as np
    import concourse.bacc as bacc
    from concourse.bass_utils import run_bass_kernel_spmd

    nc = bacc.Bacc("TRN2", target_bir_lowering=False, num_devices=1)
    arrays, args = {}, []
    for name in _INS:
        a = np.ascontiguousarray(inputs[name])
        arrays[f"in_{name}"] = a
        args.append(nc.dram_tensor(f"in_{name}", a.shape, mybir.dt.from_np(a.dtype), kind="ExternalInput").ap())
    shape = inputs['x'].shape
    args.append(nc.dram_tensor("out_y", shape, F32, kind="ExternalOutput").ap())
    program(nc, *args)
    r = run_bass_kernel_spmd(nc, [arrays], core_ids=[0])
    return r.results[0]["out_y"]
```
